# Optimizing a Trainium2 kernel written in Bass

```python
import math
import jax, jax.numpy as jnp
from jax import lax
import numpy as np

D_MODEL = 1024
BATCH = 1
SEQ = 1024
DEPTH = 1

SSM_WIDTH = D_MODEL // 2
SSM_GROUP = 16
SSM_GROUPS = SSM_WIDTH // SSM_GROUP
SSM_STATE = 64
N_HEADS = 8
HEAD_DIM = 64
ATTN_WIDTH = N_HEADS * HEAD_DIM
KV_DIM = HEAD_DIM
IDX_HEADS = 4
IDX_DIM = 64
INDEX_TOPK = 256
Q_BLOCK = 128
N_BRANCH = 2
D_FF = -(-8 * D_MODEL // (3 * 256)) * 256
RMS_EPS = 1e-6
DT_MIN = 1e-3
DT_MAX = 1e-1

IN_SIZES = (SSM_WIDTH, ATTN_WIDTH, KV_DIM, KV_DIM, IDX_HEADS * IDX_DIM, IDX_DIM, IDX_HEADS, N_BRANCH * D_MODEL)
IN_COLS = sum(IN_SIZES)
IN_SPLITS = tuple(int(s) for s in np.cumsum(IN_SIZES)[:-1])


def _rms(x, g, eps=RMS_EPS):
    xf = x.astype(jnp.float32)
    y = xf * lax.rsqrt(jnp.mean(xf * xf, axis=-1, keepdims=True) + eps)
    return (y * g.astype(jnp.float32)).astype(x.dtype)

def _complex_combine(e1, e2):
    a1r, a1i, b1r, b1i = e1
    a2r, a2i, b2r, b2i = e2
    return (a2r * a1r - a2i * a1i,
            a2r * a1i + a2i * a1r,
            a2r * b1r - a2i * b1i + b2r,
            a2r * b1i + a2i * b1r + b2i)

def _s5_branch(u, A_re, A_im, log_dt, B_re, B_im, C_re, C_im, D_skip, w_glu, b_glu):
    bsz, L, _ = u.shape
    uf = u.astype(jnp.float32).reshape(bsz, L, SSM_GROUPS, SSM_GROUP)
    ar = A_re.astype(jnp.float32)
    ai = A_im.astype(jnp.float32)
    dt = jnp.exp(log_dt.astype(jnp.float32))[:, None]
    mag = jnp.exp(ar * dt)
    abar_r = mag * jnp.cos(ai * dt)
    abar_i = mag * jnp.sin(ai * dt)
    den = ar * ar + ai * ai
    nr = abar_r - 1.0
    coef_r = (nr * ar + abar_i * ai) / den
    coef_i = (abar_i * ar - nr * ai) / den
    bu_r = jnp.einsum('gnp,blgp->blgn', B_re.astype(jnp.float32), uf)
    bu_i = jnp.einsum('gnp,blgp->blgn', B_im.astype(jnp.float32), uf)
    b_r = coef_r * bu_r - coef_i * bu_i
    b_i = coef_r * bu_i + coef_i * bu_r
    a_r = jnp.broadcast_to(abar_r, (1, L, SSM_GROUPS, SSM_STATE))
    a_i = jnp.broadcast_to(abar_i, (1, L, SSM_GROUPS, SSM_STATE))
    _, _, s_r, s_i = lax.associative_scan(_complex_combine, (a_r, a_i, b_r, b_i), axis=1)
    y = (jnp.einsum('gpn,blgn->blgp', C_re.astype(jnp.float32), s_r)
         - jnp.einsum('gpn,blgn->blgp', C_im.astype(jnp.float32), s_i)
         + D_skip.astype(jnp.float32).reshape(SSM_GROUPS, SSM_GROUP) * uf)
    y = jax.nn.gelu(y.reshape(bsz, L, SSM_WIDTH))
    y = y * jax.nn.sigmoid(y @ w_glu.astype(jnp.float32) + b_glu.astype(jnp.float32))
    return y.astype(u.dtype)

def _dsa_branch(q, k, v, qi, ki, wi):
    bsz, L = q.shape[0], q.shape[1]
    k_sel = min(INDEX_TOPK, L // 4)
    nb = L // Q_BLOCK
    q_blk = q.reshape(bsz, nb, Q_BLOCK, N_HEADS, HEAD_DIM).transpose(1, 0, 2, 3, 4)
    qi_blk = qi.reshape(bsz, nb, Q_BLOCK, IDX_HEADS, IDX_DIM).transpose(1, 0, 2, 3, 4)
    wi_blk = wi.reshape(bsz, nb, Q_BLOCK, IDX_HEADS).transpose(1, 0, 2, 3)
    starts = jnp.arange(nb, dtype=jnp.int32) * Q_BLOCK
    kif = ki.astype(jnp.float32)
    key_pos = jnp.arange(L, dtype=jnp.int32)
    w_scale = (IDX_HEADS ** -0.5) * (IDX_DIM ** -0.5)
    a_scale = HEAD_DIM ** -0.5
    gather = jax.vmap(lambda kk, ii: kk[ii])

    def block(args):
        qb, qib, wib, start = args
        pos_q = start + jnp.arange(Q_BLOCK, dtype=jnp.int32)
        visible = key_pos[None, :] <= pos_q[:, None]
        rel = jax.nn.relu(jnp.einsum('bqhd,bsd->bqhs', qib.astype(jnp.float32), kif))
        iscore = jnp.einsum('bqhs,bqh->bqs', rel, wib.astype(jnp.float32) * w_scale)
        iscore = jnp.where(visible[None], iscore, -jnp.inf)
        _, idx = lax.top_k(iscore, k_sel)
        valid = idx <= pos_q[None, :, None]
        kg = gather(k, idx).astype(jnp.float32)
        vg = gather(v, idx).astype(jnp.float32)
        logits = jnp.einsum('bqhd,bqkd->bhqk', qb.astype(jnp.float32), kg) * a_scale
        logits = jnp.where(valid[:, None], logits, -jnp.inf)
        p = jax.nn.softmax(logits, axis=-1)
        o = jnp.einsum('bhqk,bqkd->bqhd', p, vg)
        return o.astype(q.dtype)

    out = lax.map(block, (q_blk, qi_blk, wi_blk, starts))
    return out.transpose(1, 0, 2, 3, 4).reshape(bsz, L, ATTN_WIDTH)

def first_inputs(seed: int = 0) -> dict:
    key = jax.random.key(seed)
    ks = jax.random.split(key, 24)
    f32 = jnp.float32
    nrm = lambda k, shape, s: jax.random.normal(k, shape, f32) * s
    gain = lambda k, shape: 1.0 + 0.02 * jax.random.normal(k, shape, f32)
    Ld = DEPTH
    G, N, P = SSM_GROUPS, SSM_STATE, SSM_GROUP
    a_im = jnp.broadcast_to(math.pi * jnp.arange(N, dtype=f32), (Ld, G, N)) + 0.01 * jax.random.normal(ks[4], (Ld, G, N), f32)
    log_dt = jax.random.uniform(ks[5], (Ld, G), f32, math.log(DT_MIN), math.log(DT_MAX))
    return {
        "x": jax.random.normal(ks[0], (BATCH, SEQ, D_MODEL), f32),
        "norm1_g": gain(ks[1], (Ld, D_MODEL)),
        "w_in": nrm(ks[2], (Ld, D_MODEL, IN_COLS), D_MODEL ** -0.5),
        "A_re": -0.5 + 0.01 * jax.random.normal(ks[3], (Ld, G, N), f32),
        "A_im": a_im,
        "log_dt": log_dt,
        "B_re": nrm(ks[6], (Ld, G, N, P), (2 * P) ** -0.5),
        "B_im": nrm(ks[7], (Ld, G, N, P), (2 * P) ** -0.5),
        "C_re": nrm(ks[8], (Ld, G, P, N), (2 * N) ** -0.5),
        "C_im": nrm(ks[9], (Ld, G, P, N), (2 * N) ** -0.5),
        "D_skip": nrm(ks[10], (Ld, SSM_WIDTH), 1.0),
        "w_glu": nrm(ks[11], (Ld, SSM_WIDTH, SSM_WIDTH), SSM_WIDTH ** -0.5),
        "b_glu": nrm(ks[12], (Ld, SSM_WIDTH), 0.01),
        "q_norm_g": gain(ks[13], (Ld, HEAD_DIM)),
        "k_norm_g": gain(ks[14], (Ld, KV_DIM)),
        "idx_k_norm_g": gain(ks[15], (Ld, IDX_DIM)),
        "w_proj_ssm": nrm(ks[16], (Ld, SSM_WIDTH, D_MODEL), SSM_WIDTH ** -0.5),
        "w_proj_attn": nrm(ks[17], (Ld, ATTN_WIDTH, D_MODEL), ATTN_WIDTH ** -0.5),
        "w_out": nrm(ks[18], (Ld, D_MODEL, D_MODEL), D_MODEL ** -0.5),
        "norm2_g": gain(ks[19], (Ld, D_MODEL)),
        "w_ffn_gate": nrm(ks[20], (Ld, D_MODEL, D_FF), D_MODEL ** -0.5),
        "w_ffn_up": nrm(ks[21], (Ld, D_MODEL, D_FF), D_MODEL ** -0.5),
        "w_ffn_down": nrm(ks[22], (Ld, D_FF, D_MODEL), D_FF ** -0.5),
    }

def first_block(x, norm1_g, w_in, A_re, A_im, log_dt, B_re, B_im, C_re, C_im, D_skip, w_glu, b_glu,
              q_norm_g, k_norm_g, idx_k_norm_g, w_proj_ssm, w_proj_attn, w_out,
              norm2_g, w_ffn_gate, w_ffn_up, w_ffn_down):
    bsz, L, _ = x.shape
    for l in range(DEPTH):
        h = _rms(x, norm1_g[l])
        proj = h @ w_in[l]
        u, q, k, v, qi, ki, wi, gates = jnp.split(proj, IN_SPLITS, axis=-1)
        y_ssm = _s5_branch(u, A_re[l], A_im[l], log_dt[l], B_re[l], B_im[l], C_re[l], C_im[l],
                           D_skip[l], w_glu[l], b_glu[l])
        q = _rms(q.reshape(bsz, L, N_HEADS, HEAD_DIM), q_norm_g[l])
        k = _rms(k, k_norm_g[l])
        ki = _rms(ki, idx_k_norm_g[l])
        qi = qi.reshape(bsz, L, IDX_HEADS, IDX_DIM)
        y_att = _dsa_branch(q, k, v, qi, ki, wi)
        g_ssm, g_att = jnp.split(gates, N_BRANCH, axis=-1)
        merged = (jax.nn.sigmoid(g_ssm) * (y_ssm @ w_proj_ssm[l])
                  + jax.nn.sigmoid(g_att) * (y_att @ w_proj_attn[l]))
        x = x + merged @ w_out[l]
        h2 = _rms(x, norm2_g[l])
        x = x + (jax.nn.silu(h2 @ w_ffn_gate[l]) * (h2 @ w_ffn_up[l])) @ w_ffn_down[l]
    return x


DEPTH_2 = 2

SSD_HEAD_DIM = 64
SSD_WIDTH = D_MODEL
SSD_HEADS = SSD_WIDTH // SSD_HEAD_DIM
SSD_GROUPS = 4
SSD_STATE = 128
SSD_CONV = 4
SSD_CHUNK = 128
SSD_CONV_CH = SSD_WIDTH + 2 * SSD_GROUPS * SSD_STATE

DA_QK_DIM = 64
DA_V_DIM = 128
DA_HEADS = D_MODEL // DA_V_DIM
DA_QK_WIDTH = DA_HEADS * 2 * DA_QK_DIM
DA_WIDTH = DA_HEADS * DA_V_DIM
REL_BUCKETS = 32
REL_MAX_DIST = 128

EVEN_SPLITS = (SSD_WIDTH, SSD_CONV_CH, SSD_HEADS, DA_QK_WIDTH, DA_QK_WIDTH, DA_WIDTH, DA_WIDTH)
EVEN_IN = sum(EVEN_SPLITS)
EVEN_MIX = SSD_WIDTH + DA_WIDTH

HG_HEAD_DIM = 128
HG_WIDTH = 2 * D_MODEL
HG_HEADS = HG_WIDTH // HG_HEAD_DIM
HG_CHUNK = 16
ODD_IN = 4 * HG_WIDTH

N_EVEN = (DEPTH_2 + 1) // 2
N_ODD = DEPTH_2 // 2
EPS = 1e-6


def rmsnorm(x, w):
    xf = x.astype(jnp.float32)
    y = xf * lax.rsqrt(jnp.mean(xf * xf, axis=-1, keepdims=True) + EPS)
    return (y * w.astype(jnp.float32)).astype(x.dtype)

def causal_dwconv(x, w, b):
    K, C = w.shape
    y = lax.conv_general_dilated(x, w[:, None, :].astype(x.dtype), window_strides=(1,),
                                 padding=[(K - 1, 0)], dimension_numbers=("NWC", "WIO", "NWC"),
                                 feature_group_count=C)
    return y + b.astype(x.dtype)

def segsum(a):
    T = a.shape[-1]
    cs = jnp.cumsum(a, axis=-1)
    diff = cs[..., :, None] - cs[..., None, :]
    return jnp.where(jnp.tril(jnp.ones((T, T), bool)), diff, -jnp.inf)

def ssd_scan(x, dt, A, Bm, Cm):
    b, L, H, P = x.shape
    G, N = Bm.shape[2], Bm.shape[3]
    R = H // G
    c, l = L // SSD_CHUNK, SSD_CHUNK
    X = (x.astype(jnp.float32) * dt[..., None]).reshape(b, c, l, G, R, P)
    a = (dt * A).reshape(b, c, l, G, R).transpose(0, 1, 3, 4, 2)
    Bc = Bm.reshape(b, c, l, G, N)
    Cc = Cm.reshape(b, c, l, G, N)
    a_cs = jnp.cumsum(a, axis=-1)
    CB = jnp.einsum("bclgn,bcsgn->bcgls", Cc, Bc)
    scores = CB[:, :, :, None] * jnp.exp(segsum(a))
    y_diag = jnp.einsum("bcgrls,bcsgrp->bclgrp", scores, X)
    decay_states = jnp.exp(a_cs[..., -1:] - a_cs)
    states = jnp.einsum("bclgn,bcgrl,bclgrp->bcgrpn", Bc, decay_states, X)
    chunk_a = jnp.pad(a_cs[..., -1].transpose(0, 2, 3, 1), ((0, 0), (0, 0), (0, 0), (1, 0)))
    decay_chunk = jnp.exp(segsum(chunk_a))
    states = jnp.concatenate([jnp.zeros_like(states[:, :1]), states], axis=1)
    new_states = jnp.einsum("bgrzc,bcgrpn->bzgrpn", decay_chunk, states)
    prev = new_states[:, :-1]
    y_off = jnp.einsum("bclgn,bcgrpn,bcgrl->bclgrp", Cc, prev, jnp.exp(a_cs))
    return (y_diag + y_off).reshape(b, L, H, P)

def t5_bucket(rel):
    n = jnp.maximum(rel, 0)
    max_exact = REL_BUCKETS // 2
    large = max_exact + (jnp.log(jnp.maximum(n, 1).astype(jnp.float32) / max_exact)
                         / math.log(REL_MAX_DIST / max_exact) * (REL_BUCKETS - max_exact)).astype(jnp.int32)
    large = jnp.minimum(large, REL_BUCKETS - 1)
    return jnp.where(n < max_exact, n, large)

def diff_attention(q, k, v, lam, rel_table):
    b, L, H, _, d = q.shape
    nb = L // Q_BLOCK
    scale = d ** -0.5
    kpos = jnp.arange(L)
    qb = q.reshape(b, nb, Q_BLOCK, H, 2, d).transpose(1, 0, 2, 3, 4, 5)

    def block(args):
        qi, i = args
        qpos = i * Q_BLOCK + jnp.arange(Q_BLOCK)
        rel = qpos[:, None] - kpos[None, :]
        bias = rel_table[t5_bucket(rel)].transpose(2, 0, 1).astype(jnp.float32)
        s = jnp.einsum("bqhcd,bkhcd->bhcqk", qi, k).astype(jnp.float32) * scale + bias[None, :, None]
        s = jnp.where(rel >= 0, s, -jnp.inf)
        p = jax.nn.softmax(s, axis=-1)
        w = p[:, :, 0] - lam * p[:, :, 1]
        return jnp.einsum("bhqk,bkhv->bqhv", w.astype(v.dtype), v)

    out = lax.map(block, (qb, jnp.arange(nb)))
    return out.transpose(1, 0, 2, 3, 4).reshape(b, L, H, v.shape[-1])

def ssd_diffattn_mixer(u, w_in, w_out, conv_w, conv_b, dt_bias, A_log, D_skip, ssd_norm_w,
                       lq1, lk1, lq2, lk2, subln_w, rel_table, layer_idx):
    b, L, _ = u.shape
    idx = [int(s) for s in np.cumsum(EVEN_SPLITS)[:-1]]
    z, xBC, dt, q, k, v, g = jnp.split(u @ w_in, idx, axis=-1)
    xBC = jax.nn.silu(causal_dwconv(xBC, conv_w, conv_b))
    xs, Bm, Cm = jnp.split(xBC, [SSD_WIDTH, SSD_WIDTH + SSD_GROUPS * SSD_STATE], axis=-1)
    xs = xs.reshape(b, L, SSD_HEADS, SSD_HEAD_DIM)
    Bm = Bm.reshape(b, L, SSD_GROUPS, SSD_STATE)
    Cm = Cm.reshape(b, L, SSD_GROUPS, SSD_STATE)
    dt = jax.nn.softplus(dt.astype(jnp.float32) + dt_bias.astype(jnp.float32))
    A = -jnp.exp(A_log.astype(jnp.float32))
    y = ssd_scan(xs, dt, A, Bm, Cm) + xs * D_skip[:, None]
    y = y.astype(u.dtype).reshape(b, L, SSD_WIDTH)
    y_a = rmsnorm(y * jax.nn.silu(z), ssd_norm_w)
    q = q.reshape(b, L, DA_HEADS, 2, DA_QK_DIM)
    k = k.reshape(b, L, DA_HEADS, 2, DA_QK_DIM)
    v = v.reshape(b, L, DA_HEADS, DA_V_DIM)
    lam_init = 0.8 - 0.6 * math.exp(-0.3 * layer_idx)
    lam = (jnp.exp(jnp.sum(lq1.astype(jnp.float32) * lk1.astype(jnp.float32)))
           - jnp.exp(jnp.sum(lq2.astype(jnp.float32) * lk2.astype(jnp.float32))) + lam_init)
    o = diff_attention(q, k, v, lam, rel_table)
    o = rmsnorm(o, subln_w) * (1.0 - lam_init)
    y_b = o.reshape(b, L, DA_WIDTH) * jax.nn.silu(g)
    return jnp.concatenate([y_a, y_b], axis=-1) @ w_out

def gated_linear_recurrence(q, k, v, log_f):
    b, L, H, dk = q.shape
    dv = v.shape[-1]
    C = HG_CHUNK
    nc = L // C

    def to_chunks(t):
        return t.reshape(b, nc, C, H, t.shape[-1]).transpose(1, 0, 3, 2, 4)

    causal = jnp.tril(jnp.ones((C, C), bool))

    def step(S, inp):
        qi, ki, vi, gi = inp
        bcum = jnp.cumsum(gi.astype(jnp.float32), axis=2)
        diff = bcum[:, :, :, None, :] - bcum[:, :, None, :, :]
        decay = jnp.exp(jnp.where(causal[:, :, None], diff, -jnp.inf))
        att = jnp.sum(qi[:, :, :, None, :] * ki[:, :, None, :, :] * decay, axis=-1)
        o = (jnp.einsum("bhts,bhsv->bhtv", att, vi)
             + jnp.einsum("bhtd,bhdv->bhtv", qi * jnp.exp(bcum), S))
        blast = bcum[:, :, -1:, :]
        S = (jnp.exp(blast[:, :, 0, :, None]) * S
             + jnp.einsum("bhsd,bhsv->bhdv", ki * jnp.exp(blast - bcum), vi))
        return S, o

    S0 = jnp.zeros((b, H, dk, dv), jnp.float32)
    _, o = lax.scan(step, S0, (to_chunks(q), to_chunks(k), to_chunks(v), to_chunks(log_f)))
    return o.transpose(1, 0, 3, 2, 4).reshape(b, L, H, dv).astype(v.dtype)

def hgrn2_mixer(u, w_in, w_out, lower_bounds, norm_w, layer_idx):
    b, L, _ = u.shape
    q, f, i, g = jnp.split(u @ w_in, 4, axis=-1)
    lb_all = jax.nn.softmax(lower_bounds.astype(jnp.float32), axis=0)
    lb_all = jnp.cumsum(lb_all, axis=0) - lb_all[0]
    lb = lb_all[layer_idx]
    f = lb + (1.0 - lb) * jax.nn.sigmoid(f.astype(jnp.float32))
    log_f = jnp.log(f)
    k = (1.0 - f).astype(u.dtype)
    q = jax.nn.silu(q)
    hs = lambda t: t.reshape(b, L, HG_HEADS, HG_HEAD_DIM)
    o = gated_linear_recurrence(hs(q), hs(k), hs(i), hs(log_f))
    o = rmsnorm(o, norm_w).reshape(b, L, HG_WIDTH) * jax.nn.silu(g)
    return o @ w_out

def second_inputs(seed: int = 0) -> dict:
    key = jax.random.key(seed)
    ks = jax.random.split(key, 24)
    nrm = lambda k, shape, s: jax.random.normal(k, shape, jnp.float32) * s
    dt = jnp.exp(jax.random.uniform(ks[7], (N_EVEN, SSD_HEADS), jnp.float32)
                 * (math.log(0.1) - math.log(1e-3)) + math.log(1e-3))
    dt = jnp.maximum(dt, 1e-4)
    return {
        "x": jax.random.normal(ks[0], (BATCH, SEQ, D_MODEL), jnp.float32),
        "norm_w": 1.0 + nrm(ks[1], (DEPTH_2, D_MODEL), 0.02),
        "final_norm_w": 1.0 + nrm(ks[2], (D_MODEL,), 0.02),
        "rel_bias": nrm(ks[3], (REL_BUCKETS, DA_HEADS), 0.1),
        "even_w_in": nrm(ks[4], (N_EVEN, D_MODEL, EVEN_IN), D_MODEL ** -0.5),
        "even_w_out": nrm(ks[5], (N_EVEN, EVEN_MIX, D_MODEL), EVEN_MIX ** -0.5),
        "conv_w": nrm(ks[6], (N_EVEN, SSD_CONV, SSD_CONV_CH), SSD_CONV ** -0.5),
        "conv_b": nrm(ks[8], (N_EVEN, SSD_CONV_CH), 0.02),
        "dt_bias": dt + jnp.log(-jnp.expm1(-dt)),
        "A_log": jnp.log(jax.random.uniform(ks[9], (N_EVEN, SSD_HEADS), jnp.float32, 1.0, 16.0)),
        "D_skip": 1.0 + nrm(ks[10], (N_EVEN, SSD_HEADS), 0.02),
        "ssd_norm_w": 1.0 + nrm(ks[11], (N_EVEN, SSD_WIDTH), 0.02),
        "lambda_q1": nrm(ks[12], (N_EVEN, DA_QK_DIM), 0.1),
        "lambda_k1": nrm(ks[13], (N_EVEN, DA_QK_DIM), 0.1),
        "lambda_q2": nrm(ks[14], (N_EVEN, DA_QK_DIM), 0.1),
        "lambda_k2": nrm(ks[15], (N_EVEN, DA_QK_DIM), 0.1),
        "subln_w": 1.0 + nrm(ks[16], (N_EVEN, DA_V_DIM), 0.02),
        "odd_w_in": nrm(ks[17], (N_ODD, D_MODEL, ODD_IN), D_MODEL ** -0.5),
        "odd_w_out": nrm(ks[18], (N_ODD, HG_WIDTH, D_MODEL), HG_WIDTH ** -0.5),
        "hgrn_lower_bounds": nrm(ks[19], (DEPTH_2, HG_WIDTH), 0.1),
        "hgrn_norm_w": 1.0 + nrm(ks[20], (N_ODD, HG_HEAD_DIM), 0.02),
    }

def second_block(x, norm_w, final_norm_w, rel_bias, even_w_in, even_w_out, conv_w, conv_b, dt_bias,
              A_log, D_skip, ssd_norm_w, lambda_q1, lambda_k1, lambda_q2, lambda_k2, subln_w,
              odd_w_in, odd_w_out, hgrn_lower_bounds, hgrn_norm_w):
    h = x
    for layer in range(DEPTH_2):
        u = rmsnorm(h, norm_w[layer])
        if layer % 2 == 0:
            e = layer // 2
            h = h + ssd_diffattn_mixer(u, even_w_in[e], even_w_out[e], conv_w[e], conv_b[e],
                                       dt_bias[e], A_log[e], D_skip[e], ssd_norm_w[e],
                                       lambda_q1[e], lambda_k1[e], lambda_q2[e], lambda_k2[e],
                                       subln_w[e], rel_bias, layer)
        else:
            o = layer // 2
            h = h + hgrn2_mixer(u, odd_w_in[o], odd_w_out[o], hgrn_lower_bounds,
                                hgrn_norm_w[o], layer)
    return rmsnorm(h, final_norm_w)


_first_inputs = second_inputs


def second_inputs(seed=0):
    import zlib

    import numpy as np

    out = dict(_first_inputs(seed))
    spreads = {}
    factors = {'final_norm_w': 2.777,
     'rel_bias': 4.088,
     'conv_b': 3.217,
     'D_skip': 6.467,
     'ssd_norm_w': 4.654,
     'lambda_q1': 2.764,
     'lambda_q2': 8.0,
     'subln_w': 8.0,
     'hgrn_lower_bounds': 8.0,
     'hgrn_norm_w': 6.958}
    for name, (base, spread) in spreads.items():
        noise = np.random.default_rng([zlib.crc32(name.encode()), seed]).standard_normal(out[name].shape)
        drawn = base * np.exp(spread * noise) if base else spread * noise
        out[name] = __import__('jax').numpy.asarray(drawn.astype(out[name].dtype))
    for name, factor in factors.items():
        out[name] = (out[name] * factor).astype(out[name].dtype)
    return out


_narrow_inputs = second_inputs


def second_inputs(seed=0):

    out = dict(_narrow_inputs(seed))
    wider = {'final_norm_w': 3.13,
     'D_skip': 3.7,
     'ssd_norm_w': 3.48,
     'subln_w': 4.04,
     'hgrn_norm_w': 4.83}
    for name, times in wider.items():
        mean = out[name].mean()
        out[name] = (mean + times * (out[name] - mean)).astype(out[name].dtype)
    return out


def setup_inputs(seed=0):
    out = dict(first_inputs(seed))
    for name, value in second_inputs(seed + 1).items():
        if name != "x":
            out[name + "_2"] = value
    return out


def reference(
    x, norm1_g, w_in, A_re, A_im, log_dt, B_re, B_im, C_re, C_im, D_skip, w_glu, b_glu,
    q_norm_g, k_norm_g, idx_k_norm_g, w_proj_ssm, w_proj_attn, w_out, norm2_g, w_ffn_gate,
    w_ffn_up, w_ffn_down, norm_w_2, final_norm_w_2, rel_bias_2, even_w_in_2, even_w_out_2,
    conv_w_2, conv_b_2, dt_bias_2, A_log_2, D_skip_2, ssd_norm_w_2, lambda_q1_2, lambda_k1_2,
    lambda_q2_2, lambda_k2_2, subln_w_2, odd_w_in_2, odd_w_out_2, hgrn_lower_bounds_2,
    hgrn_norm_w_2,
):
    x = first_block(
        x, norm1_g, w_in, A_re, A_im, log_dt, B_re, B_im, C_re, C_im, D_skip, w_glu, b_glu,
        q_norm_g, k_norm_g, idx_k_norm_g, w_proj_ssm, w_proj_attn, w_out, norm2_g, w_ffn_gate,
        w_ffn_up, w_ffn_down,
    )
    return second_block(
        x, norm_w_2, final_norm_w_2, rel_bias_2, even_w_in_2, even_w_out_2, conv_w_2, conv_b_2,
        dt_bias_2, A_log_2, D_skip_2, ssd_norm_w_2, lambda_q1_2, lambda_k1_2, lambda_q2_2,
        lambda_k2_2, subln_w_2, odd_w_in_2, odd_w_out_2, hgrn_lower_bounds_2, hgrn_norm_w_2,
    )


_drawn_inputs = setup_inputs


def setup_inputs(seed=0):
    import zlib

    import numpy as np

    out = dict(_drawn_inputs(seed))
    spreads = {}
    factors = {'norm1_g': 3.127,
     'A_re': 8.0,
     'B_re': 3.105,
     'B_im': 3.172,
     'C_re': 3.15,
     'C_im': 3.205,
     'b_glu': 8.0,
     'q_norm_g': 8.0,
     'k_norm_g': 8.0,
     'idx_k_norm_g': 6.019}
    for name, (base, spread) in spreads.items():
        noise = np.random.default_rng([zlib.crc32(name.encode()), seed]).standard_normal(out[name].shape)
        drawn = base * np.exp(spread * noise) if base else spread * noise
        out[name] = __import__('jax').numpy.asarray(drawn.astype(out[name].dtype))
    for name, factor in factors.items():
        out[name] = (out[name] * factor).astype(out[name].dtype)
    return out
```

```python
from contextlib import ExitStack

import numpy as np

import concourse.bass as bass
from concourse import mybir
from concourse.alu_op_type import AluOpType as ALU

F32 = mybir.dt.float32
F32R = mybir.dt.float32r
U32 = mybir.dt.uint32
ACT = mybir.ActivationFunctionType
AX = mybir.AxisListType

P = 128
L = 1024
D = 1024
TT = L // P
KD = D // P
NC = 512
EPS = 1e-6
DMA = 16
HUGE = 1e30


class Place:

    def __init__(self, nc, tag):
        self.nc, self.tag, self.ctx, self.numbers = nc, tag, ExitStack(), []

    def __enter__(self):
        self.ctx.__enter__()
        return self

    def __exit__(self, *a):
        if self.numbers and a[0] is None:
            self.clear()
        return self.ctx.__exit__(*a)

    def clear(self):
        runs = []
        for n in sorted(self.numbers):
            if runs and runs[-1][1] == n:
                runs[-1][1] = n + 1
            else:
                runs.append([n, n + 1])
        with self.nc.Block() as block:
            @block.gpsimd
            def _(pool):
                for first, end in runs:
                    pool.sem_clear(range(first, end))

    def sb(self, name, shape, dt=F32):
        return self.ctx.enter_context(self.nc.sbuf_tensor(f"{self.tag}_{name}", shape, dt))

    def ps(self, name, shape, dt=F32):
        return self.ctx.enter_context(self.nc.psum_tensor(f"{self.tag}_{name}", shape, dt))

    def sem(self, name):
        sem = self.ctx.enter_context(self.nc.semaphore(f"{self.tag}_{name}"))
        self.numbers.append(sem.num)
        return sem

    def store_sem(self, name):
        return self.nc.alloc_semaphore(f"{self.tag}_{name}")


class Link:

    def __init__(self, eng, sem):
        self.eng, self.sem, self.base, self.n = eng, sem, 0, 0

    def __call__(self, ins):
        self.mark(ins)
        self.wait()

    def mark(self, ins):
        ins.then_inc(self.sem, 1)
        self.n += 1

    def wait(self):
        self.eng.wait_ge(self.sem, self.base + self.n)

    def turn(self, r, per):
        self.start, self.per = self.base + self.n, per
        self.base, self.n = self.start + r * per, 0

    def end(self, turns):
        assert self.n == self.per, (self.n, self.per)
        self.base, self.n = self.start + turns * self.per, 0


PASSES = ((0, 0), (0, 1), (1, 0))


def split_product(pe, out, lhs, rhs, steps, start=True, stop=True):
    n = len(steps) * len(PASSES)
    i = 0
    for k in steps:
        for p, q in PASSES:
            mm = pe.matmul(out, lhs(p, k), rhs(q, k), start=start and i == 0, stop=stop and i == n - 1)
            i += 1
    return mm


def pairs(eng, n, body):
    if n >= 4:
        with eng.Fori(0, n // 2) as r:
            for s in range(2):
                body(r * 2 + s, s, r)
    else:
        for i in range(n - n % 2):
            body(i, i % 2, i // 2)
    if n % 2:
        body(n - 1, 0, n // 2)


def make_identity(nc, ident):
    with Place(nc, "id") as pl:
        zero = pl.sem("zeroed")
        made = pl.sem("made")
        with nc.Block() as block:
            @block.gpsimd
            def _(pool):
                pool.memset(ident[:, :], 0.0).then_inc(zero, 1)
                pool.wait_ge(zero, 1)
                pool.affine_select(out=ident[:, :], in_=ident[:, :], compare_op=ALU.not_equal, fill=1.0,
                                   base=0, pattern=[[-1, P]], channel_multiplier=1).then_inc(made, 1)
                pool.wait_ge(made, 1)


def norm_to_features(nc, tag, x, g, XT, ident):
    with Place(nc, tag) as pl:
        xin = pl.sb("xin", [P, 2, D])
        xs = pl.sb("xs", [P, 2, D])
        sq = pl.sb("sq", [P, 2, D])
        st = pl.sb("st", [P, 2, 4])
        gc = pl.sb("gc", [P, KD])
        xg = pl.sb("xg", [P, 2, KD, P])
        pT = pl.ps("pT", [P, 2, KD, P])
        ld = [pl.sem(f"x_loaded{s}") for s in range(2)]
        g_ld = pl.sem("gain_loaded")
        summed = pl.sem("squares_summed")
        mean = pl.sem("mean_ready")
        root = pl.sem("root_ready")
        inv = pl.sem("inverse_ready")
        scaled = pl.sem("rows_scaled")
        turned = pl.sem("rows_transposed")
        gained = pl.sem("features_scaled")
        hi = pl.sem("hi_stored")
        stored = pl.sem("lo_stored")

        with nc.Block() as block:
            @block.sync
            def _(sp):
                sp.dma_start(gc[:, :], g.rearrange("(k p) -> p k", p=P),
                             allow_slow_non_contiguous=True).then_inc(g_ld, DMA)

                def body(t, s, r):
                    sp.wait_ge(scaled, t + 1)
                    sp.dma_start(xin[:, s, :], x[bass.ds(t * P, P), :]).then_inc(ld[s], DMA)
                pairs(sp, TT, body)

            @block.scalar
            def _(act):
                def body(t, s, r):
                    act.wait_ge(ld[s], (r + 1) * DMA)
                    act.wait_ge(inv, t + 1)
                    act.activation(sq[:, s, :], xin[:, s, :], ACT.Square,
                                   accum_out=st[:, s, 0:1]).then_inc(summed, 1)
                    act.wait_ge(mean, t + 1)
                    act.activation(st[:, s, 2:3], st[:, s, 1:2], ACT.Sqrt).then_inc(root, 1)
                    act.wait_ge(gained, t + 3)
                    act.activation(XT[:, 0, :, bass.ds(t * P, P)], xg[:, s, :, :], ACT.Copy).then_inc(hi, 1)
                pairs(act, TT, body)

            @block.vector
            def _(dve):
                dve.sem_inc(scaled, 2)
                dve.sem_inc(gained, 2)
                dve.sem_inc(inv, 2)
                dve.wait_ge(g_ld, DMA)

                def body(t, s, r):
                    dve.wait_ge(summed, t + 1)
                    dve.tensor_scalar(st[:, s, 1:2], st[:, s, 0:1], 1.0 / D, EPS, ALU.mult, ALU.add).then_inc(mean, 1)
                    dve.wait_ge(root, t + 1)
                    dve.reciprocal(st[:, s, 3:4], st[:, s, 2:3]).then_inc(inv, 1)
                    dve.wait_ge(inv, t + 3)
                    dve.wait_ge(turned, t + 1)
                    dve.tensor_scalar(xs[:, s, :], xin[:, s, :], st[:, s, 3:4], None, ALU.mult).then_inc(scaled, 1)
                    dve.wait_ge(turned, t + 3)
                    dve.wait_ge(stored, t + 1)
                    dve.tensor_tensor(xg[:, s, :, :], pT[:, s, :, :],
                                      gc[:, :].unsqueeze(2).to_broadcast([P, KD, P]), ALU.mult).then_inc(gained, 1)
                pairs(dve, TT, body)

            @block.gpsimd
            def _(pool):
                pool.sem_inc(stored, 2)

                def body(t, s, r):
                    pool.wait_ge(hi, t + 1)
                    pool.tensor_tensor(XT[:, 1, :, bass.ds(t * P, P)], xg[:, s, :, :],
                                       XT[:, 0, :, bass.ds(t * P, P)].bitcast(F32), ALU.subtract).then_inc(stored, 1)
                pairs(pool, TT, body)

            @block.tensor
            def _(pe):
                pe.sem_inc(turned, 2)

                def body(t, s, r):
                    pe.wait_ge(scaled, t + 3)
                    pe.wait_ge(gained, t + 1)
                    for k in range(KD):
                        last = pe.transpose(pT[:, s, k, :], xs[:, s, k * P:(k + 1) * P], ident[:, :])
                    last.then_inc(turned, 1)
                pairs(pe, TT, body)


def project(nc, tag, XT, segments):
    G, B = 8, 4
    with Place(nc, tag) as pl:
        w = pl.sb("w", [P, 2, KD, NC])
        ws = pl.sb("ws", [P, 2, 2, KD, NC], F32R)
        stage = pl.sb("stage", [P, B, NC])
        acc = pl.ps("acc", [P, B, NC])
        w_ld = [pl.sem(f"w_loaded{s}") for s in range(2)]
        rounded = pl.sem("w_rounded")
        split = pl.sem("w_split")
        out_st = pl.store_sem("out_stored")
        staged = pl.sem("stage_free")
        summed = pl.sem("group_summed")
        moved = pl.sem("group_moved")

        def each(eng, work):
            done = 0
            for seg in segments:
                width = min(NC, seg[0].shape[1])
                chunks = seg[0].shape[1] // width
                assert done % 2 == 0 and width * chunks == seg[0].shape[1]
                pairs(eng, chunks, lambda c, s, r: work(c + done, s, r + done // 2, c * width, width, seg))
                done += chunks

        with nc.Block() as block:
            @block.sync
            def _(sp):
                def body(c, s, r, col, width, seg):
                    sp.wait_ge(split, c + 1)
                    sp.dma_start(w[:, s, :, :width],
                                 seg[0].rearrange("(k p) n -> p k n", p=P)[:, :, bass.ds(col, width)]).then_inc(w_ld[s], DMA)
                each(sp, body)

            @block.vector
            def _(dve):
                dve.sem_inc(split, 2)

                def body(c, s, r, col, width, seg):
                    dve.wait_ge(w_ld[s], (r + 1) * DMA)
                    dve.wait_ge(summed, G * c + G)
                    dve.tensor_copy(ws[:, s, 0, :, :width], w[:, s, :, :width]).then_inc(rounded, 1)
                    dve.wait_ge(rounded, c + 1)
                    dve.tensor_tensor(ws[:, s, 1, :, :width], w[:, s, :, :width], ws[:, s, 0, :, :width].bitcast(F32),
                                      ALU.subtract).then_inc(split, 1)
                each(dve, body)

            @block.tensor
            def _(pe):
                pe.sem_inc(summed, 2 * G)

                def body(c, s, r, col, width, seg):
                    pe.wait_ge(split, c + 3)
                    for g in range(G):
                        pe.wait_ge(moved, c * G + g + 1)
                        if seg[2]:
                            m, h = g // 2, g % 2
                            mm = split_product(pe, acc[:, g % B, :], lambda p, k: ws[:, s, p, k, m * P:(m + 1) * P],
                                               lambda p, k: XT[:, p, k, h * NC:(h + 1) * NC], range(KD))
                        else:
                            mm = split_product(pe, acc[:, g % B, :width], lambda p, k: XT[:, p, k, g * P:(g + 1) * P],
                                               lambda p, k: ws[:, s, p, k, :width], range(KD))
                        mm.then_inc(summed, 1)
                each(pe, body)

            @block.scalar
            def _(act):
                act.sem_inc(moved, B)

                def body(c, s, r, col, width, seg):
                    n = NC if seg[2] else width
                    for g in range(G):
                        act.wait_ge(summed, c * G + g + 1 + 2 * G)
                        act.wait_ge(staged, c * G + g + 1)
                        act.activation(stage[:, g % B, :n], acc[:, g % B, :n], seg[3]).then_inc(moved, 1)
                each(act, body)

            @block.gpsimd
            def _(pool):
                pool.sem_inc(staged, B)

                def body(c, s, r, col, width, seg):
                    n = NC if seg[2] else width
                    for g in range(G):
                        if seg[2]:
                            dst = seg[1][bass.ds(col + (g // 2) * P, P), (g % 2) * NC:(g % 2 + 1) * NC]
                        else:
                            dst = seg[1][g * P:(g + 1) * P, bass.ds(col, width)]
                        pool.wait_ge(moved, c * G + g + 1 + B)
                        pool.dma_start(dst, stage[:, g % B, :n]).then_inc(out_st, DMA)
                        pool.wait_ge(out_st, (c * G + g + 1) * DMA)
                        pool.sem_inc(staged, 1)
                each(pool, body)


def reduce_tokens(nc, tag, AT, W, res, out):
    K = W.shape[0]
    KP = K // (2 * P)
    Av = AT.rearrange("(i k p) t -> i p k t", p=P, k=2)
    Wv = W.rearrange("(i k p) n -> i p k n", p=P, k=2)
    last_from = 1 + (KP - 2) // 2 * 2

    with Place(nc, tag) as pl:
        a = pl.sb("a", [P, 2, 2, L])
        w = pl.sb("w", [P, 2, 2, NC])
        sa = pl.sb("sa", [P, 2, 2, 2, L], F32R)
        sw = pl.sb("sw", [P, 2, 2, 2, NC], F32R)
        y = pl.sb("y", [P, TT, D])
        acc = pl.ps("acc", [P, TT, NC])
        ld = [pl.sem(f"item_loaded{s}") for s in range(2)]
        res_ld = pl.store_sem("residual_loaded")
        rounded = pl.sem("item_rounded")
        split = pl.sem("item_split")
        used = pl.sem("item_used")
        summed = pl.sem("tile_summed")
        added = pl.sem("tile_added")
        out_st = pl.store_sem("out_stored")

        def items(eng, h, body):
            def call(k, turn, j):
                i = h * KP + (k if turn is None else 1 + j)
                s = i % 2
                if turn is None:
                    body(k, i, s, i // 2, k == 0, k == KP - 1)
                else:
                    body(1 + j + turn * 2, i + turn * 2, s, i // 2 + turn, False, False)
            call(0, None, 0)
            if last_from > 1:
                with eng.Fori(0, (last_from - 1) // 2) as r:
                    call(None, r, 0)
                    call(None, r, 1)
            for k in range(last_from, KP):
                call(k, None, 0)

        with nc.Block() as block:
            @block.sync
            def _(sp):
                for h in range(2):
                    def body(k, i, s, before, first, last):
                        sp.wait_ge(split, i + 1)
                        sp.dma_start(a[:, s, :, :], Av[bass.ds(k, 1)].rearrange("i p k t -> (i p) k t")).then_inc(ld[s], DMA)
                        sp.dma_start(w[:, s, :, :], Wv[bass.ds(k, 1), :, :, h * NC:(h + 1) * NC].rearrange(
                            "i p k n -> (i p) k n")).then_inc(ld[s], DMA)
                    items(sp, h, body)

            @block.tensor
            def _(pe):
                pe.sem_inc(used, 2)
                for h in range(2):
                    def body(k, i, s, before, first, last):
                        pe.wait_ge(split, i + 3)
                        for t in range(TT):
                            if first and h:
                                pe.wait_ge(added, t + 1)
                            mm = split_product(pe, acc[:, t, :], lambda p, k: sa[:, s, p, k, t * P:(t + 1) * P],
                                               lambda p, k: sw[:, s, p, k, :], range(2), start=first, stop=last)
                            if last:
                                mm.then_inc(summed, 1)
                        if not last:
                            mm.then_inc(used, 1)
                        elif not h:
                            pe.wait_ge(summed, TT)
                            pe.sem_inc(used, 1)
                    items(pe, h, body)

            @block.scalar
            def _(act):
                for h in range(2):
                    def body(k, i, s, before, first, last):
                        act.wait_ge(ld[s], (before + 1) * 2 * DMA)
                        act.wait_ge(used, i + 1)
                        act.activation(sa[:, s, 0, :, :], a[:, s, :, :], ACT.Copy)
                        act.activation(sw[:, s, 0, :, :], w[:, s, :, :], ACT.Copy).then_inc(rounded, 1)
                    items(act, h, body)

            @block.vector
            def _(dve):
                dve.sem_inc(split, 2)

                def body(k, i, s, before, first, last):
                    dve.wait_ge(rounded, i + 1)
                    dve.tensor_tensor(sa[:, s, 1, :, :], a[:, s, :, :], sa[:, s, 0, :, :].bitcast(F32), ALU.subtract)
                    dve.tensor_tensor(sw[:, s, 1, :, :], w[:, s, :, :], sw[:, s, 0, :, :].bitcast(F32),
                                      ALU.subtract).then_inc(split, 1)
                for h in range(2):
                    items(dve, h, body)
                    if h == 0:
                        dve.wait_ge(res_ld, DMA)
                    for t in range(TT):
                        dve.wait_ge(summed, h * TT + t + 1)
                        yt = y[:, t, h * NC:(h + 1) * NC]
                        dve.tensor_tensor(yt, acc[:, t, :], yt, ALU.add).then_inc(added, 1)

            @block.gpsimd
            def _(pool):
                pool.dma_start(y[:, :, :], res.rearrange("(t p) n -> p t n", p=P)).then_inc(res_ld, DMA)
                for h in range(2):
                    for t in range(TT):
                        pool.wait_ge(added, h * TT + t + 1)
                        pool.dma_start(out[t * P:(t + 1) * P, h * NC:(h + 1) * NC],
                                       y[:, t, h * NC:(h + 1) * NC]).then_inc(out_st, DMA)
                pool.wait_ge(out_st, 2 * TT * DMA)


def swiglu_up(nc, tag, XT, Wg, Wu, hT):
    F = Wg.shape[1]
    CW = 2 * P
    chunks, G = F // CW, 4
    Wgv = Wg.rearrange("(k p) n -> p k n", p=P)
    Wuv = Wu.rearrange("(k p) n -> p k n", p=P)
    with Place(nc, tag) as pl:
        w = pl.sb("w", [P, 2, 2, KD, CW])
        ws = pl.sb("ws", [P, 2, 2, 2, KD, CW], F32R)
        sil = pl.sb("sil", [P, 2, NC])
        h = pl.sb("h", [P, 2, NC])
        acc = pl.ps("acc", [P, 2, 2, NC])
        w_ld = [pl.sem(f"w_loaded{s}") for s in range(2)]
        rounded = pl.sem("w_rounded")
        passed = pl.sem("passed")
        split = pl.sem("w_split")
        summed = pl.sem("group_summed")
        silu_done = pl.sem("silu_done")
        gated = pl.sem("group_gated")
        out_st = pl.sem("out_stored")
        h_free = pl.sem("h_free")
        with nc.Block() as block:
            @block.sync
            def _(sp):
                def body(c, s, r):
                    sp.wait_ge(split, c + 1)
                    sp.dma_start(w[:, s, 0, :, :], Wgv[:, :, bass.ds(c * CW, CW)]).then_inc(w_ld[s], DMA)
                    sp.dma_start(w[:, s, 1, :, :], Wuv[:, :, bass.ds(c * CW, CW)]).then_inc(w_ld[s], DMA)
                pairs(sp, chunks, body)

            @block.tensor
            def _(pe):
                pe.sem_inc(summed, 2 * G)

                def body(c, s, r):
                    pe.wait_ge(split, c + 3)
                    for g in range(G):
                        m, half = g // 2, g % 2
                        pe.wait_ge(gated, c * G + g + 1)
                        for u in range(2):
                            mm = split_product(pe, acc[:, g % 2, u, :], lambda p, k: ws[:, s, p, u, k, m * P:(m + 1) * P],
                                               lambda p, k: XT[:, p, k, half * NC:(half + 1) * NC], range(KD))
                        mm.then_inc(summed, 1)
                pairs(pe, chunks, body)

            @block.scalar
            def _(act):
                act.sem_inc(h_free, 2)

                def body(c, s, r):
                    for g in range(G):
                        act.wait_ge(summed, c * G + g + 1 + 2 * G)
                        act.wait_ge(gated, c * G + g + 1)
                        act.activation(sil[:, g % 2, :], acc[:, g % 2, 0, :], ACT.Silu).then_inc(silu_done, 1)
                        act.wait_ge(gated, c * G + g + 3)
                        act.dma_start(hT[bass.ds(c * CW + (g // 2) * P, P), (g % 2) * NC:(g % 2 + 1) * NC],
                                      h[:, g % 2, :]).then_inc(out_st, DMA)
                        act.wait_ge(out_st, (c * G + g + 1) * DMA)
                        act.sem_inc(h_free, 1)
                pairs(act, chunks, body)

            @block.vector
            def _(dve):
                dve.sem_inc(gated, 2)

                def body(c, s, r):
                    for g in range(G):
                        dve.wait_ge(silu_done, c * G + g + 1)
                        dve.wait_ge(h_free, c * G + g + 1)
                        dve.tensor_tensor(h[:, g % 2, :], acc[:, g % 2, 1, :], sil[:, g % 2, :],
                                          ALU.mult).then_inc(gated, 1)
                pairs(dve, chunks, body)

            @block.gpsimd
            def _(pool):
                pool.sem_inc(split, 2)

                def body(c, s, r):
                    pool.wait_ge(w_ld[s], (r + 1) * 2 * DMA)
                    pool.wait_ge(summed, G * c + G)
                    pool.sem_inc(passed, 1)
                    pool.tensor_copy(ws[:, s, 0], w[:, s]).then_inc(rounded, 1)
                    pool.wait_ge(rounded, c + 1)
                    pool.tensor_tensor(ws[:, s, 1], w[:, s], ws[:, s, 0].bitcast(F32), ALU.subtract).then_inc(split, 1)
                pairs(pool, chunks, body)


def merge_branches(nc, tag, ysT, yaT, Ws, Wa, gT, mT):
    KS = 4
    G = 2 * KD
    with Place(nc, tag) as pl:
        w = pl.sb("w", [P, 2, KS, D])
        y = pl.sb("y", [P, 2, KS, L])
        g = pl.sb("g", [P, 2, 2, NC])
        part = pl.sb("part", [P, 2, 2, NC])
        m = pl.sb("m", [P, 2, NC])
        acc = pl.ps("acc", [P, 2, 2, NC])
        in_ld = pl.sem("inputs_loaded")
        g_ld = [pl.sem(f"gates_loaded{s}") for s in range(2)]
        summed = pl.sem("group_summed")
        gated = pl.sem("group_gated")
        merged = pl.sem("group_merged")
        out_st = pl.store_sem("out_stored")
        with nc.Block() as block:
            @block.sync
            def _(sp):
                for b, (Y, W) in enumerate(((ysT, Ws), (yaT, Wa))):
                    sp.dma_start(y[:, b, :, :], Y.rearrange("(k p) t -> p k t", p=P)).then_inc(in_ld, DMA)
                    sp.dma_start(w[:, b, :, :], W.rearrange("(k p) n -> p k n", p=P)).then_inc(in_ld, DMA)
                for i in range(G):
                    n, h, s = i // 2, i % 2, i % 2
                    sp.wait_ge(gated, i + 1)
                    for b in range(2):
                        sp.dma_start(g[:, s, b, :], gT[b * D + n * P:b * D + (n + 1) * P,
                                                       h * NC:(h + 1) * NC]).then_inc(g_ld[s], DMA)

            @block.tensor
            def _(pe):
                pe.wait_ge(in_ld, 4 * DMA)
                for i in range(G):
                    n, h, s = i // 2, i % 2, i % 2
                    pe.wait_ge(gated, i + 1)
                    for b in range(2):
                        for k in range(KS):
                            mm = pe.matmul(acc[:, s, b, :], w[:, b, k, n * P:(n + 1) * P],
                                           y[:, b, k, h * NC:(h + 1) * NC], start=k == 0, stop=k == KS - 1)
                    mm.then_inc(summed, 1)

            @block.vector
            def _(dve):
                dve.sem_inc(gated, 2)
                for i in range(G):
                    s = i % 2
                    dve.wait_ge(summed, i + 1)
                    dve.wait_ge(g_ld[s], (i // 2 + 1) * 2 * DMA)
                    dve.wait_ge(merged, i + 1)
                    dve.tensor_tensor(part[:, s, :, :], acc[:, s, :, :], g[:, s, :, :], ALU.mult).then_inc(gated, 1)

            @block.gpsimd
            def _(pool):
                pool.sem_inc(merged, 2)
                for i in range(G):
                    n, h, s = i // 2, i % 2, i % 2
                    pool.wait_ge(gated, i + 3)
                    pool.tensor_tensor(m[:, s, :], part[:, s, 0, :], part[:, s, 1, :], ALU.add).then_inc(merged, 1)
                    pool.wait_ge(merged, i + 3)
                    pool.dma_start(mT[n * P:(n + 1) * P, h * NC:(h + 1) * NC], m[:, s, :]).then_inc(out_st, DMA)
                    pool.wait_ge(out_st, (i + 1) * DMA)


S_GROUPS, S_CH, S_N = 32, 16, 64
S_J = S_GROUPS // 2
S_T = 8
S_C = L // S_T
S_W = S_GROUPS * S_CH


def s5_branch(nc, tag, p1, prm, ident, outT):
    with Place(nc, tag) as pl:
        uc = pl.sb("uc", [S_C, S_T, S_W])
        U = pl.sb("U", [P, S_GROUPS, S_C])
        MT = pl.sb("MT", [P, S_GROUPS, P])
        WT = pl.sb("WT", [P, 2, S_J, P])
        Wn = pl.sb("Wn", [P, 2, S_J, S_T, S_CH])
        CP = pl.sb("CP", [P, 2, S_J, S_T + 1, S_CH])
        cB = pl.sb("cB", [P, 2, S_J, S_CH])
        E = pl.sb("E", [P, 2, S_J, S_C])
        w = pl.sb("w", [P, 2, S_J, S_C])
        t1 = pl.sb("t1", [P, S_J * S_C])
        t2 = pl.sb("t2", [P, S_J * S_C])
        K16 = pl.sb("K16", [S_CH, S_GROUPS, P])
        small = pl.sb("small", [P, 40, S_J])
        PW = pl.sb("PW", [P, 2, S_T + 1, S_J])
        Bn = pl.sb("Bn", [P, 2, S_J, S_CH])
        Cn = pl.sb("Cn", [P, 2, S_J, S_CH])
        z = Wn[:, :, :, :, :].rearrange("p a j s q -> p a (j s q)")
        ug = w[:, :, :, :].rearrange("p a j c -> p (a j c)").rearrange("p (g s q) -> p g s q", s=S_T, q=S_CH)
        names = ["ar", "ai", "ldt", "dt", "x", "y", "k", "r", "h", "sn", "cs", "em1", "mag", "tmp", "tmp2",
                 "den", "nr", "cr", "ci", "v", "e", "m8", "ur", "ui", "vr", "vi", "n2"]
        at = {n: small[:, i, :] for i, n in enumerate(names)}

        loaded = pl.sem("loaded")
        pl_dve = pl.sem("dve")
        phase_in = pl.sem("phase_argument_ready")
        phase = pl.sem("phase_ready")
        powers = pl.sem("powers_ready")
        pl_pool = pl.sem("pool")
        regrouped = pl.sem("u_regrouped")
        with nc.Block() as block:
            @block.sync
            def _(sp):
                def slow(dst, src):
                    sp.dma_start(dst, src, allow_slow_non_contiguous=True).then_inc(loaded, DMA)
                for n, a in (("ar", prm["A_re"]), ("ai", prm["A_im"])):
                    slow(at[n], a.rearrange("j q -> q j"))
                for q in range(2):
                    slow(at["ldt"][q * S_N:(q + 1) * S_N, :],
                         prm["log_dt"].rearrange("(j q) -> q j", q=2)[q, :].partition_broadcast(S_N))
                for i, n in enumerate(("B_re", "B_im")):
                    sp.dma_start(Bn[:, i, :, :], prm[n].rearrange("j q c -> q j c")).then_inc(loaded, DMA)
                for i, n in enumerate(("C_re", "C_im")):
                    sp.dma_start(Cn[:, i, :, :], prm[n].rearrange("j q c -> q j c")).then_inc(loaded, DMA)
                sp.dma_start(uc[:, :, :], p1[:, 0:S_W].rearrange("(c s) f -> c s f", s=S_T)).then_inc(loaded, DMA)

            @block.vector
            def _(dve):
                link = Link(dve, pl_dve)
                dve.wait_ge(loaded, 9 * DMA)

                def tt(o, a, b, op=ALU.mult):
                    link(dve.tensor_tensor(at[o], at[a], at[b], op))

                def ts(o, a, m, b=0.0):
                    link(dve.tensor_scalar(at[o], at[a], m, b, ALU.mult, ALU.add))

                def expm1_of(o, a, doublings):
                    ts("v", a, 1.0 / 256)
                    ts(o, "v", 1.0 / 120, 1.0 / 24)
                    for q in (1.0 / 6, 0.5, 1.0):
                        tt(o, o, "v")
                        ts(o, o, 1.0, q)
                    tt(o, o, "v")
                    for _ in range(doublings):
                        link(dve.scalar_tensor_tensor(at[o], at[o], 2.0, at[o], ALU.add, ALU.mult))

                def square(o, a):
                    tt(o, a, a)

                expm1_of("e", "ldt", 5)
                ts("dt", "e", 1.0, 1.0)
                for _ in range(3):
                    square("dt", "dt")
                tt("x", "ar", "dt")
                tt("y", "ai", "dt")
                ts("k", "y", 1.0 / (2 * np.pi), 12582912.0)
                ts("k", "k", 1.0, -12582912.0)
                c1 = 6.28125
                c2 = float(np.float32(np.round((2 * np.pi - c1) * 2 ** 21) / 2 ** 21))
                c3 = 2 * np.pi - c1 - c2
                link(dve.scalar_tensor_tensor(at["r"], at["k"], -c1, at["y"], ALU.mult, ALU.add))
                link(dve.scalar_tensor_tensor(at["r"], at["k"], -c2, at["r"], ALU.mult, ALU.add))
                link(dve.scalar_tensor_tensor(at["r"], at["k"], -c3, at["r"], ALU.mult, ALU.add))
                link(dve.tensor_scalar(at["r"], at["r"], 3.1415925, -3.1415925, ALU.min, ALU.max))
                link(dve.scalar_tensor_tensor(at["h"], at["r"], -1.0, at["r"], ALU.mult, ALU.max))
                dve.tensor_scalar(at["h"], at["h"], -1.0, np.pi / 2, ALU.mult, ALU.add).then_inc(phase_in, 1)
                expm1_of("em1", "x", 8)
                expm1_of("e", "x", 5)
                ts("mag", "e", 1.0, 1.0)
                for _ in range(3):
                    square("mag", "mag")
                square("m8", "mag")
                square("m8", "m8")
                square("m8", "m8")
                dve.wait_ge(phase, 2)
                square("n2", "cs")
                square("tmp", "sn")
                tt("n2", "n2", "tmp", ALU.add)
                ts("n2", "n2", -0.5, 1.5)
                tt("cs", "cs", "n2")
                tt("sn", "sn", "n2")
                link(dve.memset(PW[:, 0, 0, :], 1.0))
                link(dve.memset(PW[:, 1, 0, :], 0.0))
                link(dve.tensor_tensor(PW[:, 0, 1, :], at["mag"], at["cs"], ALU.mult))
                link(dve.tensor_tensor(PW[:, 1, 1, :], at["mag"], at["sn"], ALU.mult))
                ts("tmp", "cs", 1.0, -1.0)
                tt("nr", "em1", "cs")
                tt("nr", "nr", "tmp", ALU.add)
                square("den", "ar")
                square("tmp", "ai")
                tt("den", "den", "tmp", ALU.add)
                link(dve.reciprocal(at["den"], at["den"]))
                abi = PW[:, 1, 1, :]
                tt("cr", "nr", "ar")
                link(dve.tensor_tensor(at["tmp"], abi, at["ai"], ALU.mult))
                tt("cr", "cr", "tmp", ALU.add)
                tt("cr", "cr", "den")
                link(dve.tensor_tensor(at["ci"], abi, at["ar"], ALU.mult))
                tt("tmp", "nr", "ai")
                tt("ci", "ci", "tmp", ALU.subtract)
                tt("ci", "ci", "den")

                def cmul(eng, ln, o, a, b, shape, neg=False):
                    n = int(np.prod(shape[1:]))
                    pat = {2: None, 3: "p (a b) -> p a b"}[len(shape)]
                    u, v = t1[:, 0:n], t2[:, 0:n]
                    if pat:
                        u, v = (q.rearrange(pat, b=shape[2]) for q in (u, v))
                    ln.mark(eng.tensor_tensor(u, a[0], b[0], ALU.mult))
                    ln(eng.tensor_tensor(v, a[1], b[1], ALU.mult))
                    ln(eng.tensor_tensor(o[0], u, v, ALU.subtract))
                    ln.mark(eng.tensor_tensor(u, a[0], b[1], ALU.mult))
                    ln(eng.tensor_tensor(v, a[1], b[0], ALU.mult))
                    if neg:
                        ln(eng.scalar_tensor_tensor(o[1], u, -1.0, v, ALU.mult, ALU.subtract))
                    else:
                        ln(eng.tensor_tensor(o[1], u, v, ALU.add))

                def pw(k):
                    return PW[:, 0, k, :], PW[:, 1, k, :]

                for n in (1, 2, 4):
                    f = [q.unsqueeze(1).to_broadcast([P, n, S_J]) for q in pw(n)]
                    cmul(dve, link, (PW[:, 0, n + 1:2 * n + 1, :], PW[:, 1, n + 1:2 * n + 1, :]),
                         (PW[:, 0, 1:n + 1, :], PW[:, 1, 1:n + 1, :]), f, (P, n, S_J))

                def wide(q):
                    return q.unsqueeze(2).to_broadcast([P, S_J, S_CH])

                shape = (P, S_J, S_CH)
                cmul(dve, link, (cB[:, 0, :, :], cB[:, 1, :, :]), (Bn[:, 0, :, :], Bn[:, 1, :, :]),
                     (wide(at["cr"]), wide(at["ci"])), shape)
                for s in range(S_T):
                    cmul(dve, link, (Wn[:, 0, :, s, :], Wn[:, 1, :, s, :]), (cB[:, 0, :, :], cB[:, 1, :, :]),
                         [wide(q) for q in pw(S_T - 1 - s)], shape)
                for k in range(S_T + 1):
                    cmul(dve, link, (CP[:, 0, :, k, :], CP[:, 1, :, k, :]), (Cn[:, 0, :, :], Cn[:, 1, :, :]),
                         [wide(q) for q in pw(k)], shape, neg=True)
                u_, v_ = ("cs", "sn"), ("vr", "vi")
                for _ in range(3):
                    cmul(dve, link, (at[v_[0]], at[v_[1]]), (at[u_[0]], at[u_[1]]), (at[u_[0]], at[u_[1]]), (P, S_J))
                    u_, v_ = v_, (("ur", "ui") if v_[0] == "vr" else ("vr", "vi"))
                link(dve.memset(E[:, 0, :, 0:1], 1.0))
                link(dve.memset(E[:, 1, :, 0:1], 0.0))
                n = 1
                while n < S_C:
                    f = [at[q].unsqueeze(2).to_broadcast([P, S_J, n]) for q in u_]
                    cmul(dve, link, (E[:, 0, :, n:2 * n], E[:, 1, :, n:2 * n]), (E[:, 0, :, 0:n], E[:, 1, :, 0:n]), f,
                         (P, S_J, n))
                    n *= 2
                    if n < S_C:
                        cmul(dve, link, (at[v_[0]], at[v_[1]]), (at[u_[0]], at[u_[1]]), (at[u_[0]], at[u_[1]]),
                             (P, S_J))
                        u_, v_ = v_, u_

            @block.scalar
            def _(act):
                act.wait_ge(phase_in, 1)
                act.activation(at["sn"], at["r"], ACT.Sin).then_inc(phase, 1)
                act.activation(at["cs"], at["h"], ACT.Sin).then_inc(phase, 1)
                act.wait_ge(loaded, 9 * DMA)
                for s in range(S_T):
                    act.activation(ug[:, :, s, :], uc[:, s, :].rearrange("c (g q) -> c g q", q=S_CH),
                                   ACT.Copy).then_inc(regrouped, 1)
                act.wait_ge(regrouped, S_T)

            @block.gpsimd
            def _(pool):
                pool.memset(MT[:, :, :], 0.0).then_inc(pl_pool, 1)
                pool.wait_ge(pl_pool, 1)

        made = pl.sem("group_made")
        moved = pl.sem("group_moved")
        shifted = pl.sem("kernels_shifted")
        acc = pl.ps("acc", [P, 8, 4, P])
        groups = [("U", i) for i in range(8)] + [("W", i) for i in range(8)] + [("K", i) for i in range(8)]
        with nc.Block() as block:
            @block.tensor
            def _(pe):
                for n, (kind, i) in enumerate(groups):
                    b = n % 4
                    if n >= 4:
                        pe.wait_ge(moved, n - 3)
                    for q in range(4):
                        if kind == "U":
                            g = 4 * i + q
                            mm = pe.transpose(acc[:, b, q, :], ug[:, g, :, :].rearrange("c s q -> c (s q)"), ident[:, :])
                        elif kind == "W":
                            c, j = i // 4, (i % 4) * 4 + q
                            mm = pe.transpose(acc[:, b, q, :], Wn[:, c, j, :, :].rearrange("p s q -> p (s q)"), ident[:, :])
                        else:
                            j, a = 4 * (i // 2) + q, i % 2
                            rows = slice(a * S_N, (a + 1) * S_N)
                            for c in range(2):
                                mm = pe.matmul(acc[0:S_CH, b, q, :], cB[rows, c, j, :], CP[rows, c, j, 0:S_T, :],
                                               start=c == 0, stop=c == 1)
                    mm.then_inc(made, 1)

            @block.scalar
            def _(act):
                for n, (kind, i) in enumerate(groups):
                    b = n % 4
                    act.wait_ge(made, n + 1)
                    if kind == "U":
                        dst, src = U[:, 4 * i:4 * i + 4, :], acc[:, b, :, :]
                    elif kind == "W":
                        j = (i % 4) * 4
                        dst, src = WT[:, i // 4, j:j + 4, :], acc[:, b, :, :]
                    else:
                        g = 8 * (i // 2) + i % 2
                        dst, src = K16[:, g:g + 7:2, :], acc[0:S_CH, b, :, :]
                    act.activation(dst, src, ACT.Copy).then_inc(moved, 1)

            @block.sync
            def _(sp):
                sp.wait_ge(moved, len(groups))
                for s in range(S_T):
                    sp.dma_start(MT[s * S_CH:(s + 1) * S_CH, :, s * S_CH:P],
                                 K16[:, :, 0:P - s * S_CH]).then_inc(shifted, DMA)
                sp.wait_ge(shifted, S_T * DMA)

        win = pl.sem("inputs_summed")
        w_mv = pl.sem("inputs_moved")
        d2 = pl.sem("dve_scan")
        d_ld = pl.sem("D_loaded")
        skip = pl.sem("skip_ready")
        magc = PW
        Dc = K16
        m8w = Cn[:, :, :, :]
        dsk = pl.sb("dsk", [P, S_W])
        zc = E
        with nc.Block() as block:
            @block.sync
            def _(sp):
                sp.dma_start(dsk[:, :], prm["D_skip"].partition_broadcast(P)).then_inc(d_ld, DMA)

            @block.gpsimd
            def _(pool):
                pool.wait_ge(d_ld, DMA)
                pool.tensor_tensor(uc[:, :, :], uc[:, :, :], dsk[:, :].unsqueeze(1).to_broadcast([P, S_T, S_W]),
                                   ALU.mult).then_inc(skip, 1)
                pool.wait_ge(skip, 1)

            @block.tensor
            def _(pe):
                for n in range(8):
                    c, i = n // 4, n % 4
                    for q in range(4):
                        j = 4 * i + q
                        for a in range(2):
                            rows = slice(a * S_N, (a + 1) * S_N)
                            mm = pe.matmul(acc[rows, n, q, :], WT[:, c, j, rows], U[:, 2 * j + a, :],
                                           start=True, stop=True, skip_group_check=True)
                    mm.then_inc(win, 1)

            @block.scalar
            def _(act):
                for n in range(8):
                    act.wait_ge(win, n + 1)
                    i = n % 4
                    act.activation(w[:, n // 4, 4 * i:4 * i + 4, :], acc[:, n, :, :], ACT.Copy).then_inc(w_mv, 1)

            @block.vector
            def _(dve):
                link = Link(dve, d2)
                dve.wait_ge(w_mv, 8)
                wr, wi = w[:, 0, :, :], w[:, 1, :, :]
                er, ei = E[:, 0, :, :], E[:, 1, :, :]
                a3 = [q[:, :].rearrange("p (j c) -> p j c", c=S_C) for q in (t1, t2)]
                z3 = [z[:, q, :].rearrange("p (j c) -> p j c", c=S_C) for q in range(2)]
                link.mark(dve.tensor_tensor(a3[0], wr, er, ALU.mult))
                link(dve.tensor_tensor(a3[1], wi, ei, ALU.mult))
                link(dve.tensor_tensor(z3[0], a3[0], a3[1], ALU.add))
                link.mark(dve.tensor_tensor(a3[0], wi, er, ALU.mult))
                link(dve.tensor_tensor(a3[1], wr, ei, ALU.mult))
                link(dve.tensor_tensor(z3[1], a3[0], a3[1], ALU.subtract))
                link(dve.tensor_scalar(a3[0], er, 0.0, None, ALU.mult))
                link(dve.tensor_tensor(a3[0], a3[0], at["m8"].unsqueeze(2).to_broadcast([P, S_J, S_C]), ALU.add))
                link(dve.memset(a3[0][:, :, 0:1], 0.0))
                for q in range(2):
                    link(dve.tensor_tensor_scan(z[:, q, :], t1[:, :], z[:, q, :], 0.0, ALU.mult, ALU.add))
                n = S_C - 1
                zr, zi = z3[0][:, :, 0:n], z3[1][:, :, 0:n]
                er, ei = E[:, 0, :, 0:n], E[:, 1, :, 0:n]
                x1, x2 = a3[0][:, :, 0:n], a3[1][:, :, 0:n]
                link(dve.memset(w[:, :, :, 0:1], 0.0))
                link.mark(dve.tensor_tensor(x1, zr, er, ALU.mult))
                link(dve.tensor_tensor(x2, zi, ei, ALU.mult))
                link(dve.tensor_tensor(w[:, 0, :, 1:S_C], x1, x2, ALU.subtract))
                link.mark(dve.tensor_tensor(x1, zr, ei, ALU.mult))
                link(dve.tensor_tensor(x2, zi, er, ALU.mult))
                link(dve.tensor_tensor(w[:, 1, :, 1:S_C], x1, x2, ALU.add))

        yT = t1_yT = pl.sb("yT", [P, 4, L])
        wg = pl.sb("wg", [P, 4, S_W])
        bg = pl.sb("bg", [P, 4])
        sig = pl.sb("sig", [P, 2, NC])
        y_sum = pl.sem("outputs_summed")
        y_add = pl.sem("outputs_added")
        y_act = pl.sem("gelu_done")
        y_tr = pl.sem("y_transposed")
        y_mv = pl.sem("y_moved")
        glu_ld = pl.sem("glu_loaded")
        glu = pl.sem("glu_summed")
        sigd = pl.sem("sigmoid_done")
        gated = pl.sem("gated")
        out_st = pl.store_sem("out_stored")
        with nc.Block() as block:
            @block.sync
            def _(sp):
                sp.dma_start(wg[:, :, :], prm["w_glu"].rearrange("(k p) n -> p k n", p=P)).then_inc(glu_ld, DMA)
                sp.dma_start(bg[:, :], prm["b_glu"].rearrange("(k p) -> p k", p=P),
                             allow_slow_non_contiguous=True).then_inc(glu_ld, DMA)

            @block.tensor
            def _(pe):
                for n in range(8):
                    for q in range(4):
                        j = 4 * (n // 2) + q
                        g, rows = 2 * j + n % 2, slice((n % 2) * S_N, (n % 2 + 1) * S_N)
                        pe.matmul(acc[:, n, q, :], U[:, g, :], MT[:, g, :], start=True, stop=False)
                        pe.matmul(acc[:, n, q, :], w[rows, 0, j, :], CP[rows, 0, j, 1:S_T + 1, :], start=False, stop=False)
                        mm = pe.matmul(acc[:, n, q, :], w[rows, 1, j, :], CP[rows, 1, j, 1:S_T + 1, :],
                                       start=False, stop=True)
                    mm.then_inc(y_sum, 1)
                pe.wait_ge(y_act, 8)
                for s in range(S_T):
                    pe.wait_ge(y_add, s + 1)
                    for f in range(4):
                        mm = pe.transpose(acc[:, s, f, :], uc[:, s, f * P:(f + 1) * P], ident[:, :])
                    mm.then_inc(y_tr, 1)
                pe.wait_ge(y_mv, S_T)
                pe.wait_ge(glu_ld, 2 * DMA)
                for i in range(8):
                    n, h = i // 2, i % 2
                    for k in range(4):
                        mm = pe.matmul(acc[:, i, :, :].rearrange("p a b -> p (a b)"), wg[:, k, n * P:(n + 1) * P],
                                       yT[:, k, h * NC:(h + 1) * NC], start=k == 0, stop=k == 3)
                    mm.then_inc(glu, 1)

            @block.vector
            def _(dve):
                for n in range(8):
                    dve.wait_ge(y_sum, n + 1)
                    h = 2 * P // 2
                    yv = uc[:, :, (n // 2) * h:(n // 2 + 1) * h].rearrange("c s (j a q) -> c a j s q", a=2, q=S_CH)[:, n % 2]
                    dve.tensor_tensor(yv, acc[:, n, :, :].rearrange("c g (s q) -> c g s q", q=S_CH), yv,
                                      ALU.add).then_inc(y_add, 1)
                for s in range(S_T):
                    dve.wait_ge(y_tr, s + 1)
                    dve.tensor_copy(yT[:, :, :].rearrange("p f (c s) -> p f c s", s=S_T)[:, :, :, s],
                                    acc[:, s, :, :]).then_inc(y_mv, 1)
                for i in range(8):
                    n, h = i // 2, i % 2
                    dve.wait_ge(sigd, i + 1)
                    dve.wait_ge(glu, 8)
                    yv = yT[:, n, h * NC:(h + 1) * NC]
                    dve.tensor_tensor(yv, yv, sig[:, i % 2, :], ALU.mult).then_inc(gated, 1)

            @block.scalar
            def _(act):
                act.wait_ge(y_add, 8)
                for s in range(S_T):
                    act.activation(uc[:, s, :], uc[:, s, :], ACT.Gelu_apprx_tanh).then_inc(y_act, 1)
                act.wait_ge(glu_ld, 2 * DMA)
                for i in range(8):
                    act.wait_ge(glu, i + 1)
                    if i >= 2:
                        act.wait_ge(gated, i - 1)
                    act.activation(sig[:, i % 2, :], acc[:, i, :, :].rearrange("p a b -> p (a b)"), ACT.Sigmoid,
                                   bias=bg[:, i // 2:i // 2 + 1]).then_inc(sigd, 1)

            @block.gpsimd
            def _(pool):
                for i in range(8):
                    n, h = i // 2, i % 2
                    pool.wait_ge(gated, i + 1)
                    pool.dma_start(outT[n * P:(n + 1) * P, h * NC:(h + 1) * NC],
                                   yT[:, n, h * NC:(h + 1) * NC]).then_inc(out_st, DMA)
                pool.wait_ge(out_st, 8 * DMA)


A_H, A_D = 8, 64
I_H = 4
TOPK = 256
Q0, K0, V0, QI0, KI0, WI0 = 512, 1024, 1088, 1152, 1408, 1472
GONE = -3e38
UNSEEN = -1e37


def mask_at(qb):
    return P * (qb * (qb + 1) // 2)


def sparse_prepare(nc, tag, p1, gains, F, V, wi, ident):
    R = WI0 + I_H - Q0
    NH = A_H + 2
    with Place(nc, tag) as pl:
        row = pl.sb("row", [P, 2, R])
        xs = pl.sb("xs", [P, 2, 8, P])
        sq = pl.sb("sq", [P, 2, NH, A_D])
        st = pl.sb("st", [P, 2, 4, NH])
        gc = pl.sb("gc", [P, 8])
        pT = pl.ps("pT", [P, 2, 8, P])
        ld = [pl.sem(f"rows_loaded{s}") for s in range(2)]
        g_ld = pl.sem("gains_loaded")
        ones = pl.sem("ones_ready")
        squared = pl.sem("squared")
        mean = pl.sem("mean_ready")
        root = pl.sem("root_ready")
        copied = pl.sem("raw_columns_copied")
        inv = pl.sem("inverse_ready")
        scaled = pl.sem("rows_scaled")
        turned = pl.sem("rows_transposed")
        stored = pl.sem("features_stored")
        chain = pl.sem("dve")
        with nc.Block() as block:
            @block.sync
            def _(sp):
                sp.wait_ge(ones, 1)
                for c0, n, g in ((0, 4, gains[0]), (4, 1, gains[1]), (7, 1, gains[2])):
                    for q in range(2):
                        for c in range(c0, c0 + n):
                            sp.dma_start(gc[q * A_D:(q + 1) * A_D, c:c + 1], g.rearrange("(d o) -> d o", o=1),
                                         allow_slow_non_contiguous=True).then_inc(g_ld, DMA)

                def body(t, s, r):
                    sp.wait_ge(scaled, t + 1)
                    sp.dma_start(row[:, s, :], p1[bass.ds(t * P, P), Q0:Q0 + R]).then_inc(ld[s], DMA)
                pairs(sp, TT, body)

            @block.gpsimd
            def _(pool):
                pool.memset(gc[:, :], 1.0).then_inc(ones, 1)

                def body(t, s, r):
                    pool.wait_ge(ld[s], (r + 1) * DMA)
                    pool.wait_ge(mean, t + 1)
                    for q0, n, c in ((0, A_H, 0), (A_H, 1, K0 - Q0), (A_H + 1, 1, KI0 - Q0)):
                        v = row[:, s, c:c + n * A_D].rearrange("p (h d) -> p h d", d=A_D)
                        last = pool.tensor_tensor(sq[:, s, q0:q0 + n, :], v, v, ALU.mult)
                    last.then_inc(squared, 1)
                pairs(pool, TT, body)

            @block.scalar
            def _(act):
                def body(t, s, r):
                    act.wait_ge(ld[s], (r + 1) * DMA)
                    act.wait_ge(turned, t + 1)
                    act.activation(xs[:, s, 5:7, :], row[:, s, QI0 - Q0:KI0 - Q0].rearrange("p (a b) -> p a b", b=P),
                                   ACT.Copy)
                    act.activation(V[:, bass.ds(t, 1), :], row[:, s, V0 - Q0:QI0 - Q0].unsqueeze(1), ACT.Copy)
                    act.activation(wi[:, bass.ds(t, 1), :], row[:, s, WI0 - Q0:R].unsqueeze(1), ACT.Copy,
                                   scale=I_H ** -0.5 * A_D ** -0.5).then_inc(copied, 1)
                    act.wait_ge(mean, t + 3)
                    act.activation(st[:, s, 2, :], st[:, s, 1, :], ACT.Sqrt).then_inc(root, 1)
                pairs(act, TT, body)

            @block.vector
            def _(dve):
                dve.sem_inc(scaled, 2)
                dve.sem_inc(stored, 2)
                dve.sem_inc(mean, 2)
                dve.wait_ge(g_ld, 12 * DMA)
                link = Link(dve, chain)

                def body(t, s, r):
                    if s == 0:
                        link.turn(r, 2)
                    dve.wait_ge(squared, t + 1)
                    link(dve.tensor_reduce(st[:, s, 0, :], sq[:, s, :, :], AX.X, ALU.add))
                    dve.tensor_scalar(st[:, s, 1, :], st[:, s, 0, :], 1.0 / A_D, EPS, ALU.mult, ALU.add).then_inc(mean, 1)
                    dve.wait_ge(root, t + 1)
                    dve.reciprocal(st[:, s, 3, :], st[:, s, 2, :]).then_inc(inv, 1)
                    dve.wait_ge(inv, t + 1)
                    dve.wait_ge(turned, t + 1)
                    dve.wait_ge(copied, t + 1)
                    for q0, n, c, o in ((0, A_H, 0, 0), (A_H, 1, K0 - Q0, 4), (A_H, 1, K0 - Q0, 4.5),
                                        (A_H + 1, 1, KI0 - Q0, 7), (A_H + 1, 1, KI0 - Q0, 7.5)):
                        dst = xs[:, s, :, :].rearrange("p a b -> p (a b)")[:, int(o * P):int(o * P) + n * A_D]
                        last = dve.tensor_tensor(dst.rearrange("p (h d) -> p h d", d=A_D),
                                                 row[:, s, c:c + n * A_D].rearrange("p (h d) -> p h d", d=A_D),
                                                 st[:, s, 3, q0:q0 + n].unsqueeze(2).to_broadcast([P, n, A_D]), ALU.mult)
                    last.then_inc(scaled, 1)
                    dve.wait_ge(turned, t + 3)
                    dve.tensor_tensor(F[:, :, bass.ds(t * P, P)], pT[:, s, :, :],
                                      gc[:, :].unsqueeze(2).to_broadcast([P, 8, P]), ALU.mult).then_inc(stored, 1)
                    if s == 1:
                        link.end(TT // 2)
                pairs(dve, TT, body)

            @block.tensor
            def _(pe):
                pe.sem_inc(turned, 2)

                def body(t, s, r):
                    pe.wait_ge(scaled, t + 3)
                    pe.wait_ge(stored, t + 1)
                    for k in range(8):
                        last = pe.transpose(pT[:, s, k, :], xs[:, s, k, :], ident[:, :])
                    last.then_inc(turned, 1)
                pairs(pe, TT, body)


def sparse_masks(nc, tag, F, wi, M):
    FIRST = TOPK // P
    with Place(nc, tag) as pl:
        rel = pl.sb("rel", [P, 2, L])
        score = pl.sb("score", [P, 2, L])
        work = pl.sb("work", [P, L])
        top = pl.sb("top", [P, 8])
        acc = pl.ps("acc", [P, 2, 2, NC])
        ready = pl.sem("product_ready")
        relu = pl.sem("relu_done")
        used = pl.sem("relu_used")
        scored = pl.sem("block_scored")
        hid = pl.sem("unseen_hidden")
        found = pl.sem("block_masked")
        chain = pl.sem("dve")
        passed = pl.sem("passed")
        zeroed = pl.sem("zeroed")
        causal = pl.sem("causal_made")
        blocks = list(range(FIRST, TT))
        with nc.Block() as block:
            @block.tensor
            def _(pe):
                i = 0
                for qb in blocks:
                    for h in range(I_H):
                        rows, s = slice((h % 2) * A_D, (h % 2 + 1) * A_D), h % 2
                        if i >= 2:
                            pe.wait_ge(relu, i - 1)
                        for c in range(0, (qb + 1) * P, NC):
                            n = min(NC, (qb + 1) * P - c)
                            mm = pe.matmul(acc[:, s, c // NC, 0:n], F[rows, 5 + h // 2, qb * P:(qb + 1) * P],
                                           F[rows, 7, c:c + n], start=True, stop=True)
                        mm.then_inc(ready, 1)
                        i += 1

            @block.scalar
            def _(act):
                i = 0
                for qb in blocks:
                    w = (qb + 1) * P
                    for h in range(I_H):
                        act.wait_ge(ready, i + 1)
                        if i >= 2:
                            act.wait_ge(used, i - 1)
                        act.activation(rel[:, h % 2, 0:w], acc[:, h % 2, :, :].rearrange("p a b -> p (a b)")[:, 0:w],
                                       ACT.Relu).then_inc(relu, 1)
                        i += 1

            @block.vector
            def _(dve):
                link = Link(dve, chain)

                def score_block(b):
                    qb = blocks[b]
                    w = (qb + 1) * P
                    for h in range(I_H):
                        dve.wait_ge(relu, b * I_H + h + 1)
                        out, one = score[:, b % 2, 0:w], wi[:, qb, h:h + 1]
                        if h == 0:
                            ins = dve.tensor_scalar(out, rel[:, 0, 0:w], one, None, ALU.mult)
                        else:
                            dve.wait_ge(used, b * I_H + h)
                            ins = dve.scalar_tensor_tensor(out, rel[:, h % 2, 0:w], one, out, ALU.mult, ALU.add)
                        ins.then_inc(used, 1)
                    dve.wait_ge(used, (b + 1) * I_H)
                    dve.sem_inc(scored, 1)

                score_block(0)
                for b, qb in enumerate(blocks):
                    w = (qb + 1) * P
                    if b + 1 < len(blocks):
                        score_block(b + 1)
                    dve.wait_ge(hid, b + 1)
                    sc, wk = score[:, b % 2, 0:w], work[:, 0:w]
                    link(dve.max(top[:, :], sc))
                    link(dve.match_replace(wk, top[:, :], sc, GONE))
                    turns = TOPK // 8 - 1
                    with dve.Fori(0, turns) as r:
                        link.turn(r, 2)
                        link(dve.max(top[:, :], wk))
                        dve.sem_inc(passed, 1)
                        link(dve.match_replace(wk, top[:, :], wk, GONE))
                    link.end(turns)
                    m = M[:, mask_at(qb):mask_at(qb) + w]
                    link(dve.tensor_tensor(m, wk, sc, ALU.is_equal))
                    dve.tensor_scalar(m, m, -HUGE, None, ALU.mult).then_inc(found, 1)

            @block.gpsimd
            def _(pool):
                n = mask_at(FIRST)
                pool.memset(M[:, 0:n], 0.0).then_inc(zeroed, 1)
                pool.wait_ge(zeroed, 1)
                for qb in range(FIRST):
                    m = M[:, mask_at(qb) + qb * P:mask_at(qb) + (qb + 1) * P]
                    pool.affine_select(out=m, in_=m, compare_op=ALU.is_ge, fill=-HUGE, base=0, pattern=[[-1, P]],
                                       channel_multiplier=1).then_inc(causal, 1)
                for b, qb in enumerate(blocks):
                    pool.wait_ge(scored, b + 1)
                    d = score[:, b % 2, qb * P:(qb + 1) * P]
                    pool.affine_select(out=d, in_=d, compare_op=ALU.is_ge, fill=UNSEEN, base=0, pattern=[[-1, P]],
                                       channel_multiplier=1).then_inc(hid, 1)
                pool.wait_ge(causal, FIRST)


def sparse_attend(nc, tag, F, V, M, ident, yT):
    PAIRS = A_H // 2
    N = 2 * TT
    with Place(nc, tag) as pl:
        qs = pl.sb("qs", [P, L])
        S = pl.sb("S", [P, 2, L])
        E = pl.sb("E", [P, 2, L])
        ET = pl.sb("ET", [P, 2, TT, P])
        mx = pl.sb("mx", [P, 2, 4])
        o = pl.sb("o", [P, 2, P])
        yo = pl.sb("yo", [P, L])
        pS = pl.ps("pS", [P, 2, 2, NC])
        pE = pl.ps("pE", [P, 2, 4, P])
        pO = pl.ps("pO", [P, 2, NC])
        q_in = pl.sem("queries_staged")
        passed = pl.sem("passed")
        dots = pl.sem("logits_ready")
        masked = pl.sem("logits_masked")
        neg = pl.sem("negated")
        expd = pl.sem("exp_done")
        turned = pl.sem("exp_transposed")
        moved = pl.sem("exp_moved")
        summed = pl.sem("values_summed")
        inv = pl.sem("inverse_ready")
        normed = pl.sem("output_normed")
        o_tr = pl.sem("output_transposed")
        o_mv = pl.sem("output_moved")
        yo_free = pl.sem("yo_free")
        out_st = pl.store_sem("out_stored")
        with nc.Block() as block:
            @block.gpsimd
            def _(pool):
                pool.sem_inc(yo_free, 1)
                with pool.Fori(0, PAIRS) as hp:
                    pool.wait_ge(dots, (hp + 1) * N)
                    pool.tensor_copy(qs[:, :].unsqueeze(1), F[:, bass.ds(hp, 1), :]).then_inc(q_in, 1)
                    pool.wait_ge(o_mv, (hp + 1) * TT)
                    pool.dma_start(yT[bass.ds(hp * P, P), :], yo[:, :]).then_inc(out_st, DMA)
                    pool.wait_ge(out_st, (hp + 1) * DMA)
                    pool.sem_inc(yo_free, 1)

            @block.tensor
            def _(pe):
                pe.sem_inc(dots, N)
                pe.sem_inc(turned, 2)
                pe.sem_inc(summed, 2)
                pe.sem_inc(o_tr, 2)
                with pe.Fori(0, PAIRS) as hp:
                    def logits(i):
                        n, qb, a = hp * N + i, i // 2, i % 2
                        rows = slice(a * A_D, (a + 1) * A_D)
                        pe.wait_ge(masked, n + 1)
                        for c in range(0, (qb + 1) * P, NC):
                            k = min(NC, (qb + 1) * P - c)
                            mm = pe.matmul(pS[:, a, c // NC, 0:k], qs[rows, qb * P:(qb + 1) * P], F[rows, 4, c:c + k],
                                           start=True, stop=True)
                        mm.then_inc(dots, 1)

                    def output(i):
                        n, qb, a = hp * N + i, i // 2, i % 2
                        pe.wait_ge(expd, n + 3)
                        pe.wait_ge(moved, n + 1)
                        for c in range(qb + 1):
                            mm = pe.transpose(pE[:, c // 4, c % 4, :], E[:, a, c * P:(c + 1) * P], ident[:, :])
                        mm.then_inc(turned, 1)
                        pe.wait_ge(moved, n + 2)
                        pe.wait_ge(normed, n + 1)
                        for c in range(qb + 1):
                            mm = pe.matmul(pO[:, a, 0:A_D], ET[:, a, c, :], V[:, c, :], start=c == 0, stop=c == qb)
                        mm.then_inc(summed, 1)

                    def turn_output(qb):
                        m = hp * TT + qb
                        pe.wait_ge(normed, hp * N + 2 * qb + 4)
                        pe.transpose(pO[:, 1, P:2 * P], o[:, qb % 2, :], ident[:, :]).then_inc(o_tr, 1)

                    pe.wait_ge(q_in, hp + 1)
                    logits(0)
                    for i in range(N):
                        if i + 1 < N:
                            logits(i + 1)
                        output(i)
                        if i % 2 == 1:
                            turn_output(i // 2)

            @block.vector
            def _(dve):
                dve.sem_inc(masked, 2)
                dve.sem_inc(normed, 2)
                dve.sem_inc(moved, 1)
                with dve.Fori(0, PAIRS) as hp:
                    def mask(i):
                        n, qb, a = hp * N + i, i // 2, i % 2
                        w = (qb + 1) * P
                        dve.wait_ge(dots, n + 1 + N)
                        dve.wait_ge(expd, n + 1)
                        dve.sem_inc(passed, 1)
                        dve.tensor_tensor_reduce(S[:, a, 0:w], pS[:, a, :, :].rearrange("p a b -> p (a b)")[:, 0:w],
                                                 M[:, mask_at(qb):mask_at(qb) + w], A_D ** -0.5, GONE, ALU.add, ALU.max,
                                                 mx[:, a, 0:1]).then_inc(masked, 1)
                        dve.wait_ge(masked, n + 3)
                        dve.tensor_scalar(mx[:, a, 1:2], mx[:, a, 0:1], -1.0, None, ALU.mult).then_inc(neg, 1)

                    def finish(i):
                        n, qb, a = hp * N + i, i // 2, i % 2
                        dve.wait_ge(turned, n + 3)
                        dve.tensor_copy(ET[:, a, 0:qb + 1, :], pE[:, :, :, :].rearrange("p a b c -> p (a b) c")[:, 0:qb + 1, :]
                                        ).then_inc(moved, 1)
                        dve.reciprocal(mx[:, a, 3:4], mx[:, a, 2:3]).then_inc(inv, 1)
                        dve.wait_ge(inv, n + 1)
                        dve.wait_ge(summed, n + 3)
                        dve.wait_ge(o_tr, hp * TT + qb + 1)
                        dve.tensor_scalar(o[:, qb % 2, a * A_D:(a + 1) * A_D], pO[:, a, 0:A_D], mx[:, a, 3:4], None,
                                          ALU.mult).then_inc(normed, 1)
                        if a == 1:
                            dve.wait_ge(o_tr, hp * TT + qb + 3)
                            if qb == 0:
                                dve.wait_ge(yo_free, hp + 1)
                            dve.tensor_copy(yo[:, qb * P:(qb + 1) * P], pO[:, 1, P:2 * P]).then_inc(o_mv, 1)

                    mask(0)
                    for i in range(N):
                        if i + 1 < N:
                            mask(i + 1)
                        finish(i)

            @block.scalar
            def _(act):
                act.sem_inc(expd, 2)
                with act.Fori(0, PAIRS) as hp:
                    for i in range(N):
                        n, qb, a = hp * N + i, i // 2, i % 2
                        w = (qb + 1) * P
                        act.wait_ge(neg, n + 1)
                        act.wait_ge(turned, n + 1)
                        act.wait_ge(normed, n + 1)
                        act.activation(E[:, a, 0:w], S[:, a, 0:w], ACT.Exp, bias=mx[:, a, 1:2],
                                       accum_out=mx[:, a, 2:3]).then_inc(expd, 1)


CONV = 4
H2, P2, G2, N2 = 16, 64, 4, 128
X2 = H2 * P2
XB2 = X2 + G2 * N2


def conv_silu(nc, tag, tile0, tiles, xbcT, cw, cb, ident, featT, tok):
    with Place(nc, tag) as pl:
        x = pl.sb("x", [P, 2, CONV - 1 + L])
        y = pl.sb("y", [P, 2, L])
        f = pl.sb("f", [P, 2, L])
        t = pl.sb("t", [P, 2, TT, P])
        w = pl.sb("w", [P, tiles, CONV])
        b = pl.sb("b", [P, tiles])
        pT = pl.ps("pT", [P, 2, TT, P])
        w_ld = pl.sem("weights_loaded")
        ld = [pl.sem(f"x_loaded{s}") for s in range(2)]
        conved = pl.sem("conv_done")
        chain = pl.sem("dve")
        pad = pl.sem("padded")
        act_d = pl.sem("silu_done")
        turned = pl.sem("transposed")
        moved = pl.sem("moved")
        out_st = pl.store_sem("out_stored")
        free = pl.sem("outputs_free")
        copies = 1 + (featT is not None)
        with nc.Block() as block:
            @block.sync
            def _(sp):
                rows = slice(tile0 * P, (tile0 + tiles) * P)
                for k in range(CONV):
                    sp.dma_start(w[:, :, k], cw[k, rows].rearrange("(c p) -> p c", p=P),
                                 allow_slow_non_contiguous=True).then_inc(w_ld, DMA)
                sp.dma_start(b[:, :], cb[rows].rearrange("(c p) -> p c", p=P),
                             allow_slow_non_contiguous=True).then_inc(w_ld, DMA)

                def body(c, s, r):
                    sp.wait_ge(conved, c + 1)
                    sp.dma_start(x[:, s, CONV - 1:], xbcT[bass.ds((tile0 + c) * P, P), :]).then_inc(ld[s], DMA)
                pairs(sp, tiles, body)

            @block.vector
            def _(dve):
                dve.sem_inc(conved, 2)
                dve.memset(x[:, :, 0:CONV - 1], 0.0).then_inc(pad, 1)
                dve.wait_ge(pad, 1)
                dve.wait_ge(w_ld, (CONV + 1) * DMA)
                link = Link(dve, chain)

                def body(c, s, r):
                    if s == 0:
                        link.turn(r, 2 * (CONV - 1))
                    dve.wait_ge(ld[s], (r + 1) * DMA)
                    dve.wait_ge(act_d, c + 1)
                    link(dve.tensor_scalar(y[:, s, :], x[:, s, 0:L], w[:, bass.ds(c, 1), 0], b[:, bass.ds(c, 1)],
                                           ALU.mult, ALU.add))
                    for k in range(1, CONV):
                        ins = dve.scalar_tensor_tensor(y[:, s, :], x[:, s, k:k + L], w[:, bass.ds(c, 1), k], y[:, s, :],
                                                       ALU.mult, ALU.add)
                        if k < CONV - 1:
                            link(ins)
                        else:
                            ins.then_inc(conved, 1)
                    if s == 1:
                        link.end(tiles // 2)
                pairs(dve, tiles, body)

            @block.scalar
            def _(act):
                act.sem_inc(act_d, 2)
                act.sem_inc(moved, 2)

                def body(c, s, r):
                    act.wait_ge(conved, c + 3)
                    act.wait_ge(turned, c + 1)
                    act.wait_ge(free, c + 1)
                    act.activation(f[:, s, :], y[:, s, :], ACT.Silu).then_inc(act_d, 1)
                    act.wait_ge(turned, c + 3)
                    act.activation(t[:, s, :, :], pT[:, s, :, :], ACT.Copy).then_inc(moved, 1)
                pairs(act, tiles, body)

            @block.tensor
            def _(pe):
                pe.sem_inc(turned, 2)

                def body(c, s, r):
                    pe.wait_ge(act_d, c + 3)
                    pe.wait_ge(moved, c + 1)
                    for k in range(TT):
                        mm = pe.transpose(pT[:, s, k, :], f[:, s, k * P:(k + 1) * P], ident[:, :])
                    mm.then_inc(turned, 1)
                pairs(pe, tiles, body)

            @block.gpsimd
            def _(pool):
                pool.sem_inc(free, 2)

                def body(c, s, r):
                    if featT is not None:
                        pool.wait_ge(act_d, c + 3)
                        pool.dma_start(featT[bass.ds(c * P, P), :], f[:, s, :]).then_inc(out_st, DMA)
                    pool.wait_ge(moved, c + 3)
                    pool.dma_start(tok[:, bass.ds((tile0 + c) * P, P)].rearrange("(k p) n -> p k n", p=P),
                                   t[:, s, :, :]).then_inc(out_st, DMA)
                    pool.wait_ge(out_st, (c + 1) * copies * DMA)
                    pool.sem_inc(free, 1)
                pairs(pool, tiles, body)


def ssd_mixer(nc, tag, dt, xbt, bcT, z, prm, ident, yT):
    NCH = TT
    KINDS = 6
    DT, EA, DS, EL, NA, A0 = range(KINDS)
    with Place(nc, tag) as pl:
        tri = pl.sb("tri", [P, P])
        neg = pl.sb("neg", [P, P])
        ones = pl.sb("ones", [P, P])
        pr = pl.sb("pr", [P, KINDS, NCH, H2])
        v = pl.sb("v", [P, 3, NCH, H2])
        hd = pl.sb("hd", [P, 4, H2])
        nw = pl.sb("nw", [P, KD])
        ps0 = pl.ps("ps0", [P, 2, NCH * H2])
        loaded = pl.sem("loaded")
        made = pl.sem("masks_made")
        s_act = pl.sem("act")
        chain = pl.sem("dve")
        sums = pl.sem("sums")
        a_in = pl.sem("a_ready")
        pre = pl.sem("argument_ready")
        post = pl.sem("exponentials_ready")
        v2 = [v[:, i, :, :].rearrange("p c h -> p (c h)") for i in range(3)]
        p2 = [pr[:, i, :, :].rearrange("p c h -> p (c h)") for i in range(KINDS)]
        with nc.Block() as block:
            @block.sync
            def _(sp):
                sp.dma_start(pr[:, DT, :, :], dt.rearrange("(c p) h -> p c h", p=P)).then_inc(loaded, DMA)
                for i, n in ((0, "dt_bias"), (1, "A_log"), (3, "D")):
                    sp.dma_start(hd[:, i, :], prm[n].partition_broadcast(P)).then_inc(loaded, DMA)
                sp.dma_start(nw[:, :], prm["norm_w"].rearrange("(k p) -> p k", p=P),
                             allow_slow_non_contiguous=True).then_inc(loaded, DMA)
                sp.wait_ge(loaded, 5 * DMA)

            @block.gpsimd
            def _(pool):
                pool.memset(tri[:, :], 1.0).then_inc(made, 1)
                pool.memset(neg[:, :], 0.0).then_inc(made, 1)
                pool.memset(ones[:, :], 1.0).then_inc(made, 1)
                pool.wait_ge(made, 3)
                for t, fill in ((tri, 0.0), (neg, -HUGE)):
                    pool.affine_select(out=t[:, :], in_=t[:, :], compare_op=ALU.is_ge, fill=fill, base=0,
                                       pattern=[[1, P]], channel_multiplier=-1).then_inc(made, 1)
                pool.wait_ge(made, 5)

            @block.vector
            def _(dve):
                link = Link(dve, chain)
                dve.wait_ge(loaded, 5 * DMA)
                link(dve.tensor_tensor(v[:, 0, :, :], pr[:, DT, :, :], hd[:, 0, :].unsqueeze(1).to_broadcast([P, NCH, H2]),
                                       ALU.add))
                link(dve.scalar_tensor_tensor(v2[1], v2[0], -1.0, v2[0], ALU.mult, ALU.max))
                dve.tensor_scalar(v2[2], v2[0], 0.0, None, ALU.max).then_inc(pre, 1)
                dve.wait_ge(post, 3)
                link(dve.tensor_tensor(p2[DT], v2[0], v2[2], ALU.add))
                link(dve.tensor_scalar(hd[:, 2, :], hd[:, 2, :], -1.0, None, ALU.mult))
                dve.tensor_tensor(pr[:, A0, :, :], pr[:, DT, :, :], hd[:, 2, :].unsqueeze(1).to_broadcast([P, NCH, H2]),
                                  ALU.mult).then_inc(a_in, 1)
                dve.wait_ge(sums, 2)
                dve.wait_ge(post, 5)
                link(dve.tensor_scalar(p2[NA], v2[0], -1.0, None, ALU.mult))
                dve.tensor_tensor(v2[2], v2[1], v2[0], ALU.subtract).then_inc(pre, 1)

            @block.scalar
            def _(act):
                act.wait_ge(loaded, 5 * DMA)
                act.activation(hd[:, 2, :], hd[:, 1, :], ACT.Exp).then_inc(post, 1)
                act.wait_ge(pre, 1)
                act.activation(v2[1], v2[1], ACT.Exp, scale=-1.0).then_inc(post, 1)
                act.wait_ge(post, 2)
                act.activation(v2[0], v2[1], ACT.Ln, bias=1.0).then_inc(post, 1)
                act.wait_ge(sums, 2)
                act.activation(v2[0], ps0[:, 0, :], ACT.Copy).then_inc(post, 1)
                act.activation(v2[1], ps0[:, 1, :], ACT.Copy).then_inc(post, 1)
                act.activation(p2[EA], ps0[:, 0, :], ACT.Exp)
                act.activation(p2[EL], ps0[:, 1, :], ACT.Exp)
                act.wait_ge(pre, 2)
                act.activation(p2[DS], v2[2], ACT.Exp).then_inc(s_act, 1)
                act.wait_ge(s_act, 1)

            @block.tensor
            def _(pe):
                pe.wait_ge(made, 5)
                pe.wait_ge(a_in, 1)
                pe.matmul(ps0[:, 0, :], tri[:, :], p2[A0], start=True, stop=True, skip_group_check=True).then_inc(sums, 1)
                pe.matmul(ps0[:, 1, :], ones[:, :], p2[A0], start=True, stop=True, skip_group_check=True).then_inc(sums, 1)

        X = pl.sb("X", [P, 2, X2 + G2 * N2])
        BC = pl.sb("BC", [P, 2, 2 * G2, P])
        Z = pl.sb("Z", [P, 2, X2])
        cp = pl.sb("cp", [P, 2, KINDS, H2])
        TA = pl.sb("TA", [P, H2, P])
        R = pl.sb("R", [P, 2, 4, P])
        LT = pl.sb("LT", [P, 2, 4, P])
        SC = pl.sb("SC", [P, H2, P])
        Xd = pl.sb("Xd", [P, X2])
        Xs = pl.sb("Xs", [P, X2])
        XD = pl.sb("XD", [P, X2])
        Y = pl.sb("Y", [P, X2])
        SQ = pl.sb("SQ", [P, X2])
        ST = pl.sb("ST", [P, X2])
        YT = pl.sb("YT", [P, KD, P])
        sm = pl.sb("sm", [P, 4])
        pCB = pl.ps("pCB", [P, G2, P])
        pR = pl.ps("pR", [P, 2, 4, P])
        pYd = pl.ps("pYd", [P, H2, P2])
        pYo = pl.ps("pYo", [P, X2])
        ld = [pl.sem(f"chunk_loaded{s}") for s in range(2)]
        cop = pl.sem("values_copied")
        ta = pl.sem("triangle_ready")
        xd = pl.sem("dt_x_ready")
        xs = pl.sem("decayed_x_ready")
        y1 = pl.sem("skip_added")
        cbS = pl.sem("CB_ready")
        rS = pl.sem("sums_ready")
        msk = pl.sem("sums_masked")
        lt = pl.sem("decay_ready")
        sc = pl.sem("scores_ready")
        yo = pl.sem("off_diagonal_ready")
        yd = pl.sem("diagonal_ready")
        yt = pl.sem("outputs_added")
        ns = pl.sem("new_state_ready")
        stt = pl.sem("state_ready")
        y2 = pl.sem("gated")
        sq = pl.sem("squares_summed")
        mn = pl.sem("mean_ready")
        rt = pl.sem("root_ready")
        iv = pl.sem("inverse_ready")
        yn = pl.sem("normed")
        tr = pl.sem("transposed")
        ev = pl.sem("features_moved")
        out_st = pl.store_sem("out_stored")
        yt_free = pl.sem("YT_free")
        chain2 = pl.sem("dve2")

        def bc64(a):
            return a.unsqueeze(2).to_broadcast([P, H2, P2])

        def heads(a):
            return a.rearrange("p (h q) -> p h q", q=P2)
        with nc.Block() as block:
            @block.sync
            def _(sp):
                def body(c, s, r):
                    sp.wait_ge(tr, 2 * c + 2)
                    sp.dma_start(X[:, s, :], xbt[bass.ds(c * P, P), 0:XB2]).then_inc(ld[s], DMA)
                    sp.dma_start(BC[:, s, :, :], bcT[:, bass.ds(c * P, P)].rearrange("(g n) l -> n g l", n=P)
                                 ).then_inc(ld[s], DMA)
                    sp.dma_start(Z[:, s, :], z[bass.ds(c * P, P), :]).then_inc(ld[s], DMA)
                pairs(sp, NCH, body)

            @block.gpsimd
            def _(pool):
                pool.sem_inc(yt_free, 1)

                def body(c, s, r):
                    pool.wait_ge(tr, 2 * c + 2)
                    pool.tensor_copy(cp[:, s, :, :].unsqueeze(2), pr[:, :, bass.ds(c, 1), :]).then_inc(cop, 1)
                    pool.wait_ge(cop, c + 1)
                    if s == 1:
                        pool.wait_ge(rS, 4 * c)
                    else:
                        pool.wait_ge(yt, c + 1)
                    pool.tensor_tensor(TA[:, :, :], tri[:, :].unsqueeze(1).to_broadcast([P, H2, P]),
                                       cp[:, s, A0, :].unsqueeze(2).to_broadcast([P, H2, P]), ALU.mult).then_inc(ta, 1)
                    pool.wait_ge(ld[s], (r + 1) * 3 * DMA)
                    pool.wait_ge(yd, c + 1)
                    pool.tensor_tensor(heads(Xd[:, :]), heads(X[:, s, 0:X2]), bc64(cp[:, s, DT, :]), ALU.mult).then_inc(xd, 1)
                    pool.wait_ge(xd, c + 1)
                    pool.wait_ge(ns, c + 1)
                    pool.tensor_tensor(heads(Xs[:, :]), heads(Xd[:, :]), bc64(cp[:, s, DS, :]), ALU.mult).then_inc(xs, 1)
                    pool.tensor_tensor(heads(XD[:, :]), heads(X[:, s, 0:X2]), bc64(hd[:, 3, :]), ALU.mult).then_inc(xs, 1)
                    pool.wait_ge(xs, 2 * c + 2)
                    pool.wait_ge(yt, c + 2)
                    pool.tensor_tensor(Y[:, :], Y[:, :], XD[:, :], ALU.add).then_inc(y1, 1)
                    pool.wait_ge(ev, 2 * c + 2)
                    pool.dma_start(yT[:, bass.ds(c * P, P)].rearrange("(k p) l -> p k l", p=P), YT[:, :, :]
                                   ).then_inc(out_st, DMA)
                    pool.wait_ge(out_st, (c + 1) * DMA)
                    pool.sem_inc(yt_free, 1)
                pairs(pool, NCH, body)

            @block.tensor
            def _(pe):
                pe.sem_inc(yd, 1)
                pe.sem_inc(ns, 1)
                pe.sem_inc(tr, 4)

                def body(c, s, r):
                    pe.wait_ge(ld[s], (r + 1) * 3 * DMA)
                    pe.wait_ge(yt, c + 1)
                    for g in range(G2):
                        mm = pe.matmul(pCB[:, g, :], BC[:, s, g, :], BC[:, s, G2 + g, :], start=True, stop=True,
                                       skip_group_check=True)
                    mm.then_inc(cbS, 1)
                    pe.wait_ge(ta, c + 1)
                    for i in range(G2):
                        pe.wait_ge(msk, 4 * c + i + 1)
                        pe.matmul(pR[:, i % 2, :, :], ones[:, :], TA[:, 4 * i:4 * i + 4, :], start=True,
                                  stop=True).then_inc(rS, 1)
                    pe.wait_ge(stt, c + 1)
                    for g in range(G2):
                        mm = pe.matmul(pYo[:, g * 256:(g + 1) * 256], BC[:, s, G2 + g, :], ST[:, g * 256:(g + 1) * 256],
                                       start=True, stop=True, skip_group_check=True)
                    mm.then_inc(yo, 1)
                    pe.wait_ge(xd, c + 1)
                    for h in range(H2):
                        if h % 4 == 0:
                            pe.wait_ge(sc, 4 * c + h // 4 + 3)
                        mm = pe.matmul(pYd[:, h, :], SC[:, h, :], Xd[:, h * P2:(h + 1) * P2], start=True, stop=True,
                                       skip_group_check=True)
                    mm.then_inc(yd, 1)
                    pe.wait_ge(xs, 2 * c + 2)
                    pe.wait_ge(yt, c + 2)
                    for g in range(G2):
                        mm = pe.matmul(pYo[:, g * 256:(g + 1) * 256], X[:, s, X2 + g * P:X2 + (g + 1) * P],
                                       Xs[:, g * 256:(g + 1) * 256], start=True, stop=True, skip_group_check=True)
                    mm.then_inc(ns, 1)
                    pe.wait_ge(yn, c + 1)
                    for h in range(2):
                        for k in range(4):
                            kk = 4 * h + k
                            mm = pe.transpose(pR[:, h, k, :], Y[:, kk * P:(kk + 1) * P], ident[:, :])
                        mm.then_inc(tr, 1)
                pairs(pe, NCH, body)

            @block.scalar
            def _(act):
                act.sem_inc(lt, 2)

                def body(c, s, r):
                    for i in range(G2):
                        act.wait_ge(msk, 4 * c + i + 3)
                        act.wait_ge(sc, 4 * c + i + 1)
                        for h in range(4):
                            e = act.activation(LT[:, i % 2, h, :], R[:, i % 2, h, :], ACT.Exp,
                                               bias=cp[:, s, NA, 4 * i + h:4 * i + h + 1])
                        e.then_inc(lt, 1)
                    act.wait_ge(y2, c + 1)
                    act.activation(SQ[:, :], Y[:, :], ACT.Square, accum_out=sm[:, 0:1]).then_inc(sq, 1)
                    act.wait_ge(mn, c + 1)
                    act.activation(sm[:, 2:3], sm[:, 1:2], ACT.Sqrt).then_inc(rt, 1)
                pairs(act, NCH, body)

            @block.vector
            def _(dve):
                dve.sem_inc(msk, 2)
                dve.sem_inc(sc, 2)
                dve.sem_inc(yt, 1)
                link = Link(dve, chain2)
                link(dve.memset(ST[:, :], 0.0))
                dve.sem_inc(stt, 1)

                def body(c, s, r):
                    if s == 0:
                        link.turn(r, 4)

                    def mask(i):
                        dve.wait_ge(rS, 4 * c + i + 1)
                        dve.wait_ge(lt, 4 * c + i + 1)
                        dve.tensor_tensor(R[:, i % 2, :, :], pR[:, i % 2, :, :],
                                          neg[:, :].unsqueeze(1).to_broadcast([P, 4, P]), ALU.add).then_inc(msk, 1)
                    mask(0)
                    dve.wait_ge(cbS, c + 1)
                    dve.wait_ge(yd, c + 1)
                    for i in range(G2):
                        if i + 1 < G2:
                            mask(i + 1)
                        dve.wait_ge(lt, 4 * c + i + 3)
                        dve.tensor_tensor(SC[:, 4 * i:4 * i + 4, :], LT[:, i % 2, :, :],
                                          pCB[:, i, :].unsqueeze(1).to_broadcast([P, 4, P]), ALU.mult).then_inc(sc, 1)
                    dve.wait_ge(yo, c + 1)
                    dve.wait_ge(tr, 2 * c + 4)
                    link(dve.tensor_tensor(heads(Y[:, :]), heads(pYo[:, :]), bc64(cp[:, s, EA, :]), ALU.mult))
                    dve.wait_ge(yd, c + 2)
                    dve.tensor_tensor(heads(Y[:, :]), heads(Y[:, :]), pYd[:, :, :], ALU.add).then_inc(yt, 1)
                    link(dve.tensor_tensor(heads(ST[:, :]), heads(ST[:, :]), bc64(cp[:, s, EL, :]), ALU.mult))
                    dve.wait_ge(y1, c + 1)
                    dve.tensor_tensor(Y[:, :], Y[:, :], Z[:, s, :], ALU.mult).then_inc(y2, 1)
                    dve.wait_ge(ns, c + 2)
                    dve.tensor_tensor(ST[:, :], ST[:, :], pYo[:, :], ALU.add).then_inc(stt, 1)
                    dve.wait_ge(sq, c + 1)
                    dve.tensor_scalar(sm[:, 1:2], sm[:, 0:1], 1.0 / X2, EPS, ALU.mult, ALU.add).then_inc(mn, 1)
                    dve.wait_ge(rt, c + 1)
                    dve.reciprocal(sm[:, 3:4], sm[:, 2:3]).then_inc(iv, 1)
                    dve.wait_ge(iv, c + 1)
                    dve.tensor_scalar(Y[:, :], Y[:, :], sm[:, 3:4], None, ALU.mult).then_inc(yn, 1)
                    dve.wait_ge(yt_free, c + 1)
                    for h in range(2):
                        dve.wait_ge(tr, 2 * c + h + 5)
                        dve.tensor_tensor(YT[:, 4 * h:4 * h + 4, :], pR[:, h, :, :],
                                          nw[:, 4 * h:4 * h + 4].unsqueeze(2).to_broadcast([P, 4, P]),
                                          ALU.mult).then_inc(ev, 1)
                    if s == 1:
                        link.end(NCH // 2)
                pairs(dve, NCH, body)


D_H, D_QK, D_V = 8, 64, 128
BUCKETS, MAX_DIST = 32, 128
LAM_INIT = 0.2
NEAR = 2 * P
SKEW = 3 * P


def bucket_one_hot():
    rel = 2 * P - 1 - np.arange(SKEW)
    n = np.maximum(rel, 0)
    exact = BUCKETS // 2
    large = exact + (np.log(np.maximum(n, 1).astype(np.float32) / exact) / np.log(MAX_DIST / exact)
                     * (BUCKETS - exact)).astype(np.int32)
    bucket = np.where(n < exact, n, np.minimum(large, BUCKETS - 1))
    bucket = np.where(rel < 0, BUCKETS, bucket)
    return (bucket[None, :] == np.arange(BUCKETS + 1)[:, None]).astype(np.float32)


def diff_bias(nc, tag, rel_bias, one_hot, skew, near, far, lam, lam_src):
    with Place(nc, tag) as pl:
        tab = pl.sb("tab", [BUCKETS + 1, D_H])
        wide = pl.sb("wide", [BUCKETS + 1, D_H, P])
        oh = pl.sb("oh", [BUCKETS + 1, SKEW])
        rows = pl.sb("rows", [P, D_H, SKEW])
        lv = pl.sb("lv", [P, 4, D_QK])
        lp = pl.sb("lp", [P, 2, D_QK])
        ls = pl.sb("ls", [P, 4])
        acc = pl.ps("acc", [P, 2, NC])
        loaded = pl.sem("loaded")
        hidden = pl.sem("last_row_set")
        chain = pl.sem("dve")
        wided = pl.sem("table_widened")
        ready = pl.sem("row_ready")
        moved = pl.sem("row_moved")
        skewed = pl.sem("rows_stored")
        near_ld = pl.sem("near_loaded")
        dot = pl.sem("dots_ready")
        expd = pl.sem("exps_ready")
        with nc.Block() as block:
            @block.sync
            def _(sp):
                sp.dma_start(tab[0:BUCKETS, :], rel_bias).then_inc(loaded, DMA)
                sp.dma_start(oh[:, :], one_hot).then_inc(loaded, DMA)
                for i, v in enumerate(lam_src):
                    sp.dma_start(lv[:, i, :], v.partition_broadcast(P)).then_inc(loaded, DMA)
                sp.wait_ge(moved, D_H)
                sp.dma_start(skew.rearrange("(p n) -> p n", p=P), rows[:, :, :].rearrange("p h m -> p (h m)")
                             ).then_inc(skewed, DMA)
                sp.wait_ge(skewed, DMA)
                n = D_H * SKEW - 1
                ahead = skew[P - 1:P - 1 + P * n].rearrange("(p n) -> p n", n=n)
                for h in range(D_H):
                    sp.dma_start(near[:, h, :], ahead[:, h * SKEW:h * SKEW + NEAR]).then_inc(near_ld, DMA)
                sp.wait_ge(near_ld, D_H * DMA)

            @block.vector
            def _(dve):
                link = Link(dve, chain)
                dve.memset(tab[BUCKETS:BUCKETS + 1, :], -HUGE).then_inc(hidden, 1)
                dve.wait_ge(loaded, 6 * DMA)
                dve.wait_ge(hidden, 1)
                link(dve.tensor_scalar(tab[0:BUCKETS, :], tab[0:BUCKETS, :], D_QK ** 0.5, None, ALU.mult))
                dve.tensor_copy(wide[:, :, :], tab[:, :].unsqueeze(2).to_broadcast([BUCKETS + 1, D_H, P])).then_inc(wided, 1)
                for i in range(2):
                    link(dve.tensor_tensor(lp[:, i, :], lv[:, 2 * i, :], lv[:, 2 * i + 1, :], ALU.mult))
                dve.tensor_reduce(ls[:, 0:2], lp[:, :, :], AX.X, ALU.add).then_inc(dot, 1)
                dve.wait_ge(expd, 1)
                link(dve.tensor_tensor(ls[:, 0:1], ls[:, 3:4], ls[:, 2:3], ALU.subtract))
                link(dve.tensor_scalar(lam[:, :], ls[:, 0:1], 1.0, -LAM_INIT, ALU.mult, ALU.add))
                dve.wait_ge(moved, D_H)
                link(dve.tensor_copy(far[:, :].unsqueeze(2), rows[:, :, 0:1]))

            @block.tensor
            def _(pe):
                pe.wait_ge(wided, 1)
                for h in range(D_H):
                    if h >= 2:
                        pe.wait_ge(moved, h - 1)
                    pe.matmul(acc[:, h % 2, 0:SKEW], wide[:, h, :], oh[:, :], start=True, stop=True).then_inc(ready, 1)

            @block.scalar
            def _(act):
                for h in range(D_H):
                    act.wait_ge(ready, h + 1)
                    act.activation(rows[:, h, :], acc[:, h % 2, 0:SKEW], ACT.Copy).then_inc(moved, 1)
                act.wait_ge(dot, 1)
                act.activation(ls[:, 2:4], ls[:, 0:2], ACT.Exp).then_inc(expd, 1)


def diff_attend(nc, tag, qkT, vg, near, far, lam, subln, ident, yT):
    N = 2 * TT
    with Place(nc, tag) as pl:
        QK = pl.sb("QK", [P, 2, 2, L])
        VG = pl.sb("VG", [P, 2, 2, TT, D_V])
        B = pl.sb("B", [P, L])
        S = pl.sb("S", [P, 2, L])
        E = pl.sb("E", [P, 2, 2, L])
        W = pl.sb("W", [P, 2, L])
        ET = pl.sb("ET", [P, 2, TT, P])
        mx = pl.sb("mx", [P, 2, 2, 4])
        O = pl.sb("O", [P, TT, D_V])
        junk = pl.sb("junk", [P, 2, D_V])
        hs = pl.sb("hs", [P, 4, TT])
        YT = pl.sb("YT", [P, TT, P])
        sw = pl.sb("sw", [P, 1])
        pS = pl.ps("pS", [P, 2, 2, NC])
        pE = pl.ps("pE", [P, TT, P])
        pO = pl.ps("pO", [P, 2, NC])
        ld = [pl.sem(f"head_loaded{s}") for s in range(2)]
        w_ld = pl.sem("weight_loaded")
        b_in = pl.sem("bias_ready")
        passed = pl.sem("passed")
        dots = pl.sem("logits_ready")
        masked = pl.sem("logits_biased")
        neg = pl.sem("negated")
        expd = pl.sem("exp_done")
        inv = pl.sem("weights_ready")
        half = pl.sem("second_half_weighted")
        comb = pl.sem("halves_combined")
        turned = pl.sem("turned")
        moved = pl.sem("moved")
        summed = pl.sem("values_summed")
        kept = pl.sem("output_kept")
        sqd = pl.sem("output_squared")
        hm = pl.sem("head_mean")
        hr = pl.sem("head_root")
        hi = pl.sem("head_inverse")
        hn = pl.sem("head_normed")
        gat = pl.sem("head_gated")
        h_tr = pl.sem("head_transposed")
        h_mv = pl.sem("head_moved")
        yt_free = pl.sem("YT_free")
        out_st = pl.store_sem("out_stored")
        with nc.Block() as block:
            @block.sync
            def _(sp):
                sp.dma_start(sw[:, :], subln.rearrange("(p o) -> p o", o=1), allow_slow_non_contiguous=True).then_inc(w_ld, DMA)

                def body(h, s, r):
                    sp.wait_ge(h_tr, h + 1)
                    for i in range(2):
                        sp.dma_start(QK[:, s, i, :], qkT[bass.ds(i * D + h * P, P), :]).then_inc(ld[s], DMA)
                        sp.dma_start(VG[:, s, i, :, :], vg[:, bass.ds(i * D + h * P, P)].rearrange("(t p) d -> p t d", p=P)
                                     ).then_inc(ld[s], DMA)
                pairs(sp, D_H, body)

            @block.gpsimd
            def _(pool):
                pool.sem_inc(yt_free, 1)

                def body(h, s, r):
                    pool.wait_ge(masked, h * N + 2)
                    pool.tensor_copy(B[:, 0:L - NEAR].unsqueeze(1),
                                     far[:, bass.ds(h, 1)].unsqueeze(2).to_broadcast([P, 1, L - NEAR])).then_inc(b_in, 1)
                    pool.tensor_copy(B[:, L - NEAR:L].unsqueeze(1), near[:, bass.ds(h, 1), :]).then_inc(b_in, 1)
                    pool.wait_ge(hn, h + 1)
                    pool.tensor_tensor(O[:, :, :], O[:, :, :], VG[:, s, 1, :, :], ALU.mult).then_inc(gat, 1)
                    pool.wait_ge(h_mv, h + 2)
                    pool.dma_start(yT[bass.ds(h * P, P), :], YT[:, :, :].rearrange("p a b -> p (a b)")).then_inc(out_st, DMA)
                    pool.wait_ge(out_st, (h + 1) * DMA)
                    pool.sem_inc(yt_free, 1)
                pairs(pool, D_H, body)

            @block.tensor
            def _(pe):
                pe.sem_inc(turned, 2)
                pe.sem_inc(summed, 2)
                pe.sem_inc(h_tr, 2)

                def body(h, s, r):
                    def logits(qb):
                        for a in range(2):
                            rows = slice(a * D_QK, (a + 1) * D_QK)
                            pe.wait_ge(masked, h * N + 2 * qb + a + 1)
                            for c in range(0, (qb + 1) * P, NC):
                                k = min(NC, (qb + 1) * P - c)
                                mm = pe.matmul(pS[:, a, c // NC, 0:k], QK[rows, s, 0, qb * P:(qb + 1) * P],
                                               QK[rows, s, 1, c:c + k], start=True, stop=True)
                            mm.then_inc(dots, 1)

                    def output(qb):
                        m = h * TT + qb
                        pe.wait_ge(comb, m + 3)
                        pe.wait_ge(moved, m + 1)
                        if qb == 0:
                            pe.wait_ge(h_mv, h + 1)
                        for c in range(qb + 1):
                            mm = pe.transpose(pE[:, c, :], W[:, qb % 2, c * P:(c + 1) * P], ident[:, :])
                        mm.then_inc(turned, 1)
                        pe.wait_ge(moved, m + 2)
                        pe.wait_ge(kept, m + 1)
                        pe.wait_ge(sqd, m + 1)
                        for c in range(qb + 1):
                            mm = pe.matmul(pO[:, qb % 2, 0:D_V], ET[:, qb % 2, c, :], VG[:, s, 0, c, :],
                                           start=c == 0, stop=c == qb)
                        mm.then_inc(summed, 1)

                    pe.wait_ge(ld[s], (r + 1) * 4 * DMA)
                    logits(0)
                    for qb in range(TT):
                        if qb + 1 < TT:
                            logits(qb + 1)
                        output(qb)
                    pe.wait_ge(gat, h + 1)
                    pe.wait_ge(moved, (h + 1) * TT + 1)
                    for c in range(TT):
                        mm = pe.transpose(pE[:, c, :], O[:, c, :], ident[:, :])
                    mm.then_inc(h_tr, 1)
                pairs(pe, D_H, body)

            @block.vector
            def _(dve):
                dve.sem_inc(masked, 2)
                dve.sem_inc(comb, 2)
                dve.sem_inc(kept, 2)
                dve.sem_inc(h_mv, 1)
                dve.wait_ge(w_ld, DMA)

                def body(h, s, r):
                    def bias(qb):
                        w = (qb + 1) * P
                        for a in range(2):
                            n = h * N + 2 * qb + a
                            v = mx[:, qb % 2, a, :]
                            if qb == 0 and a == 0:
                                dve.wait_ge(b_in, 2 * h + 2)
                            dve.wait_ge(dots, n + 1)
                            dve.wait_ge(expd, n + 1)
                            dve.sem_inc(passed, 1)
                            dve.tensor_tensor_reduce(S[:, a, 0:w], pS[:, a, :, :].rearrange("p a b -> p (a b)")[:, 0:w],
                                                     B[:, L - w:L], D_QK ** -0.5, GONE, ALU.add, ALU.max,
                                                     v[:, 0:1]).then_inc(masked, 1)
                            dve.wait_ge(masked, n + 3)
                            dve.tensor_scalar(v[:, 1:2], v[:, 0:1], -1.0, None, ALU.mult).then_inc(neg, 1)

                    def combine(qb):
                        m, w = h * TT + qb, (qb + 1) * P
                        v = mx[:, qb % 2, :, :]
                        dve.wait_ge(expd, 2 * m + 4)
                        dve.reciprocal(v[:, :, 3:4], v[:, :, 2:3]).then_inc(inv, 1)
                        dve.wait_ge(inv, 2 * m + 1)
                        dve.tensor_scalar(v[:, 1, 3:4], v[:, 1, 3:4], lam[:, :], None, ALU.mult).then_inc(inv, 1)
                        dve.wait_ge(inv, 2 * m + 2)
                        dve.wait_ge(turned, m + 1)
                        dve.tensor_scalar(W[:, qb % 2, 0:w], E[:, qb % 2, 1, 0:w], v[:, 1, 3:4], None, ALU.mult).then_inc(half, 1)
                        dve.wait_ge(half, m + 1)
                        dve.scalar_tensor_tensor(W[:, qb % 2, 0:w], E[:, qb % 2, 0, 0:w], v[:, 0, 3:4], W[:, qb % 2, 0:w],
                                                 ALU.mult, ALU.add).then_inc(comb, 1)

                    def keep(qb):
                        m = h * TT + qb
                        dve.wait_ge(summed, m + 3)
                        if qb == 0:
                            dve.wait_ge(h_tr, h + 2)
                        dve.tensor_copy(O[:, qb, :], pO[:, qb % 2, 0:D_V]).then_inc(kept, 1)

                    bias(0)
                    for qb in range(TT):
                        if qb + 1 < TT:
                            bias(qb + 1)
                        combine(qb)
                        if qb:
                            keep(qb - 1)
                    keep(TT - 1)
                    dve.wait_ge(sqd, (h + 1) * TT + 2)
                    dve.tensor_scalar(hs[:, 1, :], hs[:, 0, :], 1.0 / D_V, EPS, ALU.mult, ALU.add).then_inc(hm, 1)
                    dve.wait_ge(hr, h + 1)
                    dve.reciprocal(hs[:, 3, :], hs[:, 2, :]).then_inc(hi, 1)
                    dve.wait_ge(hi, h + 1)
                    dve.wait_ge(kept, (h + 1) * TT + 2)
                    dve.tensor_tensor(O[:, :, :], O[:, :, :], hs[:, 3, :].unsqueeze(2).to_broadcast([P, TT, D_V]),
                                      ALU.mult).then_inc(hn, 1)
                    dve.wait_ge(h_tr, h + 3)
                    dve.wait_ge(yt_free, h + 1)
                    dve.tensor_scalar(YT[:, :, :], pE[:, :, :], sw[:, :], 1.0 - LAM_INIT, ALU.mult, ALU.mult).then_inc(h_mv, 1)
                pairs(dve, D_H, body)

            @block.scalar
            def _(act):
                act.sem_inc(expd, 2)
                act.sem_inc(moved, 1)
                act.sem_inc(sqd, 2)

                def body(h, s, r):
                    def exps(qb):
                        w = (qb + 1) * P
                        for a in range(2):
                            n = h * N + 2 * qb + a
                            act.wait_ge(neg, n + 1)
                            act.wait_ge(comb, h * TT + qb + 1)
                            act.activation(E[:, qb % 2, a, 0:w], S[:, a, 0:w], ACT.Exp, bias=mx[:, qb % 2, a, 1:2],
                                           accum_out=mx[:, qb % 2, a, 2:3]).then_inc(expd, 1)

                    def move(qb):
                        m = h * TT + qb
                        act.wait_ge(turned, m + 3)
                        act.wait_ge(summed, m + 1)
                        act.activation(ET[:, qb % 2, 0:qb + 1, :], pE[:, 0:qb + 1, :], ACT.Copy).then_inc(moved, 1)

                    def squares(qb):
                        m = h * TT + qb
                        act.wait_ge(kept, m + 3)
                        act.wait_ge(sqd, m + 1)
                        act.activation(junk[:, qb % 2, :], pO[:, qb % 2, 0:D_V], ACT.Square, accum_out=hs[:, 0, qb:qb + 1]).then_inc(sqd, 1)

                    exps(0)
                    for qb in range(TT):
                        if qb + 1 < TT:
                            exps(qb + 1)
                        move(qb)
                        if qb:
                            squares(qb - 1)
                    squares(TT - 1)
                    act.wait_ge(hm, h + 1)
                    act.activation(hs[:, 2, :], hs[:, 1, :], ACT.Sqrt).then_inc(hr, 1)
                pairs(act, D_H, body)


R_H, R_D = 16, 128
R_W = R_H * R_D
LEVELS = 7
HALVES = [P >> (i + 1) for i in range(LEVELS)]


def level_masks():
    s, t = np.arange(P)[:, None], np.arange(P)[None, :]
    levels = [((s // (2 * h) == t // (2 * h)) & (s % (2 * h) < h) & (t % (2 * h) >= h)) for h in HALVES]
    return np.stack(levels + [s == t], axis=1).astype(np.float32)


def linear_recurrence(nc, tag, qfT, ig, lower, masks, norm_w, ident, yT):
    K = LEVELS + 1
    C = TT
    assert K == C
    with Place(nc, tag) as pl:
        lw = pl.sb("lw", [P, 4, R_H])
        mk = pl.sb("mk", [P, K, P])
        first = pl.sb("first", [P, L])
        nw = pl.sb("nw", [P, 1])
        Q = pl.sb("Q", [P, 2, L])
        F = pl.sb("F", [P, 2, L])
        V = pl.sb("V", [P, 2, C, R_D])
        G = pl.sb("G", [P, 2, C, R_D])
        KK = pl.sb("KK", [P, L])
        LF = pl.sb("LF", [P, L])
        BB = pl.sb("BB", [P, L])
        DD = pl.sb("DD", [P, 2, L])
        QL = pl.sb("QL", [P, 2, L])
        KL = pl.sb("KL", [P, 2, L])
        KE = pl.sb("KE", [P, L])
        QE = pl.sb("QE", [P, 2, L])
        KT = pl.sb("KT", [P, 2, C, R_D])
        AT = pl.sb("AT", [P, 2, C, P])
        EL = pl.sb("EL", [P, 2, C])
        ST = pl.sb("ST", [P, R_D])
        O = pl.sb("O", [P, 2, C, R_D])
        junk = pl.sb("junk", [P, 2, R_D])
        hs = pl.sb("hs", [P, 2, 4, C])
        YT = pl.sb("YT", [P, C, P])
        pA = pl.ps("pA", [P, 2, C, P])
        pK = pl.ps("pK", [P, 4, P])
        pO = pl.ps("pO", [P, 2, NC])
        pS = pO[:, :, 2 * R_D:3 * R_D]
        loaded = pl.sem("loaded")
        chain = pl.sem("dve")
        set_up = pl.sem("set_up")
        l_in = pl.sem("lower_difference")
        l_ex = pl.sem("lower_exp")
        with nc.Block() as block:
            @block.sync
            def _(sp):
                for i in range(2):
                    sp.dma_start(lw[:, i, :], lower[i, :].rearrange("(h p) -> p h", p=P),
                                 allow_slow_non_contiguous=True).then_inc(loaded, DMA)
                sp.dma_start(mk[:, :, :], masks).then_inc(loaded, DMA)
                sp.dma_start(nw[:, :], norm_w.rearrange("(p o) -> p o", o=1),
                             allow_slow_non_contiguous=True).then_inc(loaded, DMA)
                sp.wait_ge(loaded, 4 * DMA)

            @block.gpsimd
            def _(pool):
                for x in (AT, QL, KL):
                    pool.memset(x[:], 0.0).then_inc(set_up, 1)
                pool.memset(first[:, :], 1.0).then_inc(set_up, 1)
                pool.wait_ge(set_up, 4)
                pool.memset(first[:, :].rearrange("p (c t) -> p c t", t=P)[:, :, 0:1], 0.0).then_inc(set_up, 1)
                pool.wait_ge(set_up, 5)

            @block.vector
            def _(dve):
                link = Link(dve, chain)
                dve.wait_ge(loaded, 4 * DMA)
                link(dve.tensor_tensor(lw[:, 2, :], lw[:, 0, :], lw[:, 1, :], ALU.max))
                link(dve.tensor_tensor(lw[:, 0, :], lw[:, 0, :], lw[:, 2, :], ALU.subtract))
                dve.tensor_tensor(lw[:, 1, :], lw[:, 1, :], lw[:, 2, :], ALU.subtract).then_inc(l_in, 1)
                dve.wait_ge(l_ex, 1)
                link(dve.tensor_tensor(lw[:, 2, :], lw[:, 0, :], lw[:, 1, :], ALU.add))
                link(dve.reciprocal(lw[:, 3, :], lw[:, 2, :]))
                link(dve.tensor_tensor(lw[:, 2, :], lw[:, 1, :], lw[:, 3, :], ALU.mult))
                link(dve.tensor_scalar(lw[:, 3, :], lw[:, 2, :], -1.0, 1.0, ALU.mult, ALU.add))

            @block.scalar
            def _(act):
                act.wait_ge(l_in, 1)
                act.activation(lw[:, 0:2, :], lw[:, 0:2, :], ACT.Exp).then_inc(l_ex, 1)

        q_ld = [pl.sem(f"head_loaded{s}") for s in range(2)]
        v_ld = [pl.sem(f"values_loaded{s}") for s in range(2)]
        g_ld = [pl.sem(f"gates_loaded{s}") for s in range(2)]
        fs = pl.sem("f_ready")
        ks = pl.sem("keys_ready")
        lf = pl.sem("log_ready")
        bs = pl.sem("b_ready")
        ds = pl.sem("exponents_ready")
        es = pl.sem("exponentials_ready")
        qk = pl.sem("factors_ready")
        pr = pl.sem("product_ready")
        at = pl.sem("weights_taken")
        ad = pl.sem("head_taken")
        bl = pl.sem("last_difference_ready")
        ex = pl.sem("chunk_exponentials_ready")
        ke = pl.sem("chunk_factors_ready")
        kt = pl.sem("keys_transposed")
        km = pl.sem("keys_moved")
        ch = pl.sem("chunk_ready")
        su = pl.sem("state_ready")
        om = pl.sem("output_moved")
        sqd = pl.sem("output_squared")
        hm = pl.sem("head_mean")
        hr = pl.sem("head_root")
        hi = pl.sem("head_inverse")
        hn = pl.sem("head_normed")
        hg = pl.sem("head_gated")
        ct = pl.sem("outputs_transposed")
        cm = pl.sem("outputs_moved")
        yt_free = pl.sem("YT_free")
        out_st = pl.sem("out_stored")
        passed_sp = pl.sem("passed_sync")
        passed = pl.sem("passed")

        def items(body):
            def run(eng):
                body(0, 0, 0, "A")
                body(1, 1, 0, "AB")
                with eng.Fori(0, (R_H - 2) // 2) as r:
                    body(r * 2 + 2, 0, r + 1, "ABC")
                    body(r * 2 + 3, 1, r + 1, "ABC")
                body(R_H, 0, R_H // 2, "BC")
                body(R_H + 1, 1, R_H // 2, "C")
            return run

        def halves(x, h):
            return x.rearrange("p (b u t) -> p b u t", u=2, t=h)

        def chunks(x):
            return x.rearrange("p (c t) -> p c t", t=P)

        with nc.Block() as block:
            @block.sync
            def _(sp):
                def body(n, s, r, steps):
                    if "A" in steps:
                        sp.wait_ge(ad, n + 1)
                        sp.sem_inc(passed_sp, 1)
                        sp.dma_start(Q[:, s, :], qfT[bass.ds(n * P, P), :]).then_inc(q_ld[s], DMA)
                        sp.dma_start(F[:, s, :], qfT[bass.ds(n * P + R_W, P), :]).then_inc(q_ld[s], DMA)
                        sp.wait_ge(ch, (n + 1) * C)
                        sp.sem_inc(passed_sp, 1)
                        sp.dma_start(V[:, s, :, :], ig[:, bass.ds(n * P, P)].rearrange("(c p) d -> p c d", p=P)
                                     ).then_inc(v_ld[s], DMA)
                        sp.wait_ge(hg, n + 1)
                        sp.sem_inc(passed_sp, 1)
                        sp.dma_start(G[:, s, :, :], ig[:, bass.ds(n * P + R_W, P)].rearrange("(c p) d -> p c d", p=P)
                                     ).then_inc(g_ld[s], DMA)
                    if "C" in steps:
                        sp.wait_ge(cm, (n - 2) * 2 + 2)
                        sp.sem_inc(passed_sp, 1)
                        sp.dma_start(yT[bass.ds((n - 2) * P, P), :], YT[:, :, :].rearrange("p c t -> p (c t)")
                                     ).then_inc(out_st, DMA)
                        sp.wait_ge(out_st, (n - 1) * DMA)
                        sp.sem_inc(yt_free, 1)
                sp.sem_inc(yt_free, 1)
                items(body)(sp)

            @block.tensor
            def _(pe):
                pe.sem_inc(kt, 1)
                pe.sem_inc(ch, 2 * C)
                pe.sem_inc(ct, 3)

                def body(n, s, r, steps):
                    A, B, Cs = ("A" in steps), ("B" in steps), ("C" in steps)
                    m, sb = n - 1, 1 - s
                    for j in range(K):
                        if A:
                            if j == 0:
                                pe.wait_ge(ks, n + 1)
                            else:
                                pe.wait_ge(qk, n * LEVELS + j + 1)
                            pe.wait_ge(at, n * K + j + 1)
                            for c in range(C):
                                t = slice(c * P, (c + 1) * P)
                                lh, rh = (KK[:, t], Q[:, s, t]) if j == 0 else (KL[:, (j - 1) % 2, t], QL[:, (j - 1) % 2, t])
                                mm = pe.matmul(pA[:, j % 2, c, :], lh, rh, start=True, stop=True, skip_group_check=True)
                            mm.then_inc(pr, 1)
                        if B:
                            i = m * C + j
                            if j == 0:
                                pe.wait_ge(v_ld[sb], (r if s == 0 else r + 1) * DMA)
                                pe.wait_ge(at, m * K + K + 2)
                                pe.wait_ge(km, m * 2 + 2)
                            pe.wait_ge(sqd, i + 1)
                            pe.matmul(pS[:, j % 2, 0:R_D], KT[:, sb, j, :], V[:, sb, j, :], start=True, stop=True,
                                      skip_group_check=True)
                            pe.matmul(pO[:, j % 2, 0:R_D], AT[:, sb, j, :], V[:, sb, j, :], start=True, stop=False)
                            pe.wait_ge(su, i + 1)
                            pe.matmul(pO[:, j % 2, 0:R_D], QE[:, sb, j * P:(j + 1) * P], ST[:, :], start=False,
                                      stop=True).then_inc(ch, 1)
                        if Cs and j in (3, 4):
                            h = j - 3
                            pe.wait_ge(hg, n + 1)
                            if h == 0:
                                pe.wait_ge(km, n * 2 if A else 2 * R_H)
                            else:
                                pe.wait_ge(cm, (n - 2) * 2 + 1)
                            for c in range(4):
                                mm = pe.transpose(pK[:, c, :], O[:, s, 4 * h + c, :], ident[:, :])
                            mm.then_inc(ct, 1)
                        if A and j in (5, 6):
                            h = j - 5
                            pe.wait_ge(ke, n + 1)
                            if h:
                                pe.wait_ge(km, n * 2 + 1)
                            elif Cs:
                                pe.wait_ge(cm, (n - 2) * 2 + 2)
                            elif B:
                                pe.wait_ge(km, n * 2)
                            for c in range(4):
                                mm = pe.transpose(pK[:, c, :], KE[:, (4 * h + c) * P:(4 * h + c + 1) * P], ident[:, :])
                            mm.then_inc(kt, 1)
                items(body)(pe)

            @block.vector
            def _(dve):
                dve.sem_inc(bs, 1)
                dve.sem_inc(qk, 1)
                dve.sem_inc(at, 2)
                dve.sem_inc(ad, 2)

                def body(n, s, r, steps):
                    A, B, Cs = ("A" in steps), ("B" in steps), ("C" in steps)
                    m, sb = n - 1, 1 - s
                    if A:
                        dve.wait_ge(q_ld[s], (r + 1) * 2 * DMA)
                        dve.tensor_scalar(F[:, s, :], F[:, s, :], lw[:, 3, bass.ds(n, 1)], lw[:, 2, bass.ds(n, 1)], ALU.mult,
                                          ALU.add).then_inc(fs, 1)
                        dve.wait_ge(fs, n + 1)
                        dve.tensor_scalar(KK[:, :], F[:, s, :], -1.0, 1.0, ALU.mult, ALU.add).then_inc(ks, 1)
                    if Cs:
                        dve.wait_ge(sqd, (n - 1) * C + 2)
                        dve.tensor_scalar(hs[:, s, 1, :], hs[:, s, 0, :], 1.0 / R_D, EPS, ALU.mult, ALU.add).then_inc(hm, 1)
                    if A:
                        dve.wait_ge(lf, n + 1)
                        dve.tensor_tensor_scan(BB[:, :], first[:, :], LF[:, :], 0.0, ALU.mult, ALU.add).then_inc(bs, 1)
                    if Cs:
                        dve.wait_ge(hr, n - 1)
                        dve.reciprocal(hs[:, s, 3, :], hs[:, s, 2, :]).then_inc(hi, 1)
                        dve.wait_ge(hi, n - 1)
                        dve.tensor_tensor(O[:, s, :, :], O[:, s, :, :], hs[:, s, 3, :].unsqueeze(2).to_broadcast([P, C, R_D]),
                                          ALU.mult).then_inc(hn, 1)
                    for j in range(K):
                        if A and j < LEVELS:
                            h = HALVES[j]
                            dve.wait_ge(es, n * LEVELS + j + 1)
                            e, q, k = (halves(x, h) for x in (DD[:, j % 2, :], Q[:, s, :], KK[:, :]))
                            dve.tensor_tensor(halves(QL[:, j % 2, :], h)[:, :, 1, :], q[:, :, 1, :], e[:, :, 1, :], ALU.mult)
                            dve.tensor_tensor(halves(KL[:, j % 2, :], h)[:, :, 0, :], k[:, :, 0, :], e[:, :, 0, :],
                                              ALU.mult).then_inc(qk, 1)
                        if A and j == 2:
                            dve.wait_ge(ex, n + 1)
                            dve.tensor_tensor(QE[:, s, :], Q[:, s, :], F[:, s, :], ALU.mult)
                            dve.tensor_tensor(KE[:, :], KK[:, :], KE[:, :], ALU.mult).then_inc(ke, 1)
                        if B:
                            i = m * C + j
                            if j == 0:
                                dve.memset(ST[:, :], 0.0).then_inc(su, 1)
                            dve.wait_ge(ch, i + 1 + 2 * C)
                            if j < C - 1:
                                dve.wait_ge(su, i + 1)
                                dve.scalar_tensor_tensor(ST[:, :], ST[:, :], EL[:, sb, j:j + 1], pS[:, j % 2, 0:R_D],
                                                         ALU.mult, ALU.add).then_inc(su, 1)
                            if j == 0:
                                dve.wait_ge(ct, m * 2 + 1)
                            dve.tensor_copy(O[:, sb, j, :], pO[:, j % 2, 0:R_D]).then_inc(om, 1)
                        if A:
                            dve.wait_ge(pr, n * K + j + 1)
                            if j:
                                dve.wait_ge(at, n * K + j + 2)
                            dve.sem_inc(passed, 1)
                            kind = K - 1 if j == 0 else j - 1
                            dve.copy_predicated(AT[:, s, :, :], mk[:, kind, :].bitcast(U32).unsqueeze(1).to_broadcast([P, C, P]),
                                                pA[:, j % 2, :, :]).then_inc(at, 1)
                    if A:
                        dve.wait_ge(at, n * K + K + 2)
                        dve.sem_inc(ad, 1)
                items(body)(dve)

            @block.scalar
            def _(act):
                act.sem_inc(sqd, 2)

                def body(n, s, r, steps):
                    A, B, Cs = ("A" in steps), ("B" in steps), ("C" in steps)
                    m, sb = n - 1, 1 - s
                    if A:
                        act.wait_ge(fs, n + 1)
                        act.wait_ge(bs, n + 1)
                        act.activation(LF[:, :], F[:, s, :], ACT.Ln).then_inc(lf, 1)
                    if Cs:
                        act.wait_ge(hm, n - 1)
                        act.activation(hs[:, s, 2, :], hs[:, s, 1, :], ACT.Sqrt).then_inc(hr, 1)
                    for j in range(K):
                        if A and j < LEVELS:
                            act.wait_ge(ds, n * LEVELS + j + 1)
                            act.activation(DD[:, j % 2, :], DD[:, j % 2, :], ACT.Exp).then_inc(es, 1)
                        if A and j == 0:
                            act.wait_ge(ks, n + 1)
                            act.activation(F[:, s, :], BB[:, :], ACT.Exp)
                            act.activation(EL[:, s, :].unsqueeze(2), chunks(BB[:, :])[:, :, P - 1:P], ACT.Exp)
                            act.wait_ge(bl, n + 1)
                            act.activation(KE[:, :], KE[:, :], ACT.Exp).then_inc(ex, 1)
                        if Cs and j in (3, 4):
                            h = j - 3
                            if h == 0:
                                act.wait_ge(yt_free, n - 1)
                            act.wait_ge(ct, (n - 2) * 2 + h + 4)
                            act.activation(YT[:, 4 * h:4 * h + 4, :], pK[:, :, :], ACT.Copy, scale=nw[:, :]).then_inc(cm, 1)
                        if A and j in (5, 6):
                            h = j - 5
                            act.wait_ge(kt, n * 2 + h + 2)
                            act.activation(KT[:, s, 4 * h:4 * h + 4, :], pK[:, :, :], ACT.Copy).then_inc(km, 1)
                        if B:
                            i = m * C + j
                            act.wait_ge(om, i + 1)
                            act.wait_ge(sqd, i + 1)
                            act.activation(junk[:, j % 2, :], pO[:, j % 2, 0:R_D], ACT.Square,
                                           accum_out=hs[:, sb, 0, j:j + 1]).then_inc(sqd, 1)
                items(body)(act)

            @block.gpsimd
            def _(pool):
                pool.sem_inc(hg, 2)

                def body(n, s, r, steps):
                    A, Cs = ("A" in steps), ("C" in steps)
                    for j in range(LEVELS):
                        if A:
                            h = HALVES[j]
                            if j == 0:
                                pool.wait_ge(bs, n + 2)
                                pool.wait_ge(qk, n * LEVELS + 1)
                            elif j >= 2:
                                pool.wait_ge(qk, n * LEVELS + j)
                            b, d = halves(BB[:, :], h), halves(DD[:, j % 2, :], h)
                            mid = b[:, :, 0, h - 1:h].to_broadcast([P, L // (2 * h), h])
                            pool.tensor_tensor(d[:, :, 1, :], b[:, :, 1, :], mid, ALU.subtract)
                            pool.tensor_tensor(d[:, :, 0, :], mid, b[:, :, 0, :], ALU.subtract).then_inc(ds, 1)
                        if A and j == 0:
                            pool.wait_ge(kt, n * 2 + 1)
                            b = chunks(BB[:, :])
                            pool.tensor_tensor(chunks(KE[:, :]), b[:, :, P - 1:P].to_broadcast([P, C, P]), b,
                                               ALU.subtract).then_inc(bl, 1)
                        if Cs and j == 1:
                            pool.wait_ge(hn, n - 1)
                            pool.wait_ge(g_ld[s], r * DMA)
                            pool.tensor_tensor(O[:, s, :, :], O[:, s, :, :], G[:, s, :, :], ALU.mult).then_inc(hg, 1)
                items(body)(pool)


def norm_tokens(nc, tag, x, g, out):
    with Place(nc, tag) as pl:
        xin = pl.sb("xin", [P, 2, D])
        y = pl.sb("y", [P, 2, D])
        sq = pl.sb("sq", [P, 2, D])
        st = pl.sb("st", [P, 2, 4])
        gb = pl.sb("gb", [P, D])
        ld = [pl.sem(f"x_loaded{s}") for s in range(2)]
        g_ld = pl.sem("gain_loaded")
        summed = pl.sem("squares_summed")
        mean = pl.sem("mean_ready")
        root = pl.sem("root_ready")
        inv = pl.sem("inverse_ready")
        scaled = pl.sem("rows_scaled")
        out_st = pl.store_sem("out_stored")
        y_free = pl.sem("y_free")
        with nc.Block() as block:
            @block.sync
            def _(sp):
                sp.dma_start(gb[:, :], g.partition_broadcast(P)).then_inc(g_ld, DMA)

                def body(t, s, r):
                    sp.wait_ge(scaled, t + 1)
                    sp.dma_start(xin[:, s, :], x[bass.ds(t * P, P), :]).then_inc(ld[s], DMA)
                pairs(sp, TT, body)

            @block.scalar
            def _(act):
                def body(t, s, r):
                    act.wait_ge(ld[s], (r + 1) * DMA)
                    act.wait_ge(inv, t + 1)
                    act.activation(sq[:, s, :], xin[:, s, :], ACT.Square, accum_out=st[:, s, 0:1]).then_inc(summed, 1)
                    act.wait_ge(mean, t + 1)
                    act.activation(st[:, s, 2:3], st[:, s, 1:2], ACT.Sqrt).then_inc(root, 1)
                pairs(act, TT, body)

            @block.vector
            def _(dve):
                dve.sem_inc(scaled, 2)
                dve.sem_inc(inv, 2)
                dve.wait_ge(g_ld, DMA)

                def body(t, s, r):
                    dve.wait_ge(summed, t + 1)
                    dve.tensor_scalar(st[:, s, 1:2], st[:, s, 0:1], 1.0 / D, EPS, ALU.mult, ALU.add).then_inc(mean, 1)
                    dve.wait_ge(root, t + 1)
                    dve.reciprocal(st[:, s, 3:4], st[:, s, 2:3]).then_inc(inv, 1)
                    dve.wait_ge(inv, t + 3)
                    dve.wait_ge(y_free, t + 1)
                    dve.scalar_tensor_tensor(y[:, s, :], xin[:, s, :], st[:, s, 3:4], gb[:, :], ALU.mult,
                                             ALU.mult).then_inc(scaled, 1)
                pairs(dve, TT, body)

            @block.gpsimd
            def _(pool):
                pool.sem_inc(y_free, 2)

                def body(t, s, r):
                    pool.wait_ge(scaled, t + 3)
                    pool.dma_start(out[bass.ds(t * P, P), :], y[:, s, :]).then_inc(out_st, DMA)
                    pool.wait_ge(out_st, (t + 1) * DMA)
                    pool.sem_inc(y_free, 1)
                pairs(pool, TT, body)


Z_AT, XBC_AT, DT_AT = 0, X2, X2 + XB2 + G2 * N2
QK_AT = DT_AT + H2
V_AT = QK_AT + 2 * D
GATE_AT = V_AT + D


def build_program(nc, a, out):
    def scratch(name, *shape):
        return nc.dram_tensor(name, shape, F32, kind="Internal").ap()

    p1 = scratch("first_projection", L, WI0 + I_H)
    gT = scratch("gates", 2 * D, L)
    ysT, yaT, mT = scratch("y_ssm", S_W, L), scratch("y_att", A_H * A_D, L), scratch("merged", D, L)
    x1, hT, x2 = scratch("x1", L, D), scratch("hidden", a["w_ffn_gate"].shape[2], L), scratch("x2", L, D)
    z, xbcT, dt = scratch("z", L, X2), scratch("xbc", XB2 + G2 * N2, L), scratch("dt", L, H2)
    xbt, bcT = scratch("x_b", L, 2 * X2), scratch("b_c", 2 * G2 * N2, L)
    qkT, vg, skew = scratch("q_k", 2 * D, L), scratch("v_g", L, 2 * D), scratch("skew", P * D_H * SKEW)
    yT, x3 = scratch("y_even", 2 * D, L), scratch("x3", L, D)
    qfT, ig = scratch("q_f", 2 * R_W, L), scratch("i_g", L, 2 * R_W)
    yhT, x4 = scratch("y_odd", R_W, L), scratch("x4", L, D)

    with ExitStack() as ctx:
        ident = ctx.enter_context(nc.sbuf_tensor("ident", [P, P], F32))
        make_identity(nc, ident)

        def layer_input(tag, x, g, projections):
            with Place(nc, tag) as pl:
                XT = pl.sb("XT", [P, 2, KD, L], F32R)
                norm_to_features(nc, tag + "_norm", x, g, XT, ident)
                projections(XT)

        w = a["w_in"][0]

        def first(XT):
            project(nc, "in", XT, (
                (w[:, 0:2 * NC], p1[:, 0:2 * NC], False, ACT.Copy),
                (w[:, WI0 + I_H:], gT, True, ACT.Sigmoid),
                (w[:, 2 * NC:WI0 + I_H], p1[:, 2 * NC:WI0 + I_H], False, ACT.Copy)))
        layer_input("l0", a["x"][0], a["norm1_g"][0], first)
        s5 = {n: a[n] for n in ("A_re", "A_im", "B_re", "B_im", "C_re", "C_im")}
        s5.update({n: a[n][0] for n in ("log_dt", "D_skip", "w_glu", "b_glu")})
        s5_branch(nc, "s5", p1, s5, ident, ysT)
        with Place(nc, "att") as pl:
            F = pl.sb("F", [P, 8, L])
            V = pl.sb("V", [P, TT, A_D])
            wi = pl.sb("wi", [P, TT, I_H])
            M = pl.sb("M", [P, mask_at(TT)])
            sparse_prepare(nc, "ap", p1, (a["q_norm_g"][0], a["k_norm_g"][0], a["idx_k_norm_g"][0]), F, V, wi, ident)
            sparse_masks(nc, "am", F, wi, M)
            sparse_attend(nc, "aa", F, V, M, ident, yaT)
        merge_branches(nc, "merge", ysT, yaT, a["w_proj_ssm"][0], a["w_proj_attn"][0], gT, mT)
        reduce_tokens(nc, "out1", mT, a["w_out"][0], a["x"][0], x1)
        layer_input("ffn", x1, a["norm2_g"][0],
                    lambda XT: swiglu_up(nc, "up", XT, a["w_ffn_gate"][0], a["w_ffn_up"][0], hT))
        reduce_tokens(nc, "down", hT, a["w_ffn_down"][0], x1, x2)

        e = a["even_w_in_2"][0]

        def even(XT):
            project(nc, "even", XT, (
                (e[:, Z_AT:XBC_AT], z, False, ACT.Silu),
                (e[:, GATE_AT:GATE_AT + D], vg[:, D:2 * D], False, ACT.Silu),
                (e[:, XBC_AT:DT_AT], xbcT, True, ACT.Copy),
                (e[:, QK_AT:V_AT], qkT, True, ACT.Copy),
                (e[:, V_AT:GATE_AT], vg[:, 0:D], False, ACT.Copy),
                (e[:, DT_AT:QK_AT], dt, False, ACT.Copy)))
        layer_input("l1", x2, a["norm_w_2"][0], even)
        conv_silu(nc, "cx", 0, X2 // P, xbcT, a["conv_w_2"][0], a["conv_b_2"][0], ident, None, xbt)
        conv_silu(nc, "cb", X2 // P, 2 * G2, xbcT, a["conv_w_2"][0], a["conv_b_2"][0], ident, bcT, xbt)
        ssd_mixer(nc, "ssd", dt, xbt, bcT, z, {"dt_bias": a["dt_bias_2"][0], "A_log": a["A_log_2"][0],
                                               "D": a["D_skip_2"][0], "norm_w": a["ssd_norm_w_2"][0]}, ident, yT[0:X2, :])
        with Place(nc, "dif") as pl:
            near = pl.sb("near", [P, D_H, NEAR])
            far = pl.sb("far", [P, D_H])
            lam = pl.sb("lam", [P, 1])
            diff_bias(nc, "db", a["rel_bias_2"], a["one_hot"], skew, near, far, lam,
                      [a[n][0] for n in ("lambda_q1_2", "lambda_k1_2", "lambda_q2_2", "lambda_k2_2")])
            diff_attend(nc, "da", qkT, vg, near, far, lam, a["subln_w_2"][0], ident, yT[X2:X2 + D, :])
        reduce_tokens(nc, "out2", yT, a["even_w_out_2"][0], x2, x3)

        o = a["odd_w_in_2"][0]

        def odd(XT):
            project(nc, "odd", XT, (
                (o[:, 0:R_W], qfT[0:R_W, :], True, ACT.Silu),
                (o[:, R_W:2 * R_W], qfT[R_W:2 * R_W, :], True, ACT.Sigmoid),
                (o[:, 2 * R_W:3 * R_W], ig[:, 0:R_W], False, ACT.Copy),
                (o[:, 3 * R_W:4 * R_W], ig[:, R_W:2 * R_W], False, ACT.Silu)))
        layer_input("l2", x3, a["norm_w_2"][1], odd)
        linear_recurrence(nc, "hg", qfT, ig, a["hgrn_lower_bounds_2"], a["level_masks"], a["hgrn_norm_w_2"][0], ident, yhT)
        reduce_tokens(nc, "out3", yhT, a["odd_w_out_2"][0], x3, x4)
        norm_tokens(nc, "fin", x4, a["final_norm_w_2"], out[0])


def kernel(**inputs):
    import concourse.bacc as bacc
    from concourse.bass_utils import run_bass_kernel_spmd

    arrays = {n: np.ascontiguousarray(v) for n, v in inputs.items()}
    for n in ("A_re", "A_im"):
        arrays[n] = arrays[n].reshape(S_J, P)
    for n in ("B_re", "B_im"):
        arrays[n] = arrays[n].reshape(S_J, P, S_CH)
    for n in ("C_re", "C_im"):
        arrays[n] = np.ascontiguousarray(arrays[n][0].transpose(0, 2, 1)).reshape(S_J, P, S_CH)
    arrays["one_hot"] = bucket_one_hot()
    arrays["level_masks"] = level_masks()

    nc = bacc.Bacc("TRN2", target_bir_lowering=False, num_devices=1)
    named, aps = {}, {}
    for n, v in arrays.items():
        named[f"in_{n}"] = v
        aps[n] = nc.dram_tensor(f"in_{n}", v.shape, mybir.dt.from_np(v.dtype), kind="ExternalInput").ap()
    out = nc.dram_tensor("out", (1, L, D), F32, kind="ExternalOutput").ap()
    build_program(nc, aps, out)
    return run_bass_kernel_spmd(nc, [named], core_ids=[0]).results[0]["out"]
```

```python
from contextlib import ExitStack

import numpy as np

import concourse.bass as bass
from concourse import mybir
from concourse.alu_op_type import AluOpType as ALU

F32 = mybir.dt.float32
F32R = mybir.dt.float32r
U32 = mybir.dt.uint32
ACT = mybir.ActivationFunctionType
AX = mybir.AxisListType

P = 128
L = 1024
D = 1024
TT = L // P
KD = D // P
NC = 512
EPS = 1e-6
DMA = 16
HUGE = 1e30


class Place:

    def __init__(self, nc, tag):
        self.nc, self.tag, self.ctx, self.numbers = nc, tag, ExitStack(), []

    def __enter__(self):
        self.ctx.__enter__()
        return self

    def __exit__(self, *a):
        if self.numbers and a[0] is None:
            self.clear()
        return self.ctx.__exit__(*a)

    def clear(self):
        runs = []
        for n in sorted(self.numbers):
            if runs and runs[-1][1] == n:
                runs[-1][1] = n + 1
            else:
                runs.append([n, n + 1])
        with self.nc.Block() as block:
            @block.gpsimd
            def _(pool):
                for first, end in runs:
                    pool.sem_clear(range(first, end))

    def sb(self, name, shape, dt=F32):
        return self.ctx.enter_context(self.nc.sbuf_tensor(f"{self.tag}_{name}", shape, dt))

    def ps(self, name, shape, dt=F32):
        return self.ctx.enter_context(self.nc.psum_tensor(f"{self.tag}_{name}", shape, dt))

    def sem(self, name):
        sem = self.ctx.enter_context(self.nc.semaphore(f"{self.tag}_{name}"))
        self.numbers.append(sem.num)
        return sem

    def store_sem(self, name):
        return self.nc.alloc_semaphore(f"{self.tag}_{name}")


class Link:

    def __init__(self, eng, sem):
        self.eng, self.sem, self.base, self.n = eng, sem, 0, 0

    def __call__(self, ins):
        self.mark(ins)
        self.wait()

    def mark(self, ins):
        ins.then_inc(self.sem, 1)
        self.n += 1

    def wait(self):
        self.eng.wait_ge(self.sem, self.base + self.n)

    def turn(self, r, per):
        self.start, self.per = self.base + self.n, per
        self.base, self.n = self.start + r * per, 0

    def end(self, turns):
        assert self.n == self.per, (self.n, self.per)
        self.base, self.n = self.start + turns * self.per, 0


PASSES = ((0, 0), (0, 1), (1, 0))


def split_product(pe, out, lhs, rhs, steps, start=True, stop=True):
    n = len(steps) * len(PASSES)
    i = 0
    for k in steps:
        for p, q in PASSES:
            mm = pe.matmul(out, lhs(p, k), rhs(q, k), start=start and i == 0, stop=stop and i == n - 1)
            i += 1
    return mm


def pairs(eng, n, body):
    if n >= 4:
        with eng.Fori(0, n // 2) as r:
            for s in range(2):
                body(r * 2 + s, s, r)
    else:
        for i in range(n - n % 2):
            body(i, i % 2, i // 2)
    if n % 2:
        body(n - 1, 0, n // 2)


def make_identity(nc, ident):
    with Place(nc, "id") as pl:
        zero = pl.sem("zeroed")
        made = pl.sem("made")
        with nc.Block() as block:
            @block.gpsimd
            def _(pool):
                pool.memset(ident[:, :], 0.0).then_inc(zero, 1)
                pool.wait_ge(zero, 1)
                pool.affine_select(out=ident[:, :], in_=ident[:, :], compare_op=ALU.not_equal, fill=1.0,
                                   base=0, pattern=[[-1, P]], channel_multiplier=1).then_inc(made, 1)
                pool.wait_ge(made, 1)


def norm_to_features(nc, tag, x, g, XT, ident):
    with Place(nc, tag) as pl:
        xin = pl.sb("xin", [P, TT, D])
        sq = pl.sb("sq", [P, 2, D])
        st = pl.sb("st", [P, 4, TT])
        dg = pl.sb("dg", [P, 2, P])
        gc = pl.sb("gc", [P, KD])
        xg = pl.sb("xg", [P, 2, KD, P])
        pT = pl.ps("pT", [P, 2, KD, P])
        ld = [pl.sem(f"x_loaded{t}") for t in range(TT)]
        g_ld = pl.sem("gain_loaded")
        summed = pl.sem("squares_summed")
        mean = pl.sem("mean_ready")
        root = pl.sem("root_ready")
        inv = pl.sem("inverse_ready")
        diag = pl.sem("diagonal_ready")
        turned = pl.sem("rows_transposed")
        gained = pl.sem("features_scaled")
        hi = pl.sem("hi_stored")
        stored = pl.sem("lo_stored")

        with nc.Block() as block:
            @block.sync
            def _(sp):
                for t in range(TT):
                    sp.dma_start(xin[:, t, :], x[t * P:(t + 1) * P, :]).then_inc(ld[t], DMA)
                    if t == 1:
                        sp.dma_start(gc[:, :], g.rearrange("(k p) -> p k", p=P),
                                     allow_slow_non_contiguous=True).then_inc(g_ld, DMA)

            @block.scalar
            def _(act):
                act.sem_inc(summed, 2)
                for t in range(TT):
                    act.wait_ge(ld[t], DMA)
                    act.wait_ge(summed, t + 1)
                    act.activation(sq[:, t % 2, :], xin[:, t, :], ACT.Square, accum_out=st[:, 0, t:t + 1]).then_inc(summed, 1)
                act.wait_ge(mean, 1)
                act.activation(st[:, 2, :], st[:, 1, :], ACT.Sqrt).then_inc(root, 1)

                def body(t, s, r):
                    act.wait_ge(gained, t + 3)
                    act.activation(XT[:, 0, :, bass.ds(t * P, P)], xg[:, s, :, :], ACT.Copy).then_inc(hi, 1)
                pairs(act, TT, body)

            @block.vector
            def _(dve):
                dve.sem_inc(gained, 2)
                dve.wait_ge(summed, TT + 2)
                dve.tensor_scalar(st[:, 1, :], st[:, 0, :], 1.0 / D, EPS, ALU.mult, ALU.add).then_inc(mean, 1)
                dve.wait_ge(root, 1)
                dve.reciprocal(st[:, 3, :], st[:, 2, :]).then_inc(inv, 1)
                dve.wait_ge(inv, 1)
                dve.wait_ge(g_ld, DMA)

                def diagonal(t, s):
                    dve.wait_ge(turned, t + 1)
                    dve.tensor_scalar(dg[:, s, :], ident[:, :], st[:, 3, bass.ds(t, 1)], None, ALU.mult).then_inc(diag, 1)

                def gain(t, s):
                    dve.wait_ge(turned, t + 3)
                    dve.wait_ge(stored, t + 1)
                    dve.tensor_tensor(xg[:, s, :, :], pT[:, s, :, :],
                                      gc[:, :].unsqueeze(2).to_broadcast([P, KD, P]), ALU.mult).then_inc(gained, 1)

                def body(t, s, r):
                    if s == 0:
                        diagonal(t, 0)
                        diagonal(t + 1, 1)
                    gain(t, s)
                pairs(dve, TT, body)

            @block.gpsimd
            def _(pool):
                pool.sem_inc(stored, 2)

                def body(t, s, r):
                    pool.wait_ge(hi, t + 1)
                    pool.tensor_tensor(XT[:, 1, :, bass.ds(t * P, P)], xg[:, s, :, :],
                                       XT[:, 0, :, bass.ds(t * P, P)].bitcast(F32), ALU.subtract).then_inc(stored, 1)
                pairs(pool, TT, body)

            @block.tensor
            def _(pe):
                pe.sem_inc(turned, 2)
                for t in range(TT):
                    s = t % 2
                    pe.wait_ge(diag, t + 1)
                    pe.wait_ge(gained, t + 1)
                    for k in range(KD):
                        last = pe.matmul(pT[:, s, k, :], xin[:, t, k * P:(k + 1) * P], dg[:, s, :], start=True, stop=True,
                                         skip_group_check=True)
                    last.then_inc(turned, 1)


def project(nc, tag, XT, segments):
    G, B = 8, 4
    with Place(nc, tag) as pl:
        w = pl.sb("w", [P, 2, KD, NC])
        ws = pl.sb("ws", [P, 2, 2, KD, NC], F32R)
        stage = pl.sb("stage", [P, B, NC])
        acc = pl.ps("acc", [P, B, NC])
        w_ld = [pl.sem(f"w_loaded{s}") for s in range(2)]
        rounded = pl.sem("w_rounded")
        split = pl.sem("w_split")
        out_st = pl.store_sem("out_stored")
        staged = pl.sem("stage_free")
        summed = pl.sem("group_summed")
        moved = pl.sem("group_moved")

        def each(eng, work):
            done = 0
            for seg in segments:
                width = min(NC, seg[0].shape[1])
                chunks = seg[0].shape[1] // width
                assert done % 2 == 0 and width * chunks == seg[0].shape[1]
                pairs(eng, chunks, lambda c, s, r: work(c + done, s, r + done // 2, c * width, width, seg))
                done += chunks

        with nc.Block() as block:
            @block.sync
            def _(sp):
                def body(c, s, r, col, width, seg):
                    sp.wait_ge(split, c + 1)
                    sp.dma_start(w[:, s, :, :width],
                                 seg[0].rearrange("(k p) n -> p k n", p=P)[:, :, bass.ds(col, width)]).then_inc(w_ld[s], DMA)
                each(sp, body)

            @block.vector
            def _(dve):
                dve.sem_inc(split, 2)

                def body(c, s, r, col, width, seg):
                    dve.wait_ge(w_ld[s], (r + 1) * DMA)
                    dve.wait_ge(summed, G * c + G)
                    dve.tensor_copy(ws[:, s, 0, :, :width], w[:, s, :, :width]).then_inc(rounded, 1)
                    dve.wait_ge(rounded, c + 1)
                    dve.tensor_tensor(ws[:, s, 1, :, :width], w[:, s, :, :width], ws[:, s, 0, :, :width].bitcast(F32),
                                      ALU.subtract).then_inc(split, 1)
                each(dve, body)

            @block.tensor
            def _(pe):
                pe.sem_inc(summed, 2 * G)

                def body(c, s, r, col, width, seg):
                    pe.wait_ge(split, c + 3)
                    for g in range(G):
                        pe.wait_ge(moved, c * G + g + 1)
                        if seg[2]:
                            m, h = g // 2, g % 2
                            mm = split_product(pe, acc[:, g % B, :], lambda p, k: ws[:, s, p, k, m * P:(m + 1) * P],
                                               lambda p, k: XT[:, p, k, h * NC:(h + 1) * NC], range(KD))
                        else:
                            mm = split_product(pe, acc[:, g % B, :width], lambda p, k: XT[:, p, k, g * P:(g + 1) * P],
                                               lambda p, k: ws[:, s, p, k, :width], range(KD))
                        mm.then_inc(summed, 1)
                each(pe, body)

            @block.scalar
            def _(act):
                act.sem_inc(moved, B)

                def body(c, s, r, col, width, seg):
                    n = NC if seg[2] else width
                    for g in range(G):
                        act.wait_ge(summed, c * G + g + 1 + 2 * G)
                        act.wait_ge(staged, c * G + g + 1)
                        act.activation(stage[:, g % B, :n], acc[:, g % B, :n], seg[3]).then_inc(moved, 1)
                each(act, body)

            @block.gpsimd
            def _(pool):
                pool.sem_inc(staged, B)

                def body(c, s, r, col, width, seg):
                    n = NC if seg[2] else width
                    for g in range(G):
                        if seg[2]:
                            dst = seg[1][bass.ds(col + (g // 2) * P, P), (g % 2) * NC:(g % 2 + 1) * NC]
                        else:
                            dst = seg[1][g * P:(g + 1) * P, bass.ds(col, width)]
                        pool.wait_ge(moved, c * G + g + 1 + B)
                        pool.dma_start(dst, stage[:, g % B, :n]).then_inc(out_st, DMA)
                        pool.wait_ge(out_st, (c * G + g + 1) * DMA)
                        pool.sem_inc(staged, 1)
                each(pool, body)


def reduce_tokens(nc, tag, AT, W, res, out):
    K = W.shape[0]
    KP = K // (2 * P)
    Av = AT.rearrange("(i k p) t -> i p k t", p=P, k=2)
    Wv = W.rearrange("(i k p) n -> i p k n", p=P, k=2)
    last_from = 1 + (KP - 2) // 2 * 2

    with Place(nc, tag) as pl:
        a = pl.sb("a", [P, 2, 2, L])
        w = pl.sb("w", [P, 2, 2, NC])
        sa = pl.sb("sa", [P, 2, 2, 2, L], F32R)
        sw = pl.sb("sw", [P, 2, 2, 2, NC], F32R)
        y = pl.sb("y", [P, TT, D])
        acc = pl.ps("acc", [P, TT, NC])
        ld = [pl.sem(f"item_loaded{s}") for s in range(2)]
        res_ld = pl.store_sem("residual_loaded")
        rounded = pl.sem("item_rounded")
        split = pl.sem("item_split")
        used = pl.sem("item_used")
        summed = pl.sem("tile_summed")
        added = pl.sem("tile_added")
        out_st = pl.store_sem("out_stored")

        def items(eng, h, body):
            def call(k, turn, j):
                i = h * KP + (k if turn is None else 1 + j)
                s = i % 2
                if turn is None:
                    body(k, i, s, i // 2, k == 0, k == KP - 1)
                else:
                    body(1 + j + turn * 2, i + turn * 2, s, i // 2 + turn, False, False)
            call(0, None, 0)
            if last_from > 1:
                with eng.Fori(0, (last_from - 1) // 2) as r:
                    call(None, r, 0)
                    call(None, r, 1)
            for k in range(last_from, KP):
                call(k, None, 0)

        with nc.Block() as block:
            @block.sync
            def _(sp):
                for h in range(2):
                    def body(k, i, s, before, first, last):
                        sp.wait_ge(split, i + 1)
                        sp.dma_start(a[:, s, :, :], Av[bass.ds(k, 1)].rearrange("i p k t -> (i p) k t")).then_inc(ld[s], DMA)
                        sp.dma_start(w[:, s, :, :], Wv[bass.ds(k, 1), :, :, h * NC:(h + 1) * NC].rearrange(
                            "i p k n -> (i p) k n")).then_inc(ld[s], DMA)
                    items(sp, h, body)

            @block.tensor
            def _(pe):
                pe.sem_inc(used, 2)
                for h in range(2):
                    def body(k, i, s, before, first, last):
                        pe.wait_ge(split, i + 3)
                        for t in range(TT):
                            if first and h:
                                pe.wait_ge(added, t + 1)
                            mm = split_product(pe, acc[:, t, :], lambda p, k: sa[:, s, p, k, t * P:(t + 1) * P],
                                               lambda p, k: sw[:, s, p, k, :], range(2), start=first, stop=last)
                            if last:
                                mm.then_inc(summed, 1)
                        if not last:
                            mm.then_inc(used, 1)
                        elif not h:
                            pe.wait_ge(summed, TT)
                            pe.sem_inc(used, 1)
                    items(pe, h, body)

            @block.scalar
            def _(act):
                for h in range(2):
                    def body(k, i, s, before, first, last):
                        act.wait_ge(ld[s], (before + 1) * 2 * DMA)
                        act.wait_ge(used, i + 1)
                        act.activation(sa[:, s, 0, :, :], a[:, s, :, :], ACT.Copy)
                        act.activation(sw[:, s, 0, :, :], w[:, s, :, :], ACT.Copy).then_inc(rounded, 1)
                    items(act, h, body)

            @block.vector
            def _(dve):
                dve.sem_inc(split, 2)

                def body(k, i, s, before, first, last):
                    dve.wait_ge(rounded, i + 1)
                    dve.tensor_tensor(sa[:, s, 1, :, :], a[:, s, :, :], sa[:, s, 0, :, :].bitcast(F32), ALU.subtract)
                    dve.tensor_tensor(sw[:, s, 1, :, :], w[:, s, :, :], sw[:, s, 0, :, :].bitcast(F32),
                                      ALU.subtract).then_inc(split, 1)
                for h in range(2):
                    items(dve, h, body)
                    if h == 0:
                        dve.wait_ge(res_ld, DMA)
                    for t in range(TT):
                        dve.wait_ge(summed, h * TT + t + 1)
                        yt = y[:, t, h * NC:(h + 1) * NC]
                        dve.tensor_tensor(yt, acc[:, t, :], yt, ALU.add).then_inc(added, 1)

            @block.gpsimd
            def _(pool):
                pool.dma_start(y[:, :, :], res.rearrange("(t p) n -> p t n", p=P)).then_inc(res_ld, DMA)
                for h in range(2):
                    for t in range(TT):
                        pool.wait_ge(added, h * TT + t + 1)
                        pool.dma_start(out[t * P:(t + 1) * P, h * NC:(h + 1) * NC],
                                       y[:, t, h * NC:(h + 1) * NC]).then_inc(out_st, DMA)
                pool.wait_ge(out_st, 2 * TT * DMA)


def swiglu_up(nc, tag, XT, Wg, Wu, hT):
    F = Wg.shape[1]
    CW = 2 * P
    chunks, G = F // CW, 4
    Wgv = Wg.rearrange("(k p) n -> p k n", p=P)
    Wuv = Wu.rearrange("(k p) n -> p k n", p=P)
    with Place(nc, tag) as pl:
        w = pl.sb("w", [P, 2, 2, KD, CW])
        ws = pl.sb("ws", [P, 2, 2, 2, KD, CW], F32R)
        sil = pl.sb("sil", [P, 2, NC])
        h = pl.sb("h", [P, 2, NC])
        acc = pl.ps("acc", [P, 2, 2, NC])
        w_ld = [pl.sem(f"w_loaded{s}") for s in range(2)]
        rounded = pl.sem("w_rounded")
        passed = pl.sem("passed")
        split = pl.sem("w_split")
        summed = pl.sem("group_summed")
        silu_done = pl.sem("silu_done")
        gated = pl.sem("group_gated")
        out_st = pl.sem("out_stored")
        h_free = pl.sem("h_free")
        with nc.Block() as block:
            @block.sync
            def _(sp):
                def body(c, s, r):
                    sp.wait_ge(split, c + 1)
                    sp.dma_start(w[:, s, 0, :, :], Wgv[:, :, bass.ds(c * CW, CW)]).then_inc(w_ld[s], DMA)
                    sp.dma_start(w[:, s, 1, :, :], Wuv[:, :, bass.ds(c * CW, CW)]).then_inc(w_ld[s], DMA)
                pairs(sp, chunks, body)

            @block.tensor
            def _(pe):
                pe.sem_inc(summed, 2 * G)

                def body(c, s, r):
                    pe.wait_ge(split, c + 3)
                    for g in range(G):
                        m, half = g // 2, g % 2
                        pe.wait_ge(gated, c * G + g + 1)
                        for u in range(2):
                            mm = split_product(pe, acc[:, g % 2, u, :], lambda p, k: ws[:, s, p, u, k, m * P:(m + 1) * P],
                                               lambda p, k: XT[:, p, k, half * NC:(half + 1) * NC], range(KD))
                        mm.then_inc(summed, 1)
                pairs(pe, chunks, body)

            @block.scalar
            def _(act):
                act.sem_inc(h_free, 2)

                def body(c, s, r):
                    for g in range(G):
                        act.wait_ge(summed, c * G + g + 1 + 2 * G)
                        act.wait_ge(gated, c * G + g + 1)
                        act.activation(sil[:, g % 2, :], acc[:, g % 2, 0, :], ACT.Silu).then_inc(silu_done, 1)
                        act.wait_ge(gated, c * G + g + 3)
                        act.dma_start(hT[bass.ds(c * CW + (g // 2) * P, P), (g % 2) * NC:(g % 2 + 1) * NC],
                                      h[:, g % 2, :]).then_inc(out_st, DMA)
                        act.wait_ge(out_st, (c * G + g + 1) * DMA)
                        act.sem_inc(h_free, 1)
                pairs(act, chunks, body)

            @block.vector
            def _(dve):
                dve.sem_inc(gated, 2)

                def body(c, s, r):
                    for g in range(G):
                        dve.wait_ge(silu_done, c * G + g + 1)
                        dve.wait_ge(h_free, c * G + g + 1)
                        dve.tensor_tensor(h[:, g % 2, :], acc[:, g % 2, 1, :], sil[:, g % 2, :],
                                          ALU.mult).then_inc(gated, 1)
                pairs(dve, chunks, body)

            @block.gpsimd
            def _(pool):
                pool.sem_inc(split, 2)

                def body(c, s, r):
                    pool.wait_ge(w_ld[s], (r + 1) * 2 * DMA)
                    pool.wait_ge(summed, G * c + G)
                    pool.sem_inc(passed, 1)
                    pool.tensor_copy(ws[:, s, 0], w[:, s]).then_inc(rounded, 1)
                    pool.wait_ge(rounded, c + 1)
                    pool.tensor_tensor(ws[:, s, 1], w[:, s], ws[:, s, 0].bitcast(F32), ALU.subtract).then_inc(split, 1)
                pairs(pool, chunks, body)


def merge_branches(nc, tag, ysT, yaT, Ws, Wa, gT, mT):
    KS = 4
    G = 2 * KD
    with Place(nc, tag) as pl:
        w = pl.sb("w", [P, 2, KS, D])
        y = pl.sb("y", [P, 2, KS, L])
        g = pl.sb("g", [P, 2, 2, NC])
        part = pl.sb("part", [P, 2, 2, NC])
        m = pl.sb("m", [P, 2, NC])
        acc = pl.ps("acc", [P, 2, 2, NC])
        in_ld = pl.sem("inputs_loaded")
        g_ld = [pl.sem(f"gates_loaded{s}") for s in range(2)]
        summed = pl.sem("group_summed")
        gated = pl.sem("group_gated")
        merged = pl.sem("group_merged")
        out_st = [pl.sem(f"out_stored{s}") for s in range(2)]
        with nc.Block() as block:
            @block.sync
            def _(sp):
                for b, (Y, W) in enumerate(((ysT, Ws), (yaT, Wa))):
                    sp.dma_start(y[:, b, :, :], Y.rearrange("(k p) t -> p k t", p=P)).then_inc(in_ld, DMA)
                    sp.dma_start(w[:, b, :, :], W.rearrange("(k p) n -> p k n", p=P)).then_inc(in_ld, DMA)
                for i in range(G):
                    n, h, s = i // 2, i % 2, i % 2
                    sp.wait_ge(gated, i + 1)
                    for b in range(2):
                        sp.dma_start(g[:, s, b, :], gT[b * D + n * P:b * D + (n + 1) * P,
                                                       h * NC:(h + 1) * NC]).then_inc(g_ld[s], DMA)

            @block.tensor
            def _(pe):
                pe.wait_ge(in_ld, 4 * DMA)
                for i in range(G):
                    n, h, s = i // 2, i % 2, i % 2
                    pe.wait_ge(gated, i + 1)
                    for b in range(2):
                        for k in range(KS):
                            mm = pe.matmul(acc[:, s, b, :], w[:, b, k, n * P:(n + 1) * P],
                                           y[:, b, k, h * NC:(h + 1) * NC], start=k == 0, stop=k == KS - 1)
                    mm.then_inc(summed, 1)

            @block.vector
            def _(dve):
                dve.sem_inc(gated, 2)
                for i in range(G):
                    s = i % 2
                    dve.wait_ge(summed, i + 1)
                    dve.wait_ge(g_ld[s], (i // 2 + 1) * 2 * DMA)
                    dve.wait_ge(merged, i + 1)
                    dve.tensor_tensor(part[:, s, :, :], acc[:, s, :, :], g[:, s, :, :], ALU.mult).then_inc(gated, 1)

            @block.gpsimd
            def _(pool):
                pool.sem_inc(merged, 2)
                for i in range(G):
                    s = i % 2
                    pool.wait_ge(gated, i + 3)
                    if i >= 2:
                        pool.wait_ge(out_st[s], i // 2 * DMA)
                    pool.tensor_tensor(m[:, s, :], part[:, s, 0, :], part[:, s, 1, :], ALU.add).then_inc(merged, 1)

            @block.scalar
            def _(act):
                for i in range(G):
                    n, h, s = i // 2, i % 2, i % 2
                    act.wait_ge(merged, i + 3)
                    act.dma_start(mT[n * P:(n + 1) * P, h * NC:(h + 1) * NC], m[:, s, :]).then_inc(out_st[s], DMA)
                for s in range(2):
                    act.wait_ge(out_st[s], G // 2 * DMA)


S_GROUPS, S_CH, S_N = 32, 16, 64
S_J = S_GROUPS // 2
S_T = 8
S_C = L // S_T
S_W = S_GROUPS * S_CH


def s5_branch(nc, tag, p1, prm, ident, outT):
    with Place(nc, tag) as pl:
        uc = pl.sb("uc", [S_C, S_T, S_W])
        U = pl.sb("U", [P, S_GROUPS, S_C])
        MT = pl.sb("MT", [P, S_GROUPS, P])
        WT = pl.sb("WT", [P, 2, S_J, P])
        Wn = pl.sb("Wn", [P, 2, S_J, S_T, S_CH])
        CP = pl.sb("CP", [P, 2, S_J, S_T + 1, S_CH])
        cB = pl.sb("cB", [P, 2, S_J, S_CH])
        E = pl.sb("E", [P, 2, S_J, S_C])
        w = pl.sb("w", [P, 2, S_J, S_C])
        t1 = pl.sb("t1", [P, S_J * S_C])
        t2 = pl.sb("t2", [P, S_J * S_C])
        K16 = pl.sb("K16", [S_CH, S_GROUPS, P])
        small = pl.sb("small", [P, 40, S_J])
        PW = pl.sb("PW", [P, 2, S_T + 1, S_J])
        Bn = pl.sb("Bn", [P, 2, S_J, S_CH])
        Cn = pl.sb("Cn", [P, 2, S_J, S_CH])
        z = Wn[:, :, :, :, :].rearrange("p a j s q -> p a (j s q)")
        ug = w[:, :, :, :].rearrange("p a j c -> p (a j c)").rearrange("p (g s q) -> p g s q", s=S_T, q=S_CH)
        names = ["ar", "ai", "ldt", "dt", "x", "y", "k", "r", "h", "sn", "cs", "em1", "mag", "tmp", "tmp2",
                 "den", "nr", "cr", "ci", "v", "e", "m8", "ur", "ui", "vr", "vi", "n2"]
        at = {n: small[:, i, :] for i, n in enumerate(names)}

        loaded = pl.sem("loaded")
        pl_dve = pl.sem("dve")
        phase_in = pl.sem("phase_argument_ready")
        phase = pl.sem("phase_ready")
        powers = pl.sem("powers_ready")
        pl_pool = pl.sem("pool")
        regrouped = pl.sem("u_regrouped")

        def cmul(eng, ln, o, a, b, shape, neg=False, at0=0):
            n = int(np.prod(shape[1:]))
            pat = {2: None, 3: "p (a b) -> p a b"}[len(shape)]
            u, v = t1[:, at0:at0 + n], t2[:, at0:at0 + n]
            if pat:
                u, v = (q.rearrange(pat, b=shape[2]) for q in (u, v))
            ln.mark(eng.tensor_tensor(u, a[0], b[0], ALU.mult))
            ln(eng.tensor_tensor(v, a[1], b[1], ALU.mult))
            ln(eng.tensor_tensor(o[0], u, v, ALU.subtract))
            ln.mark(eng.tensor_tensor(u, a[0], b[1], ALU.mult))
            ln(eng.tensor_tensor(v, a[1], b[0], ALU.mult))
            if neg:
                ln(eng.scalar_tensor_tensor(o[1], u, -1.0, v, ALU.mult, ALU.subtract))
            else:
                ln(eng.tensor_tensor(o[1], u, v, ALU.add))

        def pw(k):
            return PW[:, 0, k, :], PW[:, 1, k, :]

        def wide(q):
            return q.unsqueeze(2).to_broadcast([P, S_J, S_CH])
        shape = (P, S_J, S_CH)

        with nc.Block() as block:
            @block.sync
            def _(sp):
                def slow(dst, src):
                    sp.dma_start(dst, src, allow_slow_non_contiguous=True).then_inc(loaded, DMA)
                for n, a in (("ar", prm["A_re"]), ("ai", prm["A_im"])):
                    slow(at[n], a.rearrange("j q -> q j"))
                for q in range(2):
                    slow(at["ldt"][q * S_N:(q + 1) * S_N, :],
                         prm["log_dt"].rearrange("(j q) -> q j", q=2)[q, :].partition_broadcast(S_N))
                for i, n in enumerate(("B_re", "B_im")):
                    sp.dma_start(Bn[:, i, :, :], prm[n].rearrange("j q c -> q j c")).then_inc(loaded, DMA)
                for i, n in enumerate(("C_re", "C_im")):
                    sp.dma_start(Cn[:, i, :, :], prm[n].rearrange("j q c -> q j c")).then_inc(loaded, DMA)
                sp.dma_start(uc[:, :, :], p1[:, 0:S_W].rearrange("(c s) f -> c s f", s=S_T)).then_inc(loaded, DMA)

            @block.vector
            def _(dve):
                link = Link(dve, pl_dve)
                dve.wait_ge(loaded, 9 * DMA)

                def tt(o, a, b, op=ALU.mult):
                    link(dve.tensor_tensor(at[o], at[a], at[b], op))

                def ts(o, a, m, b=0.0):
                    link(dve.tensor_scalar(at[o], at[a], m, b, ALU.mult, ALU.add))

                def expm1_of(o, a, doublings):
                    ts("v", a, 1.0 / 256)
                    ts(o, "v", 1.0 / 120, 1.0 / 24)
                    for q in (1.0 / 6, 0.5, 1.0):
                        tt(o, o, "v")
                        ts(o, o, 1.0, q)
                    tt(o, o, "v")
                    for _ in range(doublings):
                        link(dve.scalar_tensor_tensor(at[o], at[o], 2.0, at[o], ALU.add, ALU.mult))

                def square(o, a):
                    tt(o, a, a)

                expm1_of("e", "ldt", 5)
                ts("dt", "e", 1.0, 1.0)
                for _ in range(3):
                    square("dt", "dt")
                tt("x", "ar", "dt")
                tt("y", "ai", "dt")
                ts("k", "y", 1.0 / (2 * np.pi), 12582912.0)
                ts("k", "k", 1.0, -12582912.0)
                c1 = 6.28125
                c2 = float(np.float32(np.round((2 * np.pi - c1) * 2 ** 21) / 2 ** 21))
                c3 = 2 * np.pi - c1 - c2
                link(dve.scalar_tensor_tensor(at["r"], at["k"], -c1, at["y"], ALU.mult, ALU.add))
                link(dve.scalar_tensor_tensor(at["r"], at["k"], -c2, at["r"], ALU.mult, ALU.add))
                link(dve.scalar_tensor_tensor(at["r"], at["k"], -c3, at["r"], ALU.mult, ALU.add))
                link(dve.tensor_scalar(at["r"], at["r"], 3.1415925, -3.1415925, ALU.min, ALU.max))
                link(dve.scalar_tensor_tensor(at["h"], at["r"], -1.0, at["r"], ALU.mult, ALU.max))
                dve.tensor_scalar(at["h"], at["h"], -1.0, np.pi / 2, ALU.mult, ALU.add).then_inc(phase_in, 1)
                expm1_of("em1", "x", 8)
                expm1_of("e", "x", 5)
                ts("mag", "e", 1.0, 1.0)
                for _ in range(3):
                    square("mag", "mag")
                square("m8", "mag")
                square("m8", "m8")
                square("m8", "m8")
                dve.wait_ge(phase, 2)
                square("n2", "cs")
                square("tmp", "sn")
                tt("n2", "n2", "tmp", ALU.add)
                ts("n2", "n2", -0.5, 1.5)
                tt("cs", "cs", "n2")
                tt("sn", "sn", "n2")
                link(dve.memset(PW[:, 0, 0, :], 1.0))
                link(dve.memset(PW[:, 1, 0, :], 0.0))
                link(dve.tensor_tensor(PW[:, 0, 1, :], at["mag"], at["cs"], ALU.mult))
                link(dve.tensor_tensor(PW[:, 1, 1, :], at["mag"], at["sn"], ALU.mult))
                ts("tmp", "cs", 1.0, -1.0)
                tt("nr", "em1", "cs")
                tt("nr", "nr", "tmp", ALU.add)
                square("den", "ar")
                square("tmp", "ai")
                tt("den", "den", "tmp", ALU.add)
                link(dve.reciprocal(at["den"], at["den"]))
                abi = PW[:, 1, 1, :]
                tt("cr", "nr", "ar")
                link(dve.tensor_tensor(at["tmp"], abi, at["ai"], ALU.mult))
                tt("cr", "cr", "tmp", ALU.add)
                tt("cr", "cr", "den")
                link(dve.tensor_tensor(at["ci"], abi, at["ar"], ALU.mult))
                tt("tmp", "nr", "ai")
                tt("ci", "ci", "tmp", ALU.subtract)
                tt("ci", "ci", "den")

                for n in (1, 2, 4):
                    f = [q.unsqueeze(1).to_broadcast([P, n, S_J]) for q in pw(n)]
                    cmul(dve, link, (PW[:, 0, n + 1:2 * n + 1, :], PW[:, 1, n + 1:2 * n + 1, :]),
                         (PW[:, 0, 1:n + 1, :], PW[:, 1, 1:n + 1, :]), f, (P, n, S_J))

                cmul(dve, link, (cB[:, 0, :, :], cB[:, 1, :, :]), (Bn[:, 0, :, :], Bn[:, 1, :, :]),
                     (wide(at["cr"]), wide(at["ci"])), shape)
                dve.sem_inc(powers, 1)
                for k in range(S_T + 1):
                    cmul(dve, link, (CP[:, 0, :, k, :], CP[:, 1, :, k, :]), (Cn[:, 0, :, :], Cn[:, 1, :, :]),
                         [wide(q) for q in pw(k)], shape, neg=True)
                u_, v_ = ("cs", "sn"), ("vr", "vi")
                for _ in range(3):
                    cmul(dve, link, (at[v_[0]], at[v_[1]]), (at[u_[0]], at[u_[1]]), (at[u_[0]], at[u_[1]]), (P, S_J))
                    u_, v_ = v_, (("ur", "ui") if v_[0] == "vr" else ("vr", "vi"))
                link(dve.memset(E[:, 0, :, 0:1], 1.0))
                link(dve.memset(E[:, 1, :, 0:1], 0.0))
                n = 1
                while n < S_C:
                    f = [at[q].unsqueeze(2).to_broadcast([P, S_J, n]) for q in u_]
                    cmul(dve, link, (E[:, 0, :, n:2 * n], E[:, 1, :, n:2 * n]), (E[:, 0, :, 0:n], E[:, 1, :, 0:n]), f,
                         (P, S_J, n))
                    n *= 2
                    if n < S_C:
                        cmul(dve, link, (at[v_[0]], at[v_[1]]), (at[u_[0]], at[u_[1]]), (at[u_[0]], at[u_[1]]),
                             (P, S_J))
                        u_, v_ = v_, u_

            @block.scalar
            def _(act):
                act.wait_ge(phase_in, 1)
                act.activation(at["sn"], at["r"], ACT.Sin).then_inc(phase, 1)
                act.activation(at["cs"], at["h"], ACT.Sin).then_inc(phase, 1)
                act.wait_ge(loaded, 9 * DMA)
                for s in range(S_T):
                    act.activation(ug[:, :, s, :], uc[:, s, :].rearrange("c (g q) -> c g q", q=S_CH),
                                   ACT.Copy).then_inc(regrouped, 1)
                act.wait_ge(regrouped, S_T)

            @block.gpsimd
            def _(pool):
                link = Link(pool, pl_pool)
                link(pool.memset(MT[:, :, :], 0.0))
                pool.wait_ge(powers, 1)
                for s in range(S_T):
                    cmul(pool, link, (Wn[:, 0, :, s, :], Wn[:, 1, :, s, :]), (cB[:, 0, :, :], cB[:, 1, :, :]),
                         [wide(q) for q in pw(S_T - 1 - s)], shape, at0=S_J * S_C // 2)

        made = pl.sem("group_made")
        moved = pl.sem("group_moved")
        shifted = pl.sem("kernels_shifted")
        acc = pl.ps("acc", [P, 8, 4, P])
        groups = [("U", i) for i in range(8)] + [("W", i) for i in range(8)] + [("K", i) for i in range(8)]
        with nc.Block() as block:
            @block.tensor
            def _(pe):
                for n, (kind, i) in enumerate(groups):
                    b = n % 4
                    if n >= 4:
                        pe.wait_ge(moved, n - 3)
                    for q in range(4):
                        if kind == "U":
                            g = 4 * i + q
                            mm = pe.transpose(acc[:, b, q, :], ug[:, g, :, :].rearrange("c s q -> c (s q)"), ident[:, :])
                        elif kind == "W":
                            c, j = i // 4, (i % 4) * 4 + q
                            mm = pe.transpose(acc[:, b, q, :], Wn[:, c, j, :, :].rearrange("p s q -> p (s q)"), ident[:, :])
                        else:
                            j, a = 4 * (i // 2) + q, i % 2
                            rows = slice(a * S_N, (a + 1) * S_N)
                            for c in range(2):
                                mm = pe.matmul(acc[0:S_CH, b, q, :], cB[rows, c, j, :], CP[rows, c, j, 0:S_T, :],
                                               start=c == 0, stop=c == 1)
                    mm.then_inc(made, 1)

            @block.scalar
            def _(act):
                for n, (kind, i) in enumerate(groups):
                    b = n % 4
                    act.wait_ge(made, n + 1)
                    if kind == "U":
                        dst, src = U[:, 4 * i:4 * i + 4, :], acc[:, b, :, :]
                    elif kind == "W":
                        j = (i % 4) * 4
                        dst, src = WT[:, i // 4, j:j + 4, :], acc[:, b, :, :]
                    else:
                        g = 8 * (i // 2) + i % 2
                        dst, src = K16[:, g:g + 7:2, :], acc[0:S_CH, b, :, :]
                    act.activation(dst, src, ACT.Copy).then_inc(moved, 1)

            @block.sync
            def _(sp):
                sp.wait_ge(moved, len(groups))
                for s in range(S_T):
                    sp.dma_start(MT[s * S_CH:(s + 1) * S_CH, :, s * S_CH:P],
                                 K16[:, :, 0:P - s * S_CH]).then_inc(shifted, DMA)
                sp.wait_ge(shifted, S_T * DMA)

        win = pl.sem("inputs_summed")
        w_mv = pl.sem("inputs_moved")
        d2 = pl.sem("dve_scan")
        d_ld = pl.sem("D_loaded")
        skip = pl.sem("skip_ready")
        dsk = pl.sb("dsk", [P, S_W])
        with nc.Block() as block:
            @block.sync
            def _(sp):
                sp.dma_start(dsk[:, :], prm["D_skip"].partition_broadcast(P)).then_inc(d_ld, DMA)

            @block.gpsimd
            def _(pool):
                pool.wait_ge(d_ld, DMA)
                pool.tensor_tensor(uc[:, :, :], uc[:, :, :], dsk[:, :].unsqueeze(1).to_broadcast([P, S_T, S_W]),
                                   ALU.mult).then_inc(skip, 1)
                pool.wait_ge(skip, 1)

            @block.tensor
            def _(pe):
                for n in range(8):
                    c, i = n // 4, n % 4
                    for q in range(4):
                        j = 4 * i + q
                        for a in range(2):
                            rows = slice(a * S_N, (a + 1) * S_N)
                            mm = pe.matmul(acc[rows, n, q, :], WT[:, c, j, rows], U[:, 2 * j + a, :],
                                           start=True, stop=True, skip_group_check=True)
                    mm.then_inc(win, 1)

            @block.scalar
            def _(act):
                for n in range(8):
                    act.wait_ge(win, n + 1)
                    i = n % 4
                    act.activation(w[:, n // 4, 4 * i:4 * i + 4, :], acc[:, n, :, :], ACT.Copy).then_inc(w_mv, 1)

            @block.vector
            def _(dve):
                link = Link(dve, d2)
                dve.wait_ge(w_mv, 8)
                wr, wi = w[:, 0, :, :], w[:, 1, :, :]
                er, ei = E[:, 0, :, :], E[:, 1, :, :]
                a3 = [q[:, :].rearrange("p (j c) -> p j c", c=S_C) for q in (t1, t2)]
                z3 = [z[:, q, :].rearrange("p (j c) -> p j c", c=S_C) for q in range(2)]
                link.mark(dve.tensor_tensor(a3[0], wr, er, ALU.mult))
                link(dve.tensor_tensor(a3[1], wi, ei, ALU.mult))
                link(dve.tensor_tensor(z3[0], a3[0], a3[1], ALU.add))
                link.mark(dve.tensor_tensor(a3[0], wi, er, ALU.mult))
                link(dve.tensor_tensor(a3[1], wr, ei, ALU.mult))
                link(dve.tensor_tensor(z3[1], a3[0], a3[1], ALU.subtract))
                link(dve.tensor_scalar(a3[0], er, 0.0, None, ALU.mult))
                link(dve.tensor_tensor(a3[0], a3[0], at["m8"].unsqueeze(2).to_broadcast([P, S_J, S_C]), ALU.add))
                link(dve.memset(a3[0][:, :, 0:1], 0.0))
                for q in range(2):
                    link(dve.tensor_tensor_scan(z[:, q, :], t1[:, :], z[:, q, :], 0.0, ALU.mult, ALU.add))
                n = S_C - 1
                zr, zi = z3[0][:, :, 0:n], z3[1][:, :, 0:n]
                er, ei = E[:, 0, :, 0:n], E[:, 1, :, 0:n]
                x1, x2 = a3[0][:, :, 0:n], a3[1][:, :, 0:n]
                link(dve.memset(w[:, :, :, 0:1], 0.0))
                link.mark(dve.tensor_tensor(x1, zr, er, ALU.mult))
                link(dve.tensor_tensor(x2, zi, ei, ALU.mult))
                link(dve.tensor_tensor(w[:, 0, :, 1:S_C], x1, x2, ALU.subtract))
                link.mark(dve.tensor_tensor(x1, zr, ei, ALU.mult))
                link(dve.tensor_tensor(x2, zi, er, ALU.mult))
                link(dve.tensor_tensor(w[:, 1, :, 1:S_C], x1, x2, ALU.add))

        yT = pl.sb("yT", [P, 4, L])
        wg = pl.sb("wg", [P, 4, S_W])
        bg = pl.sb("bg", [P, 4])
        sig = pl.sb("sig", [P, 2, NC])
        y_sum = pl.sem("outputs_summed")
        y_add = pl.sem("outputs_added")
        y_act = pl.sem("gelu_done")
        y_tr = pl.sem("y_transposed")
        y_mv = pl.sem("y_moved")
        glu_ld = pl.sem("glu_loaded")
        glu = pl.sem("glu_summed")
        sigd = pl.sem("sigmoid_done")
        gated = pl.sem("gated")
        out_st = pl.store_sem("out_stored")
        with nc.Block() as block:
            @block.sync
            def _(sp):
                sp.dma_start(wg[:, :, :], prm["w_glu"].rearrange("(k p) n -> p k n", p=P)).then_inc(glu_ld, DMA)
                sp.dma_start(bg[:, :], prm["b_glu"].rearrange("(k p) -> p k", p=P),
                             allow_slow_non_contiguous=True).then_inc(glu_ld, DMA)

            @block.tensor
            def _(pe):
                for n in range(8):
                    for q in range(4):
                        j = 4 * (n // 2) + q
                        g, rows = 2 * j + n % 2, slice((n % 2) * S_N, (n % 2 + 1) * S_N)
                        pe.matmul(acc[:, n, q, :], U[:, g, :], MT[:, g, :], start=True, stop=False)
                        pe.matmul(acc[:, n, q, :], w[rows, 0, j, :], CP[rows, 0, j, 1:S_T + 1, :], start=False, stop=False)
                        mm = pe.matmul(acc[:, n, q, :], w[rows, 1, j, :], CP[rows, 1, j, 1:S_T + 1, :],
                                       start=False, stop=True)
                    mm.then_inc(y_sum, 1)
                pe.wait_ge(y_act, 8)
                for s in range(S_T):
                    pe.wait_ge(y_add, s + 1)
                    for f in range(4):
                        mm = pe.transpose(acc[:, s, f, :], uc[:, s, f * P:(f + 1) * P], ident[:, :])
                    mm.then_inc(y_tr, 1)
                pe.wait_ge(y_mv, S_T)
                pe.wait_ge(glu_ld, 2 * DMA)
                for i in range(8):
                    n, h = i // 2, i % 2
                    for k in range(4):
                        mm = pe.matmul(acc[:, i, :, :].rearrange("p a b -> p (a b)"), wg[:, k, n * P:(n + 1) * P],
                                       yT[:, k, h * NC:(h + 1) * NC], start=k == 0, stop=k == 3)
                    mm.then_inc(glu, 1)

            @block.vector
            def _(dve):
                for n in range(8):
                    dve.wait_ge(y_sum, n + 1)
                    h = 2 * P // 2
                    yv = uc[:, :, (n // 2) * h:(n // 2 + 1) * h].rearrange("c s (j a q) -> c a j s q", a=2, q=S_CH)[:, n % 2]
                    dve.tensor_tensor(yv, acc[:, n, :, :].rearrange("c g (s q) -> c g s q", q=S_CH), yv,
                                      ALU.add).then_inc(y_add, 1)
                for s in range(S_T):
                    dve.wait_ge(y_tr, s + 1)
                    dve.tensor_copy(yT[:, :, :].rearrange("p f (c s) -> p f c s", s=S_T)[:, :, :, s],
                                    acc[:, s, :, :]).then_inc(y_mv, 1)
                for i in range(8):
                    n, h = i // 2, i % 2
                    dve.wait_ge(sigd, i + 1)
                    dve.wait_ge(glu, 8)
                    yv = yT[:, n, h * NC:(h + 1) * NC]
                    dve.tensor_tensor(yv, yv, sig[:, i % 2, :], ALU.mult).then_inc(gated, 1)

            @block.scalar
            def _(act):
                act.wait_ge(y_add, 8)
                for s in range(S_T):
                    act.activation(uc[:, s, :], uc[:, s, :], ACT.Gelu_apprx_tanh).then_inc(y_act, 1)
                act.wait_ge(glu_ld, 2 * DMA)
                for i in range(8):
                    act.wait_ge(glu, i + 1)
                    if i >= 2:
                        act.wait_ge(gated, i - 1)
                    act.activation(sig[:, i % 2, :], acc[:, i, :, :].rearrange("p a b -> p (a b)"), ACT.Sigmoid,
                                   bias=bg[:, i // 2:i // 2 + 1]).then_inc(sigd, 1)

            @block.gpsimd
            def _(pool):
                for i in range(8):
                    n, h = i // 2, i % 2
                    pool.wait_ge(gated, i + 1)
                    pool.dma_start(outT[n * P:(n + 1) * P, h * NC:(h + 1) * NC],
                                   yT[:, n, h * NC:(h + 1) * NC]).then_inc(out_st, DMA)
                pool.wait_ge(out_st, 8 * DMA)


A_H, A_D = 8, 64
I_H = 4
TOPK = 256
Q0, K0, V0, QI0, KI0, WI0 = 512, 1024, 1088, 1152, 1408, 1472
GONE = -3e38
UNSEEN = -1e37


def mask_at(qb):
    return P * (qb * (qb + 1) // 2)


def sparse_prepare(nc, tag, p1, gains, F, V, wi, ident):
    R = WI0 + I_H - Q0
    NH = A_H + 2
    with Place(nc, tag) as pl:
        row = pl.sb("row", [P, 2, R])
        xs = pl.sb("xs", [P, 2, 8, P])
        sq = pl.sb("sq", [P, 2, NH, A_D])
        st = pl.sb("st", [P, 2, 4, NH])
        gc = pl.sb("gc", [P, 8])
        pT = pl.ps("pT", [P, 2, 8, P])
        ld = [pl.sem(f"rows_loaded{s}") for s in range(2)]
        g_ld = pl.sem("gains_loaded")
        ones = pl.sem("ones_ready")
        squared = pl.sem("squared")
        mean = pl.sem("mean_ready")
        root = pl.sem("root_ready")
        copied = pl.sem("raw_columns_copied")
        inv = pl.sem("inverse_ready")
        scaled = pl.sem("rows_scaled")
        turned = pl.sem("rows_transposed")
        stored = pl.sem("features_stored")
        chain = pl.sem("dve")
        with nc.Block() as block:
            @block.sync
            def _(sp):
                sp.wait_ge(ones, 1)
                for c0, n, g in ((0, 4, gains[0]), (4, 1, gains[1]), (7, 1, gains[2])):
                    for q in range(2):
                        for c in range(c0, c0 + n):
                            sp.dma_start(gc[q * A_D:(q + 1) * A_D, c:c + 1], g.rearrange("(d o) -> d o", o=1),
                                         allow_slow_non_contiguous=True).then_inc(g_ld, DMA)

                def body(t, s, r):
                    sp.wait_ge(scaled, t + 1)
                    sp.dma_start(row[:, s, :], p1[bass.ds(t * P, P), Q0:Q0 + R]).then_inc(ld[s], DMA)
                pairs(sp, TT, body)

            @block.gpsimd
            def _(pool):
                pool.memset(gc[:, :], 1.0).then_inc(ones, 1)

                def body(t, s, r):
                    pool.wait_ge(ld[s], (r + 1) * DMA)
                    pool.wait_ge(mean, t + 1)
                    for q0, n, c in ((0, A_H, 0), (A_H, 1, K0 - Q0), (A_H + 1, 1, KI0 - Q0)):
                        v = row[:, s, c:c + n * A_D].rearrange("p (h d) -> p h d", d=A_D)
                        last = pool.tensor_tensor(sq[:, s, q0:q0 + n, :], v, v, ALU.mult)
                    last.then_inc(squared, 1)
                pairs(pool, TT, body)

            @block.scalar
            def _(act):
                def body(t, s, r):
                    act.wait_ge(ld[s], (r + 1) * DMA)
                    act.wait_ge(turned, t + 1)
                    act.activation(xs[:, s, 5:7, :], row[:, s, QI0 - Q0:KI0 - Q0].rearrange("p (a b) -> p a b", b=P),
                                   ACT.Copy)
                    act.activation(V[:, bass.ds(t, 1), :], row[:, s, V0 - Q0:QI0 - Q0].unsqueeze(1), ACT.Copy)
                    act.activation(wi[:, bass.ds(t, 1), :], row[:, s, WI0 - Q0:R].unsqueeze(1), ACT.Copy,
                                   scale=I_H ** -0.5 * A_D ** -0.5).then_inc(copied, 1)
                    act.wait_ge(mean, t + 3)
                    act.activation(st[:, s, 2, :], st[:, s, 1, :], ACT.Sqrt).then_inc(root, 1)
                pairs(act, TT, body)

            @block.vector
            def _(dve):
                dve.sem_inc(scaled, 2)
                dve.sem_inc(stored, 2)
                dve.sem_inc(mean, 2)
                dve.wait_ge(g_ld, 12 * DMA)
                link = Link(dve, chain)

                def body(t, s, r):
                    if s == 0:
                        link.turn(r, 2)
                    dve.wait_ge(squared, t + 1)
                    link(dve.tensor_reduce(st[:, s, 0, :], sq[:, s, :, :], AX.X, ALU.add))
                    dve.tensor_scalar(st[:, s, 1, :], st[:, s, 0, :], 1.0 / A_D, EPS, ALU.mult, ALU.add).then_inc(mean, 1)
                    dve.wait_ge(root, t + 1)
                    dve.reciprocal(st[:, s, 3, :], st[:, s, 2, :]).then_inc(inv, 1)
                    dve.wait_ge(inv, t + 1)
                    dve.wait_ge(turned, t + 1)
                    dve.wait_ge(copied, t + 1)
                    for q0, n, c, o in ((0, A_H, 0, 0), (A_H, 1, K0 - Q0, 4), (A_H, 1, K0 - Q0, 4.5),
                                        (A_H + 1, 1, KI0 - Q0, 7), (A_H + 1, 1, KI0 - Q0, 7.5)):
                        dst = xs[:, s, :, :].rearrange("p a b -> p (a b)")[:, int(o * P):int(o * P) + n * A_D]
                        last = dve.tensor_tensor(dst.rearrange("p (h d) -> p h d", d=A_D),
                                                 row[:, s, c:c + n * A_D].rearrange("p (h d) -> p h d", d=A_D),
                                                 st[:, s, 3, q0:q0 + n].unsqueeze(2).to_broadcast([P, n, A_D]), ALU.mult)
                    last.then_inc(scaled, 1)
                    dve.wait_ge(turned, t + 3)
                    dve.tensor_tensor(F[:, :, bass.ds(t * P, P)], pT[:, s, :, :],
                                      gc[:, :].unsqueeze(2).to_broadcast([P, 8, P]), ALU.mult).then_inc(stored, 1)
                    if s == 1:
                        link.end(TT // 2)
                pairs(dve, TT, body)

            @block.tensor
            def _(pe):
                pe.sem_inc(turned, 2)

                def body(t, s, r):
                    pe.wait_ge(scaled, t + 3)
                    pe.wait_ge(stored, t + 1)
                    for k in range(8):
                        last = pe.transpose(pT[:, s, k, :], xs[:, s, k, :], ident[:, :])
                    last.then_inc(turned, 1)
                pairs(pe, TT, body)


def masks_and_gates(nc, tag, F, wi, M, XT, Wg, gT):
    FIRST = TOPK // P
    CW, G, B = 2 * P, 4, 4
    chunks = Wg.shape[1] // CW
    blocks = list(range(FIRST, TT))
    NB = len(blocks)
    def chunk_run(c0, c1):
        return [("gates", c) for c in range(c0, c1)]
    assert NB == 6 and chunks == 8
    order = ([("scores", 0), ("scores", 1), ("scores", 2)] + chunk_run(0, 3) + [("scores", 3), ("scores", 4)]
             + chunk_run(3, 7) + [("scores", 5)] + chunk_run(7, 8))
    Wv = Wg.rearrange("(k p) n -> p k n", p=P)
    with Place(nc, tag) as pl:
        rel = pl.sb("rel", [P, I_H, L])
        score = pl.sb("score", [P, 2, L])
        work = pl.sb("work", [P, 2, L])
        top = pl.sb("top", [P, 2, 8])
        w = pl.sb("w", [P, 2, KD, CW])
        ws = pl.sb("ws", [P, 2, 2, KD, CW], F32R)
        stage = pl.sb("stage", [P, B, NC])
        acc = pl.ps("acc", [P, 2, 2, NC])
        g_acc = pl.ps("g_acc", [P, B, NC])
        ready = pl.sem("product_ready")
        relu = pl.sem("relu_done")
        used = pl.sem("relu_used")
        scored = pl.sem("block_scored")
        hid = pl.sem("unseen_hidden")
        found = pl.sem("block_masked")
        chain = [pl.sem(f"search{u}") for u in range(2)]
        passed = pl.sem("passed")
        passed_sp = pl.sem("passed_sync")
        zeroed = pl.sem("zeroed")
        causal = pl.sem("causal_made")
        w_ld = [pl.sem(f"w_loaded{s}") for s in range(2)]
        rounded = pl.sem("w_rounded")
        split = pl.sem("w_split")
        summed = pl.sem("group_summed")
        moved = pl.sem("group_moved")
        staged = pl.sem("stage_free")
        out_st = pl.sem("out_stored")

        def in_turn(score_of, gates_of):
            for what, i in order:
                if what == "scores":
                    score_of(i)
                else:
                    gates_of(i, i % 2)

        with nc.Block() as block:
            @block.sync
            def _(sp):
                def load(c, s):
                    sp.dma_start(w[:, s, :, :], Wv[:, :, bass.ds(c * CW, CW)]).then_inc(w_ld[s], DMA)

                def store(c):
                    for g in range(G):
                        sp.wait_ge(moved, c * G + g + 1 + B)
                        sp.sem_inc(passed_sp, 1)
                        sp.dma_start(gT[bass.ds(c * CW + (g // 2) * P, P), (g % 2) * NC:(g % 2 + 1) * NC],
                                     stage[:, g % B, :]).then_inc(out_st, DMA)
                        sp.wait_ge(out_st, (c * G + g + 1) * DMA)
                        sp.sem_inc(staged, 1)
                sp.sem_inc(staged, B)
                load(0, 0)
                load(1, 1)

                def body(c, s, r):
                    sp.wait_ge(split, c + 1)
                    sp.sem_inc(passed_sp, 1)
                    load(c + 2, s)
                    store(c)
                pairs(sp, chunks - 2, body)
                store(chunks - 2)
                store(chunks - 1)

            @block.tensor
            def _(pe):
                pe.sem_inc(summed, 2 * G)

                def score_of(b):
                    qb = blocks[b]
                    for h in range(I_H):
                        rows, s, i = slice((h % 2) * A_D, (h % 2 + 1) * A_D), h % 2, b * I_H + h
                        if i >= 2:
                            pe.wait_ge(relu, i - 1)
                        for c in range(0, (qb + 1) * P, NC):
                            n = min(NC, (qb + 1) * P - c)
                            mm = pe.matmul(acc[:, s, c // NC, 0:n], F[rows, 5 + h // 2, qb * P:(qb + 1) * P],
                                           F[rows, 7, c:c + n], start=True, stop=True)
                        mm.then_inc(ready, 1)

                def gates_of(c, s):
                    pe.wait_ge(split, c + 1)
                    for g in range(G):
                        m, h = g // 2, g % 2
                        pe.wait_ge(moved, c * G + g + 1)
                        split_product(pe, g_acc[:, g, :], lambda p, k: ws[:, s, p, k, m * P:(m + 1) * P],
                                      lambda p, k: XT[:, p, k, h * NC:(h + 1) * NC], range(KD)).then_inc(summed, 1)
                in_turn(score_of, gates_of)

            @block.scalar
            def _(act):
                act.sem_inc(moved, B)

                def score_of(b):
                    w = (blocks[b] + 1) * P
                    for h in range(I_H):
                        act.wait_ge(ready, b * I_H + h + 1)
                        if b:
                            act.wait_ge(used, (b - 1) * I_H + h + 1)
                        act.activation(rel[:, h, 0:w], acc[:, h % 2, :, :].rearrange("p a b -> p (a b)")[:, 0:w],
                                       ACT.Relu).then_inc(relu, 1)

                def gates_of(c, s):
                    for g in range(G):
                        act.wait_ge(summed, c * G + g + 1 + 2 * G)
                        act.wait_ge(staged, c * G + g + 1)
                        act.activation(stage[:, g, :], g_acc[:, g, :], ACT.Sigmoid).then_inc(moved, 1)
                in_turn(score_of, gates_of)

            @block.vector
            def _(dve):
                def score_block(b):
                    qb = blocks[b]
                    w = (qb + 1) * P
                    for h in range(I_H):
                        dve.wait_ge(relu, b * I_H + h + 1)
                        out, one = score[:, b % 2, 0:w], wi[:, qb, h:h + 1]
                        if h == 0:
                            ins = dve.tensor_scalar(out, rel[:, 0, 0:w], one, None, ALU.mult)
                        else:
                            dve.wait_ge(used, b * I_H + h)
                            ins = dve.scalar_tensor_tensor(out, rel[:, h, 0:w], one, out, ALU.mult, ALU.add)
                        ins.then_inc(used, 1)
                    dve.wait_ge(used, (b + 1) * I_H)
                    dve.sem_inc(scored, 1)

                links = [Link(dve, c) for c in chain]
                turns = TOPK // 8 - 1
                for b0 in range(0, NB, 2):
                    score_block(b0)
                    score_block(b0 + 1)
                    two = []
                    for u in range(2):
                        w = (blocks[b0 + u] + 1) * P
                        at = mask_at(blocks[b0 + u])
                        two.append((links[u], score[:, u, 0:w], work[:, u, 0:w], top[:, u, :], M[:, at:at + w]))
                    dve.wait_ge(hid, b0 + 2)
                    for link, sc, wk, tp, m in two:
                        link.mark(dve.max(tp, sc))
                    for link, sc, wk, tp, m in two:
                        link.wait()
                        link.mark(dve.match_replace(wk, tp, sc, GONE))
                    with dve.Fori(0, turns) as r:
                        for link, sc, wk, tp, m in two:
                            link.turn(r, 2)
                            link.wait()
                            dve.sem_inc(passed, 1)
                            link.mark(dve.max(tp, wk))
                        for link, sc, wk, tp, m in two:
                            link.wait()
                            dve.sem_inc(passed, 1)
                            link.mark(dve.match_replace(wk, tp, wk, GONE))
                    for link, sc, wk, tp, m in two:
                        link.end(turns)
                        link.wait()
                        link.mark(dve.tensor_tensor(m, wk, sc, ALU.is_equal))
                    for link, sc, wk, tp, m in two:
                        link.wait()
                        dve.tensor_scalar(m, m, -HUGE, None, ALU.mult).then_inc(found, 1)

            @block.gpsimd
            def _(pool):
                def split_chunk(c):
                    s = c % 2
                    pool.wait_ge(w_ld[s], (c // 2 + 1) * DMA)
                    if c >= 2:
                        pool.wait_ge(summed, G * c + G)
                    pool.tensor_copy(ws[:, s, 0], w[:, s]).then_inc(rounded, 1)
                    pool.wait_ge(rounded, c + 1)
                    pool.tensor_tensor(ws[:, s, 1], w[:, s], ws[:, s, 0].bitcast(F32), ALU.subtract).then_inc(split, 1)

                def hide(b):
                    qb = blocks[b]
                    pool.wait_ge(scored, b + 1)
                    d = score[:, b % 2, qb * P:(qb + 1) * P]
                    pool.affine_select(out=d, in_=d, compare_op=ALU.is_ge, fill=UNSEEN, base=0, pattern=[[-1, P]],
                                       channel_multiplier=1).then_inc(hid, 1)

                n = mask_at(FIRST)
                pool.memset(M[:, 0:n], 0.0).then_inc(zeroed, 1)
                pool.wait_ge(zeroed, 1)
                for qb in range(FIRST):
                    m = M[:, mask_at(qb) + qb * P:mask_at(qb) + (qb + 1) * P]
                    pool.affine_select(out=m, in_=m, compare_op=ALU.is_ge, fill=-HUGE, base=0, pattern=[[-1, P]],
                                       channel_multiplier=1).then_inc(causal, 1)
                hide(0)
                hide(1)
                for c in range(4):
                    split_chunk(c)
                hide(2)
                hide(3)
                for c in range(4, chunks):
                    split_chunk(c)
                hide(4)
                hide(5)
                pool.wait_ge(causal, FIRST)


def sparse_attend(nc, tag, F, V, M, ident, yT):
    PAIRS = A_H // 2
    N = 2 * TT
    with Place(nc, tag) as pl:
        raw = pl.sb("raw", [P, 2, L])
        X = pl.sb("X", [P, 2, 2, L], F32R)
        K = pl.sb("K", [P, 2, L], F32R)
        S = pl.sb("S", [P, 4, L])
        E = pl.sb("E", [P, 2, L])
        ET = pl.sb("ET", [P, 4, TT, P])
        mx = pl.sb("mx", [P, 4, 4])
        o = pl.sb("o", [P, 2, P])
        yo = pl.sb("yo", [P, L])
        pS = pl.ps("pS", [P, 2, 2, NC])
        pE = pl.ps("pE", [P, TT, P])
        pO = pl.ps("pO", [P, 2, NC])
        raw_ld = pl.sem("queries_loaded")
        k_hi = pl.sem("hi_of_keys")
        k_split = pl.sem("keys_split")
        x_hi = pl.sem("hi_of_queries")
        x_lo = pl.sem("lo_of_queries")
        x_split = pl.sem("queries_split")
        passed = pl.sem("passed")
        passed_sp = pl.sem("passed_sync")
        dots = pl.sem("logits_ready")
        masked = pl.sem("logits_masked")
        neg = pl.sem("negated")
        expd = pl.sem("exp_done")
        turned = pl.sem("exp_transposed")
        moved = pl.sem("exp_moved")
        summed = pl.sem("values_summed")
        inv = pl.sem("inverse_ready")
        normed = pl.sem("output_normed")
        o_tr = pl.sem("output_transposed")
        o_mv = pl.sem("output_moved")
        yo_free = pl.sem("yo_free")
        out_st = pl.store_sem("out_stored")
        with nc.Block() as block:
            @block.sync
            def _(sp):
                def body(h, s, r):
                    sp.wait_ge(x_split, h + 1)
                    sp.sem_inc(passed_sp, 1)
                    for rows in (slice(0, A_D), slice(A_D, P)):
                        for a in range(2):
                            sp.dma_start(raw[rows, a:a + 1, :], F[a * A_D:(a + 1) * A_D, bass.ds(h, 1), :]).then_inc(raw_ld, DMA)
                pairs(sp, PAIRS, body)

            @block.gpsimd
            def _(pool):
                pool.sem_inc(yo_free, 1)
                pool.sem_inc(x_split, 1)
                pool.wait_ge(k_hi, 1)
                pool.tensor_tensor(K[:, 1, :], F[:, 4, :], K[:, 0, :].bitcast(F32), ALU.subtract).then_inc(k_split, 1)
                pool.wait_ge(k_split, 1)

                def subtract(h, s):
                    pool.wait_ge(x_hi, h + 1)
                    pool.tensor_tensor(X[A_D:P, s, :, :], raw[A_D:P, :, :], X[A_D:P, s, :, :].bitcast(F32),
                                       ALU.subtract).then_inc(x_lo, 1)
                    pool.wait_ge(x_lo, h + 1)
                    pool.sem_inc(x_split, 1)

                def body(h, s, r):
                    subtract(h, s)
                    pool.wait_ge(o_mv, (h + 1) * TT + 1)
                    pool.dma_start(yT[bass.ds(h * P, P), :], yo[:, :]).then_inc(out_st, DMA)
                    pool.wait_ge(out_st, (h + 1) * DMA)
                    pool.sem_inc(yo_free, 1)
                pairs(pool, PAIRS, body)

            @block.tensor
            def _(pe):
                pe.sem_inc(turned, 2)
                pe.sem_inc(summed, 4)
                pe.sem_inc(o_tr, 2)
                pe.wait_ge(k_split, 1)

                def body(h, s, r):
                    def logits(i):
                        n, qb, a = h * N + i, i // 2, i % 2
                        pe.wait_ge(masked, n + 1)
                        for c in range(0, (qb + 1) * P, NC):
                            k = min(NC, (qb + 1) * P - c)
                            for part in range(2):
                                mm = pe.matmul(pS[:, a, c // NC, 0:k], X[:, s, a, qb * P:(qb + 1) * P], K[:, part, c:c + k],
                                               start=part == 0, stop=part == 1)
                        mm.then_inc(dots, 1)

                    def turn(i):
                        n, qb, a = h * N + i, i // 2, i % 2
                        pe.wait_ge(expd, n + 5)
                        pe.wait_ge(moved, n + 1)
                        for c in range(qb + 1):
                            mm = pe.transpose(pE[:, c, :], E[:, a, c * P:(c + 1) * P], ident[:, :])
                        mm.then_inc(turned, 1)

                    def values(i):
                        n, qb, a = h * N + i, i // 2, i % 2
                        pe.wait_ge(moved, n + 2)
                        pe.wait_ge(normed, n + 3)
                        if a == 1:
                            pe.wait_ge(o_mv, h * TT + qb + 1)
                        for c in range(qb + 1):
                            mm = pe.matmul(pO[:, a, 0:A_D], ET[:, i % 4, c, :], V[:, c, :], start=c == 0, stop=c == qb)
                        mm.then_inc(summed, 1)

                    def turn_output(qb):
                        pe.wait_ge(normed, h * N + 2 * qb + 6)
                        pe.transpose(pO[:, 1, P:2 * P], o[:, qb % 2, :], ident[:, :]).then_inc(o_tr, 1)

                    pe.wait_ge(x_split, h + 2)
                    logits(0)
                    logits(1)
                    for i in range(N + 2):
                        if i + 2 < N:
                            logits(i + 2)
                        if i >= 2:
                            values(i - 2)
                        if i % 2 == 0 and i >= 4:
                            turn_output((i - 4) // 2)
                        if i < N:
                            turn(i)
                    turn_output(TT - 1)
                pairs(pe, PAIRS, body)

            @block.vector
            def _(dve):
                dve.sem_inc(masked, 2)
                dve.sem_inc(normed, 4)
                dve.sem_inc(o_mv, 1)

                def body(h, s, r):
                    def mask(i):
                        n, qb, a = h * N + i, i // 2, i % 2
                        w, v = (qb + 1) * P, mx[:, i % 4, :]
                        dve.wait_ge(dots, n + 1)
                        dve.wait_ge(expd, n + 1)
                        dve.sem_inc(passed, 1)
                        dve.tensor_tensor_reduce(S[:, i % 4, 0:w], pS[:, a, :, :].rearrange("p a b -> p (a b)")[:, 0:w],
                                                 M[:, mask_at(qb):mask_at(qb) + w], A_D ** -0.5, GONE, ALU.add, ALU.max,
                                                 v[:, 0:1]).then_inc(masked, 1)
                        dve.wait_ge(masked, n + 3)
                        dve.tensor_scalar(v[:, 1:2], v[:, 0:1], -1.0, None, ALU.mult).then_inc(neg, 1)

                    def norm(i):
                        n, qb, a = h * N + i, i // 2, i % 2
                        v = mx[:, i % 4, :]
                        dve.wait_ge(expd, n + 5)
                        dve.reciprocal(v[:, 3:4], v[:, 2:3]).then_inc(inv, 1)
                        dve.wait_ge(inv, n + 1)
                        dve.wait_ge(summed, n + 5)
                        dve.wait_ge(o_tr, h * TT + qb + 1)
                        dve.tensor_scalar(o[:, qb % 2, a * A_D:(a + 1) * A_D], pO[:, a, 0:A_D], v[:, 3:4], None,
                                          ALU.mult).then_inc(normed, 1)

                    def move_output(qb):
                        dve.wait_ge(o_tr, h * TT + qb + 3)
                        if qb == 0:
                            dve.wait_ge(yo_free, h + 1)
                        dve.tensor_copy(yo[:, qb * P:(qb + 1) * P], pO[:, 1, P:2 * P]).then_inc(o_mv, 1)

                    mask(0)
                    for i in range(N + 2):
                        if i + 1 < N:
                            mask(i + 1)
                        if i >= 2:
                            norm(i - 2)
                        if i % 2 == 0 and i >= 4:
                            move_output((i - 4) // 2)
                    move_output(TT - 1)
                pairs(dve, PAIRS, body)

            @block.scalar
            def _(act):
                act.sem_inc(expd, 4)
                act.sem_inc(moved, 1)
                act.activation(K[:, 0, :], F[:, 4, :], ACT.Copy).then_inc(k_hi, 1)

                def round_queries(h, s):
                    act.wait_ge(raw_ld, (h + 1) * 4 * DMA)
                    act.activation(X[:, s, :, :], raw[:, :, :], ACT.Copy).then_inc(x_hi, 1)

                def body(h, s, r):
                    def exps(i):
                        n, qb, a = h * N + i, i // 2, i % 2
                        w = (qb + 1) * P
                        act.wait_ge(neg, n + 1)
                        act.wait_ge(turned, n + 1)
                        act.wait_ge(normed, n + 1)
                        act.activation(E[:, a, 0:w], S[:, i % 4, 0:w], ACT.Exp, bias=mx[:, i % 4, 1:2],
                                       accum_out=mx[:, i % 4, 2:3]).then_inc(expd, 1)

                    def move(i):
                        n, qb, a = h * N + i, i // 2, i % 2
                        act.wait_ge(turned, n + 3)
                        act.wait_ge(summed, n + 1)
                        act.activation(ET[:, i % 4, 0:qb + 1, :], pE[:, 0:qb + 1, :], ACT.Copy).then_inc(moved, 1)

                    round_queries(h, s)
                    exps(0)
                    for i in range(N):
                        if i + 1 < N:
                            exps(i + 1)
                        move(i)
                pairs(act, PAIRS, body)


CONV = 4
H2, P2, G2, N2 = 16, 64, 4, 128
X2 = H2 * P2
XB2 = X2 + G2 * N2


def conv_silu(nc, tag, tile0, tiles, xbcT, cw, cb, ident, featT, tok):
    with Place(nc, tag) as pl:
        x = pl.sb("x", [P, 2, CONV - 1 + L])
        y = pl.sb("y", [P, 2, L])
        f = pl.sb("f", [P, 2, L])
        t = pl.sb("t", [P, 2, TT, P])
        w = pl.sb("w", [P, tiles, CONV])
        b = pl.sb("b", [P, tiles])
        pT = pl.ps("pT", [P, 2, TT, P])
        w_ld = pl.sem("weights_loaded")
        ld = [pl.sem(f"x_loaded{s}") for s in range(2)]
        conved = pl.sem("conv_done")
        chain = pl.sem("dve")
        pad = pl.sem("padded")
        act_d = pl.sem("silu_done")
        turned = pl.sem("transposed")
        moved = pl.sem("moved")
        out_st = pl.sem("out_stored")
        free = pl.sem("outputs_free")
        passed_sp = pl.sem("passed_sync")
        copies = 1 + (featT is not None)
        with nc.Block() as block:
            @block.sync
            def _(sp):
                rows = slice(tile0 * P, (tile0 + tiles) * P)
                for k in range(CONV):
                    sp.dma_start(w[:, :, k], cw[k, rows].rearrange("(c p) -> p c", p=P),
                                 allow_slow_non_contiguous=True).then_inc(w_ld, DMA)
                sp.dma_start(b[:, :], cb[rows].rearrange("(c p) -> p c", p=P),
                             allow_slow_non_contiguous=True).then_inc(w_ld, DMA)

                sp.sem_inc(free, 2)

                def load(c, s):
                    sp.dma_start(x[:, s, CONV - 1:], xbcT[bass.ds((tile0 + c) * P, P), :]).then_inc(ld[s], DMA)

                def store(c, s):
                    if featT is not None:
                        sp.wait_ge(act_d, c + 3)
                        sp.sem_inc(passed_sp, 1)
                        sp.dma_start(featT[bass.ds(c * P, P), :], f[:, s, :]).then_inc(out_st, DMA)
                    sp.wait_ge(moved, c + 3)
                    sp.sem_inc(passed_sp, 1)
                    sp.dma_start(tok[:, bass.ds((tile0 + c) * P, P)].rearrange("(k p) n -> p k n", p=P),
                                 t[:, s, :, :]).then_inc(out_st, DMA)
                    sp.wait_ge(out_st, (c + 1) * copies * DMA)
                    sp.sem_inc(free, 1)

                load(0, 0)
                load(1, 1)

                def body(c, s, r):
                    sp.wait_ge(conved, c + 3)
                    sp.sem_inc(passed_sp, 1)
                    load(c + 2, s)
                    store(c, s)
                pairs(sp, tiles - 2, body)
                store(tiles - 2, 0)
                store(tiles - 1, 1)

            @block.vector
            def _(dve):
                dve.sem_inc(conved, 2)
                dve.memset(x[:, :, 0:CONV - 1], 0.0).then_inc(pad, 1)
                dve.wait_ge(pad, 1)
                dve.wait_ge(w_ld, (CONV + 1) * DMA)
                link = Link(dve, chain)

                def body(c, s, r):
                    if s == 0:
                        link.turn(r, 2 * (CONV - 1))
                    dve.wait_ge(ld[s], (r + 1) * DMA)
                    dve.wait_ge(act_d, c + 1)
                    link(dve.tensor_scalar(y[:, s, :], x[:, s, 0:L], w[:, bass.ds(c, 1), 0], b[:, bass.ds(c, 1)],
                                           ALU.mult, ALU.add))
                    for k in range(1, CONV):
                        ins = dve.scalar_tensor_tensor(y[:, s, :], x[:, s, k:k + L], w[:, bass.ds(c, 1), k], y[:, s, :],
                                                       ALU.mult, ALU.add)
                        if k < CONV - 1:
                            link(ins)
                        else:
                            ins.then_inc(conved, 1)
                    if s == 1:
                        link.end(tiles // 2)
                pairs(dve, tiles, body)

            @block.scalar
            def _(act):
                act.sem_inc(act_d, 2)
                act.sem_inc(moved, 2)

                def body(c, s, r):
                    act.wait_ge(conved, c + 3)
                    act.wait_ge(turned, c + 1)
                    act.wait_ge(free, c + 1)
                    act.activation(f[:, s, :], y[:, s, :], ACT.Silu).then_inc(act_d, 1)
                    act.wait_ge(turned, c + 3)
                    act.activation(t[:, s, :, :], pT[:, s, :, :], ACT.Copy).then_inc(moved, 1)
                pairs(act, tiles, body)

            @block.tensor
            def _(pe):
                pe.sem_inc(turned, 2)

                def body(c, s, r):
                    pe.wait_ge(act_d, c + 3)
                    pe.wait_ge(moved, c + 1)
                    for k in range(TT):
                        mm = pe.transpose(pT[:, s, k, :], f[:, s, k * P:(k + 1) * P], ident[:, :])
                    mm.then_inc(turned, 1)
                pairs(pe, tiles, body)


def ssd_mixer(nc, tag, dt, xbt, bcT, z, prm, ident, yT):
    NCH = TT
    KINDS = 6
    DT, EA, DS, EL, NA, A0 = range(KINDS)
    with Place(nc, tag) as pl:
        tri = pl.sb("tri", [P, P])
        neg = pl.sb("neg", [P, P])
        ones = pl.sb("ones", [P, P])
        pr = pl.sb("pr", [P, KINDS, NCH, H2])
        v = pl.sb("v", [P, 3, NCH, H2])
        hd = pl.sb("hd", [P, 4, H2])
        nw = pl.sb("nw", [P, KD])
        ps0 = pl.ps("ps0", [P, 2, NCH * H2])
        loaded = pl.sem("loaded")
        made = pl.sem("masks_made")
        s_act = pl.sem("act")
        chain = pl.sem("dve")
        sums = pl.sem("sums")
        a_in = pl.sem("a_ready")
        pre = pl.sem("argument_ready")
        post = pl.sem("exponentials_ready")
        v2 = [v[:, i, :, :].rearrange("p c h -> p (c h)") for i in range(3)]
        p2 = [pr[:, i, :, :].rearrange("p c h -> p (c h)") for i in range(KINDS)]
        with nc.Block() as block:
            @block.sync
            def _(sp):
                sp.dma_start(pr[:, DT, :, :], dt.rearrange("(c p) h -> p c h", p=P)).then_inc(loaded, DMA)
                for i, n in ((0, "dt_bias"), (1, "A_log"), (3, "D")):
                    sp.dma_start(hd[:, i, :], prm[n].partition_broadcast(P)).then_inc(loaded, DMA)
                sp.dma_start(nw[:, :], prm["norm_w"].rearrange("(k p) -> p k", p=P),
                             allow_slow_non_contiguous=True).then_inc(loaded, DMA)
                sp.wait_ge(loaded, 5 * DMA)

            @block.gpsimd
            def _(pool):
                pool.memset(tri[:, :], 1.0).then_inc(made, 1)
                pool.memset(neg[:, :], 0.0).then_inc(made, 1)
                pool.memset(ones[:, :], 1.0).then_inc(made, 1)
                pool.wait_ge(made, 3)
                for t, fill in ((tri, 0.0), (neg, -HUGE)):
                    pool.affine_select(out=t[:, :], in_=t[:, :], compare_op=ALU.is_ge, fill=fill, base=0,
                                       pattern=[[1, P]], channel_multiplier=-1).then_inc(made, 1)
                pool.wait_ge(made, 5)

            @block.vector
            def _(dve):
                link = Link(dve, chain)
                dve.wait_ge(loaded, 5 * DMA)
                link(dve.tensor_tensor(v[:, 0, :, :], pr[:, DT, :, :], hd[:, 0, :].unsqueeze(1).to_broadcast([P, NCH, H2]),
                                       ALU.add))
                link(dve.scalar_tensor_tensor(v2[1], v2[0], -1.0, v2[0], ALU.mult, ALU.max))
                dve.tensor_scalar(v2[2], v2[0], 0.0, None, ALU.max).then_inc(pre, 1)
                dve.wait_ge(post, 3)
                link(dve.tensor_tensor(p2[DT], v2[0], v2[2], ALU.add))
                link(dve.tensor_scalar(hd[:, 2, :], hd[:, 2, :], -1.0, None, ALU.mult))
                dve.tensor_tensor(pr[:, A0, :, :], pr[:, DT, :, :], hd[:, 2, :].unsqueeze(1).to_broadcast([P, NCH, H2]),
                                  ALU.mult).then_inc(a_in, 1)
                dve.wait_ge(sums, 2)
                dve.wait_ge(post, 5)
                link(dve.tensor_scalar(p2[NA], v2[0], -1.0, None, ALU.mult))
                dve.tensor_tensor(v2[2], v2[1], v2[0], ALU.subtract).then_inc(pre, 1)

            @block.scalar
            def _(act):
                act.wait_ge(loaded, 5 * DMA)
                act.activation(hd[:, 2, :], hd[:, 1, :], ACT.Exp).then_inc(post, 1)
                act.wait_ge(pre, 1)
                act.activation(v2[1], v2[1], ACT.Exp, scale=-1.0).then_inc(post, 1)
                act.wait_ge(post, 2)
                act.activation(v2[0], v2[1], ACT.Ln, bias=1.0).then_inc(post, 1)
                act.wait_ge(sums, 2)
                act.activation(v2[0], ps0[:, 0, :], ACT.Copy).then_inc(post, 1)
                act.activation(v2[1], ps0[:, 1, :], ACT.Copy).then_inc(post, 1)
                act.activation(p2[EA], ps0[:, 0, :], ACT.Exp)
                act.activation(p2[EL], ps0[:, 1, :], ACT.Exp)
                act.wait_ge(pre, 2)
                act.activation(p2[DS], v2[2], ACT.Exp).then_inc(s_act, 1)
                act.wait_ge(s_act, 1)

            @block.tensor
            def _(pe):
                pe.wait_ge(made, 5)
                pe.wait_ge(a_in, 1)
                pe.matmul(ps0[:, 0, :], tri[:, :], p2[A0], start=True, stop=True, skip_group_check=True).then_inc(sums, 1)
                pe.matmul(ps0[:, 1, :], ones[:, :], p2[A0], start=True, stop=True, skip_group_check=True).then_inc(sums, 1)

        X = pl.sb("X", [P, 2, X2 + G2 * N2])
        BC = pl.sb("BC", [P, 2, 2 * G2, P])
        Z = pl.sb("Z", [P, 2, X2])
        cp = pl.sb("cp", [P, 2, KINDS, H2])
        TA = pl.sb("TA", [P, H2, P])
        R = pl.sb("R", [P, 2, 4, P])
        LT = pl.sb("LT", [P, 2, 4, P])
        SC = pl.sb("SC", [P, H2, P])
        Xd = pl.sb("Xd", [P, X2])
        Xs = pl.sb("Xs", [P, X2])
        XD = pl.sb("XD", [P, X2])
        Y = pl.sb("Y", [P, X2])
        SQ = pl.sb("SQ", [P, X2])
        ST = pl.sb("ST", [P, X2])
        YT = pl.sb("YT", [P, KD, P])
        sm = pl.sb("sm", [P, 4])
        pCB = pl.ps("pCB", [P, G2, P])
        pR = pl.ps("pR", [P, 2, 4, P])
        pYd = pl.ps("pYd", [P, H2, P2])
        pYo = pl.ps("pYo", [P, X2])
        ld = [pl.sem(f"chunk_loaded{s}") for s in range(2)]
        cop = pl.sem("values_copied")
        ta = pl.sem("triangle_ready")
        xd = pl.sem("dt_x_ready")
        xs = pl.sem("decayed_x_ready")
        y1 = pl.sem("skip_added")
        cbS = pl.sem("CB_ready")
        rS = pl.sem("sums_ready")
        msk = pl.sem("sums_masked")
        lt = pl.sem("decay_ready")
        sc = pl.sem("scores_ready")
        yo = pl.sem("off_diagonal_ready")
        yd = pl.sem("diagonal_ready")
        yt = pl.sem("outputs_added")
        ns = pl.sem("new_state_ready")
        stt = pl.sem("state_ready")
        y2 = pl.sem("gated")
        sq = pl.sem("squares_summed")
        mn = pl.sem("mean_ready")
        rt = pl.sem("root_ready")
        iv = pl.sem("inverse_ready")
        yn = pl.sem("normed")
        tr = pl.sem("transposed")
        ev = pl.sem("features_moved")
        out_st = pl.sem("out_stored")
        passed_sp = pl.sem("passed_sync")
        yt_free = pl.sem("YT_free")
        chain2 = pl.sem("dve2")

        def bc64(a):
            return a.unsqueeze(2).to_broadcast([P, H2, P2])

        def heads(a):
            return a.rearrange("p (h q) -> p h q", q=P2)
        with nc.Block() as block:
            @block.sync
            def _(sp):
                sp.sem_inc(yt_free, 1)

                def load(c, s):
                    sp.dma_start(X[:, s, :], xbt[bass.ds(c * P, P), 0:XB2]).then_inc(ld[s], DMA)
                    sp.dma_start(BC[:, s, :, :], bcT[:, bass.ds(c * P, P)].rearrange("(g n) l -> n g l", n=P)
                                 ).then_inc(ld[s], DMA)
                    sp.dma_start(Z[:, s, :], z[bass.ds(c * P, P), :]).then_inc(ld[s], DMA)

                def store(c):
                    sp.wait_ge(ev, 2 * c + 3)
                    sp.sem_inc(passed_sp, 1)
                    sp.dma_start(yT[:, bass.ds(c * P, P)].rearrange("(k p) l -> p k l", p=P), YT[:, :, :]
                                 ).then_inc(out_st, DMA)
                    sp.wait_ge(out_st, (c + 1) * DMA)
                    sp.sem_inc(yt_free, 1)

                load(0, 0)
                load(1, 1)

                def body(c, s, r):
                    sp.wait_ge(tr, 2 * c + 6)
                    sp.sem_inc(passed_sp, 1)
                    load(c + 2, s)
                    store(c)
                pairs(sp, NCH - 2, body)
                store(NCH - 2)
                store(NCH - 1)

            @block.gpsimd
            def _(pool):
                def body(c, s, r):
                    pool.wait_ge(tr, 2 * c + 2)
                    pool.tensor_copy(cp[:, s, :, :].unsqueeze(2), pr[:, :, bass.ds(c, 1), :]).then_inc(cop, 1)
                    pool.wait_ge(cop, c + 1)
                    if s == 1:
                        pool.wait_ge(rS, 4 * c)
                    else:
                        pool.wait_ge(yt, c + 1)
                    pool.tensor_tensor(TA[:, :, :], tri[:, :].unsqueeze(1).to_broadcast([P, H2, P]),
                                       cp[:, s, A0, :].unsqueeze(2).to_broadcast([P, H2, P]), ALU.mult).then_inc(ta, 1)
                    pool.wait_ge(ld[s], (r + 1) * 3 * DMA)
                    pool.wait_ge(yd, c + 1)
                    pool.tensor_tensor(heads(Xd[:, :]), heads(X[:, s, 0:X2]), bc64(cp[:, s, DT, :]), ALU.mult).then_inc(xd, 1)
                    pool.wait_ge(xd, c + 1)
                    pool.wait_ge(ns, c + 1)
                    pool.tensor_tensor(heads(Xs[:, :]), heads(Xd[:, :]), bc64(cp[:, s, DS, :]), ALU.mult).then_inc(xs, 1)
                    pool.tensor_tensor(heads(XD[:, :]), heads(X[:, s, 0:X2]), bc64(hd[:, 3, :]), ALU.mult).then_inc(xs, 1)
                    pool.wait_ge(xs, 2 * c + 2)
                    pool.wait_ge(yt, c + 2)
                    pool.tensor_tensor(Y[:, :], Y[:, :], XD[:, :], ALU.add).then_inc(y1, 1)
                pairs(pool, NCH, body)

            @block.tensor
            def _(pe):
                pe.sem_inc(yd, 1)
                pe.sem_inc(ns, 1)
                pe.sem_inc(tr, 4)

                def body(c, s, r):
                    pe.wait_ge(ld[s], (r + 1) * 3 * DMA)
                    pe.wait_ge(yt, c + 1)
                    for g in range(G2):
                        mm = pe.matmul(pCB[:, g, :], BC[:, s, g, :], BC[:, s, G2 + g, :], start=True, stop=True,
                                       skip_group_check=True)
                    mm.then_inc(cbS, 1)
                    pe.wait_ge(ta, c + 1)
                    pe.wait_ge(ev, 2 * c + 1)
                    for i in range(G2):
                        pe.wait_ge(msk, 4 * c + i + 1)
                        pe.matmul(pR[:, i % 2, :, :], ones[:, :], TA[:, 4 * i:4 * i + 4, :], start=True,
                                  stop=True).then_inc(rS, 1)
                    pe.wait_ge(stt, c + 1)
                    for g in range(G2):
                        mm = pe.matmul(pYo[:, g * 256:(g + 1) * 256], BC[:, s, G2 + g, :], ST[:, g * 256:(g + 1) * 256],
                                       start=True, stop=True, skip_group_check=True)
                    mm.then_inc(yo, 1)
                    pe.wait_ge(xd, c + 1)
                    for h in range(H2):
                        if h % 4 == 0:
                            pe.wait_ge(sc, 4 * c + h // 4 + 3)
                        mm = pe.matmul(pYd[:, h, :], SC[:, h, :], Xd[:, h * P2:(h + 1) * P2], start=True, stop=True,
                                       skip_group_check=True)
                    mm.then_inc(yd, 1)
                    pe.wait_ge(xs, 2 * c + 2)
                    pe.wait_ge(yt, c + 2)
                    for g in range(G2):
                        mm = pe.matmul(pYo[:, g * 256:(g + 1) * 256], X[:, s, X2 + g * P:X2 + (g + 1) * P],
                                       Xs[:, g * 256:(g + 1) * 256], start=True, stop=True, skip_group_check=True)
                    mm.then_inc(ns, 1)
                    pe.wait_ge(yn, c + 1)
                    for h in range(2):
                        for k in range(4):
                            kk = 4 * h + k
                            mm = pe.transpose(pR[:, h, k, :], Y[:, kk * P:(kk + 1) * P], ident[:, :])
                        mm.then_inc(tr, 1)
                pairs(pe, NCH, body)

            @block.scalar
            def _(act):
                act.sem_inc(lt, 2)

                def body(c, s, r):
                    for i in range(G2):
                        act.wait_ge(msk, 4 * c + i + 3)
                        act.wait_ge(sc, 4 * c + i + 1)
                        for h in range(4):
                            e = act.activation(LT[:, i % 2, h, :], R[:, i % 2, h, :], ACT.Exp,
                                               bias=cp[:, s, NA, 4 * i + h:4 * i + h + 1])
                        e.then_inc(lt, 1)
                    act.wait_ge(y2, c + 1)
                    act.activation(SQ[:, :], Y[:, :], ACT.Square, accum_out=sm[:, 0:1]).then_inc(sq, 1)
                    act.wait_ge(mn, c + 1)
                    act.activation(sm[:, 2:3], sm[:, 1:2], ACT.Sqrt).then_inc(rt, 1)
                pairs(act, NCH, body)

            @block.vector
            def _(dve):
                dve.sem_inc(msk, 2)
                dve.sem_inc(sc, 2)
                dve.sem_inc(ev, 1)
                dve.sem_inc(yt, 1)
                link = Link(dve, chain2)
                link(dve.memset(ST[:, :], 0.0))
                dve.sem_inc(stt, 1)

                def body(c, s, r):
                    if s == 0:
                        link.turn(r, 4)

                    def mask(i):
                        dve.wait_ge(rS, 4 * c + i + 1)
                        dve.wait_ge(lt, 4 * c + i + 1)
                        dve.tensor_tensor(R[:, i % 2, :, :], pR[:, i % 2, :, :],
                                          neg[:, :].unsqueeze(1).to_broadcast([P, 4, P]), ALU.add).then_inc(msk, 1)
                    mask(0)
                    dve.wait_ge(cbS, c + 1)
                    dve.wait_ge(yd, c + 1)
                    for i in range(G2):
                        if i + 1 < G2:
                            mask(i + 1)
                        dve.wait_ge(lt, 4 * c + i + 3)
                        dve.tensor_tensor(SC[:, 4 * i:4 * i + 4, :], LT[:, i % 2, :, :],
                                          pCB[:, i, :].unsqueeze(1).to_broadcast([P, 4, P]), ALU.mult).then_inc(sc, 1)
                    dve.wait_ge(yo, c + 1)
                    dve.wait_ge(tr, 2 * c + 4)
                    link(dve.tensor_tensor(heads(Y[:, :]), heads(pYo[:, :]), bc64(cp[:, s, EA, :]), ALU.mult))
                    dve.wait_ge(yd, c + 2)
                    dve.tensor_tensor(heads(Y[:, :]), heads(Y[:, :]), pYd[:, :, :], ALU.add).then_inc(yt, 1)
                    link(dve.tensor_tensor(heads(ST[:, :]), heads(ST[:, :]), bc64(cp[:, s, EL, :]), ALU.mult))
                    dve.wait_ge(y1, c + 1)
                    dve.tensor_tensor(Y[:, :], Y[:, :], Z[:, s, :], ALU.mult).then_inc(y2, 1)
                    dve.wait_ge(ns, c + 2)
                    dve.tensor_tensor(ST[:, :], ST[:, :], pYo[:, :], ALU.add).then_inc(stt, 1)
                    dve.wait_ge(sq, c + 1)
                    dve.tensor_scalar(sm[:, 1:2], sm[:, 0:1], 1.0 / X2, EPS, ALU.mult, ALU.add).then_inc(mn, 1)
                    dve.wait_ge(rt, c + 1)
                    dve.reciprocal(sm[:, 3:4], sm[:, 2:3]).then_inc(iv, 1)
                    dve.wait_ge(iv, c + 1)
                    dve.tensor_scalar(Y[:, :], Y[:, :], sm[:, 3:4], None, ALU.mult).then_inc(yn, 1)
                    dve.wait_ge(yt_free, c + 1)
                    for h in range(2):
                        dve.wait_ge(tr, 2 * c + h + 5)
                        dve.tensor_tensor(YT[:, 4 * h:4 * h + 4, :], pR[:, h, :, :],
                                          nw[:, 4 * h:4 * h + 4].unsqueeze(2).to_broadcast([P, 4, P]),
                                          ALU.mult).then_inc(ev, 1)
                    if s == 1:
                        link.end(NCH // 2)
                pairs(dve, NCH, body)


D_H, D_QK, D_V = 8, 64, 128
BUCKETS, MAX_DIST = 32, 128
LAM_INIT = 0.2
NEAR = 2 * P
SKEW = 3 * P


def bucket_one_hot():
    rel = 2 * P - 1 - np.arange(SKEW)
    n = np.maximum(rel, 0)
    exact = BUCKETS // 2
    large = exact + (np.log(np.maximum(n, 1).astype(np.float32) / exact) / np.log(MAX_DIST / exact)
                     * (BUCKETS - exact)).astype(np.int32)
    bucket = np.where(n < exact, n, np.minimum(large, BUCKETS - 1))
    bucket = np.where(rel < 0, BUCKETS, bucket)
    return (bucket[None, :] == np.arange(BUCKETS + 1)[:, None]).astype(np.float32)


def diff_bias(nc, tag, rel_bias, one_hot, skew, near, far, lam, lam_src):
    with Place(nc, tag) as pl:
        tab = pl.sb("tab", [BUCKETS + 1, D_H])
        wide = pl.sb("wide", [BUCKETS + 1, D_H, P])
        oh = pl.sb("oh", [BUCKETS + 1, SKEW])
        rows = pl.sb("rows", [P, D_H, SKEW])
        lv = pl.sb("lv", [P, 4, D_QK])
        lp = pl.sb("lp", [P, 2, D_QK])
        ls = pl.sb("ls", [P, 4])
        acc = pl.ps("acc", [P, 2, NC])
        loaded = pl.sem("loaded")
        hidden = pl.sem("last_row_set")
        chain = pl.sem("dve")
        wided = pl.sem("table_widened")
        ready = pl.sem("row_ready")
        moved = pl.sem("row_moved")
        skewed = pl.sem("rows_stored")
        near_ld = pl.sem("near_loaded")
        dot = pl.sem("dots_ready")
        expd = pl.sem("exps_ready")
        with nc.Block() as block:
            @block.sync
            def _(sp):
                sp.dma_start(tab[0:BUCKETS, :], rel_bias).then_inc(loaded, DMA)
                sp.dma_start(oh[:, :], one_hot).then_inc(loaded, DMA)
                for i, v in enumerate(lam_src):
                    sp.dma_start(lv[:, i, :], v.partition_broadcast(P)).then_inc(loaded, DMA)
                sp.wait_ge(moved, D_H)
                sp.dma_start(skew.rearrange("(p n) -> p n", p=P), rows[:, :, :].rearrange("p h m -> p (h m)")
                             ).then_inc(skewed, DMA)
                sp.wait_ge(skewed, DMA)
                n = D_H * SKEW - 1
                ahead = skew[P - 1:P - 1 + P * n].rearrange("(p n) -> p n", n=n)
                for h in range(D_H):
                    sp.dma_start(near[:, h, :], ahead[:, h * SKEW:h * SKEW + NEAR]).then_inc(near_ld, DMA)
                sp.wait_ge(near_ld, D_H * DMA)

            @block.vector
            def _(dve):
                link = Link(dve, chain)
                dve.memset(tab[BUCKETS:BUCKETS + 1, :], -HUGE).then_inc(hidden, 1)
                dve.wait_ge(loaded, 6 * DMA)
                dve.wait_ge(hidden, 1)
                link(dve.tensor_scalar(tab[0:BUCKETS, :], tab[0:BUCKETS, :], D_QK ** 0.5, None, ALU.mult))
                dve.tensor_copy(wide[:, :, :], tab[:, :].unsqueeze(2).to_broadcast([BUCKETS + 1, D_H, P])).then_inc(wided, 1)
                for i in range(2):
                    link(dve.tensor_tensor(lp[:, i, :], lv[:, 2 * i, :], lv[:, 2 * i + 1, :], ALU.mult))
                dve.tensor_reduce(ls[:, 0:2], lp[:, :, :], AX.X, ALU.add).then_inc(dot, 1)
                dve.wait_ge(expd, 1)
                link(dve.tensor_tensor(ls[:, 0:1], ls[:, 3:4], ls[:, 2:3], ALU.subtract))
                link(dve.tensor_scalar(lam[:, :], ls[:, 0:1], 1.0, -LAM_INIT, ALU.mult, ALU.add))
                dve.wait_ge(moved, D_H)
                link(dve.tensor_copy(far[:, :].unsqueeze(2), rows[:, :, 0:1]))

            @block.tensor
            def _(pe):
                pe.wait_ge(wided, 1)
                for h in range(D_H):
                    if h >= 2:
                        pe.wait_ge(moved, h - 1)
                    pe.matmul(acc[:, h % 2, 0:SKEW], wide[:, h, :], oh[:, :], start=True, stop=True).then_inc(ready, 1)

            @block.scalar
            def _(act):
                for h in range(D_H):
                    act.wait_ge(ready, h + 1)
                    act.activation(rows[:, h, :], acc[:, h % 2, 0:SKEW], ACT.Copy).then_inc(moved, 1)
                act.wait_ge(dot, 1)
                act.activation(ls[:, 2:4], ls[:, 0:2], ACT.Exp).then_inc(expd, 1)


def diff_attend(nc, tag, qkT, vg, near, far, lam, subln, ident, yT):
    N = 2 * TT
    with Place(nc, tag) as pl:
        raw = pl.sb("raw", [P, 4, L])
        X = pl.sb("X", [P, 2, 6, L], F32R)
        VG = pl.sb("VG", [P, 2, 2, TT, D_V])
        B = pl.sb("B", [P, 2, L])
        S = pl.sb("S", [P, 2, 2, L])
        E = pl.sb("E", [P, 2, 2, L])
        W = pl.sb("W", [P, 2, L])
        ET = pl.sb("ET", [P, 2, TT, P])
        mx = pl.sb("mx", [P, 2, 2, 4])
        O = pl.sb("O", [P, 2, TT, D_V])
        junk = pl.sb("junk", [P, 2, D_V])
        hs = pl.sb("hs", [P, 2, 4, TT])
        YT = pl.sb("YT", [P, TT, P])
        sw = pl.sb("sw", [P, 1])
        pS = pl.ps("pS", [P, 2, 2, NC])
        pE = pl.ps("pE", [P, TT, P])
        pO = pl.ps("pO", [P, 2, NC])
        raw_ld = pl.sem("raw_loaded")
        vg_ld = [pl.sem(f"values_loaded{s}") for s in range(2)]
        w_ld = pl.sem("weight_loaded")
        x_hi = pl.sem("hi_parts_ready")
        x_sub = pl.sem("lo_of_queries")
        x_split = pl.sem("parts_ready")
        b_far = pl.sem("bias_far")
        b_in = pl.sem("bias_ready")
        passed = pl.sem("passed")
        passed_sp = pl.sem("passed_sync")
        passed_pool = pl.sem("passed_pool")
        dots = pl.sem("logits_ready")
        masked = pl.sem("logits_biased")
        neg = pl.sem("negated")
        expd = pl.sem("exp_done")
        inv = pl.sem("weights_ready")
        half = pl.sem("second_half_weighted")
        comb = pl.sem("halves_combined")
        turned = pl.sem("turned")
        moved = pl.sem("moved")
        summed = pl.sem("values_summed")
        kept = pl.sem("output_kept")
        sqd = pl.sem("output_squared")
        hm = pl.sem("head_mean")
        hr = pl.sem("head_root")
        hi = pl.sem("head_inverse")
        hn = pl.sem("head_normed")
        gat = pl.sem("head_gated")
        h_tr = pl.sem("head_transposed")
        h_mv = pl.sem("head_moved")
        yt_free = pl.sem("YT_free")
        out_st = pl.store_sem("out_stored")

        def heads(eng, body):
            body(0, 0, 0, True, False)
            with eng.Fori(0, (D_H - 2) // 2) as r:
                body(r * 2 + 1, 1, r, False, False)
                body(r * 2 + 2, 0, r + 1, False, False)
            body(D_H - 1, 1, (D_H - 1) // 2, False, True)

        with nc.Block() as block:
            @block.sync
            def _(sp):
                sp.dma_start(sw[:, :], subln.rearrange("(p o) -> p o", o=1), allow_slow_non_contiguous=True).then_inc(w_ld, DMA)

                def body(h, s, r):
                    sp.wait_ge(x_split, h + 1)
                    sp.sem_inc(passed_sp, 1)
                    for i in range(2):
                        for rows in (slice(0, D_QK), slice(D_QK, P)):
                            sp.dma_start(raw[rows, 2 * i:2 * i + 2, :],
                                         qkT[bass.ds(i * D + h * P, P), :].rearrange("(a p) t -> p a t", a=2)
                                         ).then_inc(raw_ld, DMA)
                    sp.wait_ge(gat, h + 1)
                    sp.sem_inc(passed_sp, 1)
                    for i in range(2):
                        sp.dma_start(VG[:, s, i, :, :], vg[:, bass.ds(i * D + h * P, P)].rearrange("(t p) d -> p t d", p=P)
                                     ).then_inc(vg_ld[s], DMA)
                pairs(sp, D_H, body)

            @block.gpsimd
            def _(pool):
                pool.sem_inc(x_split, 1)
                pool.sem_inc(gat, 2)
                pool.sem_inc(yt_free, 1)

                def set_bias(h, s):
                    pool.tensor_copy(B[:, s, 0:L - NEAR].unsqueeze(1),
                                     far[:, bass.ds(h, 1)].unsqueeze(2).to_broadcast([P, 1, L - NEAR])).then_inc(b_far, 1)
                    pool.tensor_copy(B[:, s, L - NEAR:L].unsqueeze(1), near[:, bass.ds(h, 1), :]).then_inc(b_in, 1)

                def subtract(h, s):
                    pool.wait_ge(b_far, h + 1)
                    pool.wait_ge(b_in, h + 1)
                    pool.wait_ge(x_hi, h + 1)
                    pool.tensor_tensor(X[D_QK:P, s, 0:2, :], raw[D_QK:P, 0:2, :], X[D_QK:P, s, 0:2, :].bitcast(F32),
                                       ALU.subtract).then_inc(x_sub, 1)
                    pool.wait_ge(x_sub, 2 * h + 1)
                    pool.tensor_tensor(X[:, s, 4:6, :], raw[:, 2:4, :], X[:, s, 2:4, :].bitcast(F32),
                                       ALU.subtract).then_inc(x_sub, 1)
                    pool.wait_ge(x_sub, 2 * h + 2)
                    pool.sem_inc(x_split, 1)

                def gate(h, s):
                    pool.wait_ge(hn, h + 1)
                    pool.tensor_tensor(O[:, s, :, :], O[:, s, :, :], VG[:, s, 1, :, :], ALU.mult).then_inc(gat, 1)

                def store(h):
                    pool.wait_ge(h_mv, 2 * h + 3)
                    pool.dma_start(yT[bass.ds(h * P, P), :], YT[:, :, :].rearrange("p a b -> p (a b)")).then_inc(out_st, DMA)
                    pool.wait_ge(out_st, (h + 1) * DMA)
                    pool.sem_inc(yt_free, 1)

                def body(h, s, r, first, last):
                    if first:
                        set_bias(h, s)
                        subtract(h, s)
                    else:
                        gate(h - 1, 1 - s)
                    if not last:
                        pool.wait_ge(masked, h * N + 2)
                        pool.sem_inc(passed_pool, 1)
                        set_bias(h + 1, 1 - s)
                    if not first:
                        store(h - 1)
                    if not last:
                        subtract(h + 1, 1 - s)
                heads(pool, body)
                gate(D_H - 1, 1)
                store(D_H - 1)

            @block.tensor
            def _(pe):
                pe.sem_inc(turned, 2)
                pe.sem_inc(summed, 2)
                pe.sem_inc(h_tr, 4)

                def logits(h, s, qb):
                    if qb == 0:
                        pe.wait_ge(x_split, h + 2)
                    for a in range(2):
                        n = h * N + 2 * qb + a
                        pe.wait_ge(masked, n + 1)
                        for c in range(0, (qb + 1) * P, NC):
                            k = min(NC, (qb + 1) * P - c)
                            for part in range(2):
                                mm = pe.matmul(pS[:, a, c // NC, 0:k], X[:, s, a, qb * P:(qb + 1) * P],
                                               X[:, s, 2 + 2 * part + a, c:c + k], start=part == 0, stop=part == 1)
                        mm.then_inc(dots, 1)

                def values(h, s, r, qb):
                    m = h * TT + qb
                    if qb == 0:
                        pe.wait_ge(vg_ld[s], (r + 1) * 2 * DMA)
                    pe.wait_ge(moved, m + 2)
                    pe.wait_ge(kept, m + 1)
                    for c in range(qb + 1):
                        mm = pe.matmul(pO[:, qb % 2, 0:D_V], ET[:, qb % 2, c, :], VG[:, s, 0, c, :],
                                       start=c == 0, stop=c == qb)
                    mm.then_inc(summed, 1)

                def turn(h, qb):
                    m = h * TT + qb
                    pe.wait_ge(comb, m + 3)
                    pe.wait_ge(moved, m + 1)
                    if qb == TT // 2:
                        pe.wait_ge(h_mv, 2 * h + 1)
                    for c in range(qb + 1):
                        mm = pe.transpose(pE[:, c, :], W[:, qb % 2, c * P:(c + 1) * P], ident[:, :])
                    mm.then_inc(turned, 1)

                def turn_head(h, s, i):
                    pe.wait_ge(gat, h + 3)
                    pe.wait_ge(h_mv, 2 * h + i + 1)
                    if i == 0:
                        pe.wait_ge(moved, (h + 1) * TT + 1)
                    for c in range(TT // 2):
                        mm = pe.transpose(pE[:, TT // 2 + c, :], O[:, s, i * (TT // 2) + c, :], ident[:, :])
                    mm.then_inc(h_tr, 1)

                def body(h, s, r, first, last):
                    if first:
                        logits(h, s, 0)
                        logits(h, s, 1)
                    for k in range(TT):
                        if k + 2 < TT:
                            logits(h, s, k + 2)
                        elif not last:
                            logits(h + 1, 1 - s, k + 2 - TT)
                        if k > 0:
                            values(h, s, r, k - 1)
                        elif not first:
                            values(h - 1, 1 - s, r if s else r - 1, TT - 1)
                        if k in (2, 3) and not first:
                            turn_head(h - 1, 1 - s, k - 2)
                        turn(h, k)
                heads(pe, body)
                values(D_H - 1, 1, (D_H - 1) // 2, TT - 1)
                turn_head(D_H - 1, 1, 0)
                turn_head(D_H - 1, 1, 1)

            @block.vector
            def _(dve):
                dve.sem_inc(masked, 2)
                dve.sem_inc(comb, 2)
                dve.sem_inc(kept, 2)
                dve.sem_inc(h_mv, 1)
                dve.wait_ge(w_ld, DMA)

                def bias(h, s, qb):
                    w, m = (qb + 1) * P, h * TT + qb
                    v = mx[:, qb % 2, :, :]
                    if qb == 0:
                        dve.wait_ge(b_in, h + 1)
                        dve.wait_ge(b_far, h + 1)
                    for a in range(2):
                        dve.wait_ge(dots, 2 * m + a + 1)
                        dve.wait_ge(expd, 2 * m + a + 1)
                        dve.sem_inc(passed, 1)
                        dve.tensor_tensor_reduce(S[:, qb % 2, a, 0:w], pS[:, a, :, :].rearrange("p a b -> p (a b)")[:, 0:w],
                                                 B[:, s, L - w:L], D_QK ** -0.5, GONE, ALU.add, ALU.max,
                                                 v[:, a, 0:1]).then_inc(masked, 1)
                    dve.wait_ge(masked, 2 * m + 4)
                    dve.tensor_scalar(v[:, :, 1:2], v[:, :, 0:1], -1.0, None, ALU.mult).then_inc(neg, 1)

                def combine(h, qb):
                    m, w = h * TT + qb, (qb + 1) * P
                    v = mx[:, qb % 2, :, :]
                    dve.wait_ge(expd, 2 * m + 6)
                    dve.reciprocal(v[:, :, 3:4], v[:, :, 2:3]).then_inc(inv, 1)
                    dve.wait_ge(inv, 2 * m + 1)
                    dve.tensor_scalar(v[:, 1, 3:4], v[:, 1, 3:4], lam[:, :], None, ALU.mult).then_inc(inv, 1)
                    dve.wait_ge(inv, 2 * m + 2)
                    dve.wait_ge(turned, m + 1)
                    dve.tensor_scalar(W[:, qb % 2, 0:w], E[:, qb % 2, 1, 0:w], v[:, 1, 3:4], None, ALU.mult).then_inc(half, 1)
                    dve.wait_ge(half, m + 1)
                    dve.scalar_tensor_tensor(W[:, qb % 2, 0:w], E[:, qb % 2, 0, 0:w], v[:, 0, 3:4], W[:, qb % 2, 0:w],
                                             ALU.mult, ALU.add).then_inc(comb, 1)

                def keep(h, s, qb):
                    dve.wait_ge(summed, h * TT + qb + 3)
                    if qb == 0:
                        dve.wait_ge(h_tr, 2 * h + 2)
                    dve.tensor_copy(O[:, s, qb, :], pO[:, qb % 2, 0:D_V]).then_inc(kept, 1)

                def norm(h, s):
                    dve.wait_ge(sqd, (h + 1) * TT + 2)
                    dve.tensor_scalar(hs[:, s, 1, :], hs[:, s, 0, :], 1.0 / D_V, EPS, ALU.mult, ALU.add).then_inc(hm, 1)
                    dve.wait_ge(hr, h + 1)
                    dve.reciprocal(hs[:, s, 3, :], hs[:, s, 2, :]).then_inc(hi, 1)
                    dve.wait_ge(hi, h + 1)
                    dve.wait_ge(kept, (h + 1) * TT + 2)
                    dve.tensor_tensor(O[:, s, :, :], O[:, s, :, :], hs[:, s, 3, :].unsqueeze(2).to_broadcast([P, TT, D_V]),
                                      ALU.mult).then_inc(hn, 1)

                def move_head(h, i):
                    dve.wait_ge(h_tr, 2 * h + i + 5)
                    if i == 0:
                        dve.wait_ge(yt_free, h + 1)
                    at = i * (TT // 2)
                    dve.tensor_scalar(YT[:, at:at + TT // 2, :], pE[:, TT // 2:TT, :], sw[:, :], 1.0 - LAM_INIT,
                                      ALU.mult, ALU.mult).then_inc(h_mv, 1)

                def body(h, s, r, first, last):
                    if first:
                        bias(h, s, 0)
                    for k in range(TT):
                        if k + 1 < TT:
                            bias(h, s, k + 1)
                        elif not last:
                            bias(h + 1, 1 - s, 0)
                        combine(h, k)
                        if k > 0:
                            keep(h, s, k - 1)
                        elif not first:
                            keep(h - 1, 1 - s, TT - 1)
                        if k == 1 and not first:
                            norm(h - 1, 1 - s)
                        if k in (2, 3) and not first:
                            move_head(h - 1, k - 2)
                heads(dve, body)
                keep(D_H - 1, 1, TT - 1)
                norm(D_H - 1, 1)
                move_head(D_H - 1, 0)
                move_head(D_H - 1, 1)

            @block.scalar
            def _(act):
                act.sem_inc(expd, 4)
                act.sem_inc(moved, 1)
                act.sem_inc(sqd, 2)

                def round_head(h, s):
                    act.wait_ge(raw_ld, (h + 1) * 4 * DMA)
                    act.activation(X[:, s, 0:4, :], raw[:, :, :], ACT.Copy).then_inc(x_hi, 1)

                def exps(h, qb):
                    m, w = h * TT + qb, (qb + 1) * P
                    act.wait_ge(neg, m + 1)
                    act.wait_ge(comb, m + 1)
                    for a in range(2):
                        act.activation(E[:, qb % 2, a, 0:w], S[:, qb % 2, a, 0:w], ACT.Exp, bias=mx[:, qb % 2, a, 1:2],
                                       accum_out=mx[:, qb % 2, a, 2:3]).then_inc(expd, 1)

                def move(h, qb):
                    m = h * TT + qb
                    act.wait_ge(turned, m + 3)
                    act.wait_ge(summed, m + 1)
                    act.activation(ET[:, qb % 2, 0:qb + 1, :], pE[:, 0:qb + 1, :], ACT.Copy).then_inc(moved, 1)

                def squares(h, s, qb):
                    m = h * TT + qb
                    act.wait_ge(kept, m + 3)
                    act.wait_ge(sqd, m + 1)
                    act.activation(junk[:, qb % 2, :], O[:, s, qb, :], ACT.Square, accum_out=hs[:, s, 0, qb:qb + 1]).then_inc(sqd, 1)

                def root(h, s):
                    act.wait_ge(hm, h + 1)
                    act.activation(hs[:, s, 2, :], hs[:, s, 1, :], ACT.Sqrt).then_inc(hr, 1)

                def body(h, s, r, first, last):
                    if first:
                        round_head(h, s)
                        exps(h, 0)
                    for k in range(TT):
                        if k + 1 < TT:
                            exps(h, k + 1)
                        elif not last:
                            exps(h + 1, 0)
                        move(h, k)
                        if k > 0:
                            squares(h, s, k - 1)
                        elif not first:
                            squares(h - 1, 1 - s, TT - 1)
                        if k == 1 and not first:
                            root(h - 1, 1 - s)
                        if k == 3 and not last:
                            round_head(h + 1, 1 - s)
                heads(act, body)
                squares(D_H - 1, 1, TT - 1)
                root(D_H - 1, 1)


R_H, R_D = 16, 128
R_W = R_H * R_D
LEVELS = 7
HALVES = [P >> (i + 1) for i in range(LEVELS)]


def level_masks():
    s, t = np.arange(P)[:, None], np.arange(P)[None, :]
    levels = [((s // (2 * h) == t // (2 * h)) & (s % (2 * h) < h) & (t % (2 * h) >= h)) for h in HALVES]
    return np.stack(levels + [s == t], axis=1).astype(np.float32)


def linear_recurrence(nc, tag, qfT, ig, lower, masks, norm_w, ident, yT):
    K = LEVELS + 1
    C = TT
    assert K == C
    with Place(nc, tag) as pl:
        lw = pl.sb("lw", [P, 4, R_H])
        mk = pl.sb("mk", [P, K, P])
        first = pl.sb("first", [P, L])
        nw = pl.sb("nw", [P, 1])
        Q = pl.sb("Q", [P, 2, L])
        F = pl.sb("F", [P, 2, L])
        V = pl.sb("V", [P, 2, C, R_D])
        G = pl.sb("G", [P, 2, C, R_D])
        KK = pl.sb("KK", [P, 2, L])
        LF = pl.sb("LF", [P, L])
        BB = pl.sb("BB", [P, 2, L])
        DD = pl.sb("DD", [P, 3, L])
        QL = pl.sb("QL", [P, 2, L])
        KL = pl.sb("KL", [P, 2, L])
        KE = pl.sb("KE", [P, L])
        QE = pl.sb("QE", [P, 2, L])
        KT = pl.sb("KT", [P, 2, C, R_D])
        AT = pl.sb("AT", [P, 2, C, P])
        EL = pl.sb("EL", [P, 2, C])
        ST = pl.sb("ST", [P, R_D])
        O = pl.sb("O", [P, 2, C, R_D])
        junk = pl.sb("junk", [P, 2, R_D])
        hs = pl.sb("hs", [P, 2, 4, C])
        YT = pl.sb("YT", [P, C, P])
        pA = pl.ps("pA", [P, 2, C, P])
        pK = pl.ps("pK", [P, 4, P])
        pO = pl.ps("pO", [P, 2, NC])
        pS = pO[:, :, 2 * R_D:3 * R_D]
        loaded = pl.sem("loaded")
        chain = pl.sem("dve")
        set_up = pl.sem("set_up")
        l_in = pl.sem("lower_difference")
        l_ex = pl.sem("lower_exp")
        with nc.Block() as block:
            @block.sync
            def _(sp):
                for i in range(2):
                    sp.dma_start(lw[:, i, :], lower[i, :].rearrange("(h p) -> p h", p=P),
                                 allow_slow_non_contiguous=True).then_inc(loaded, DMA)
                sp.dma_start(mk[:, :, :], masks).then_inc(loaded, DMA)
                sp.dma_start(nw[:, :], norm_w.rearrange("(p o) -> p o", o=1),
                             allow_slow_non_contiguous=True).then_inc(loaded, DMA)
                sp.wait_ge(loaded, 4 * DMA)

            @block.gpsimd
            def _(pool):
                for x in (AT, QL, KL):
                    pool.memset(x[:], 0.0).then_inc(set_up, 1)
                pool.memset(first[:, :], 1.0).then_inc(set_up, 1)
                pool.wait_ge(set_up, 4)
                pool.memset(first[:, :].rearrange("p (c t) -> p c t", t=P)[:, :, 0:1], 0.0).then_inc(set_up, 1)
                pool.wait_ge(set_up, 5)

            @block.vector
            def _(dve):
                link = Link(dve, chain)
                dve.wait_ge(loaded, 4 * DMA)
                link(dve.tensor_tensor(lw[:, 2, :], lw[:, 0, :], lw[:, 1, :], ALU.max))
                link(dve.tensor_tensor(lw[:, 0, :], lw[:, 0, :], lw[:, 2, :], ALU.subtract))
                dve.tensor_tensor(lw[:, 1, :], lw[:, 1, :], lw[:, 2, :], ALU.subtract).then_inc(l_in, 1)
                dve.wait_ge(l_ex, 1)
                link(dve.tensor_tensor(lw[:, 2, :], lw[:, 0, :], lw[:, 1, :], ALU.add))
                link(dve.reciprocal(lw[:, 3, :], lw[:, 2, :]))
                link(dve.tensor_tensor(lw[:, 2, :], lw[:, 1, :], lw[:, 3, :], ALU.mult))
                link(dve.tensor_scalar(lw[:, 3, :], lw[:, 2, :], -1.0, 1.0, ALU.mult, ALU.add))

            @block.scalar
            def _(act):
                act.wait_ge(l_in, 1)
                act.activation(lw[:, 0:2, :], lw[:, 0:2, :], ACT.Exp).then_inc(l_ex, 1)

        q_ld = [pl.sem(f"head_loaded{s}") for s in range(2)]
        v_ld = [pl.sem(f"values_loaded{s}") for s in range(2)]
        g_ld = [pl.sem(f"gates_loaded{s}") for s in range(2)]
        fs = pl.sem("f_ready")
        ks = pl.sem("keys_ready")
        lf = pl.sem("log_ready")
        bs = pl.sem("b_ready")
        ds = pl.sem("exponents_ready")
        es = pl.sem("exponentials_ready")
        qk = pl.sem("factors_ready")
        pr = pl.sem("product_ready")
        at = pl.sem("weights_taken")
        ad = pl.sem("head_taken")
        bl = pl.sem("last_difference_ready")
        ex = pl.sem("chunk_exponentials_ready")
        ke = pl.sem("chunk_factors_ready")
        kt = pl.sem("keys_transposed")
        km = pl.sem("keys_moved")
        ch = pl.sem("chunk_ready")
        su = pl.sem("state_ready")
        om = pl.sem("output_moved")
        sqd = pl.sem("output_squared")
        hm = pl.sem("head_mean")
        hr = pl.sem("head_root")
        hi = pl.sem("head_inverse")
        hn = pl.sem("head_normed")
        hg = pl.sem("head_gated")
        ct = pl.sem("outputs_transposed")
        cm = pl.sem("outputs_moved")
        yt_free = pl.sem("YT_free")
        out_st = pl.sem("out_stored")
        passed_sp = pl.sem("passed_sync")
        passed = pl.sem("passed")

        def items(body):
            def run(eng):
                body(-1, 1, -1, "P")
                body(0, 0, 0, "PA")
                body(1, 1, 0, "PAB")
                with eng.Fori(0, (R_H - 4) // 2) as r:
                    body(r * 2 + 2, 0, r + 1, "PABC")
                    body(r * 2 + 3, 1, r + 1, "PABC")
                body(R_H - 2, 0, R_H // 2 - 1, "PABC")
                body(R_H - 1, 1, R_H // 2 - 1, "ABC")
                body(R_H, 0, R_H // 2, "BC")
                body(R_H + 1, 1, R_H // 2, "C")
            return run

        def dd(j):
            return DD[:, j % 2 if j else 2, :]

        def halves(x, h):
            return x.rearrange("p (b u t) -> p b u t", u=2, t=h)

        def chunks(x):
            return x.rearrange("p (c t) -> p c t", t=P)

        with nc.Block() as block:
            @block.sync
            def _(sp):
                def body(n, s, r, steps):
                    if "P" in steps:
                        sp.wait_ge(ad, n + 2)
                        sp.sem_inc(passed_sp, 1)
                        sp.dma_start(Q[:, 1 - s, :], qfT[bass.ds(n * P + P, P), :]).then_inc(q_ld[1 - s], DMA)
                        sp.dma_start(F[:, 1 - s, :], qfT[bass.ds(n * P + P + R_W, P), :]).then_inc(q_ld[1 - s], DMA)
                    if "A" in steps:
                        sp.wait_ge(ch, (n + 1) * C)
                        sp.sem_inc(passed_sp, 1)
                        sp.dma_start(V[:, s, :, :], ig[:, bass.ds(n * P, P)].rearrange("(c p) d -> p c d", p=P)
                                     ).then_inc(v_ld[s], DMA)
                        sp.wait_ge(hg, n + 1)
                        sp.sem_inc(passed_sp, 1)
                        sp.dma_start(G[:, s, :, :], ig[:, bass.ds(n * P + R_W, P)].rearrange("(c p) d -> p c d", p=P)
                                     ).then_inc(g_ld[s], DMA)
                    if "C" in steps:
                        sp.wait_ge(cm, (n - 2) * 2 + 2)
                        sp.sem_inc(passed_sp, 1)
                        sp.dma_start(yT[bass.ds((n - 2) * P, P), :], YT[:, :, :].rearrange("p c t -> p (c t)")
                                     ).then_inc(out_st, DMA)
                        sp.wait_ge(out_st, (n - 1) * DMA)
                        sp.sem_inc(yt_free, 1)
                sp.sem_inc(yt_free, 1)
                items(body)(sp)

            @block.tensor
            def _(pe):
                pe.sem_inc(kt, 1)
                pe.sem_inc(ch, 2 * C)
                pe.sem_inc(ct, 3)

                def body(n, s, r, steps):
                    A, B, Cs = ("A" in steps), ("B" in steps), ("C" in steps)
                    m, sb = n - 1, 1 - s
                    for j in range(K):
                        if A:
                            if j == 0:
                                pe.wait_ge(ks, n + 1)
                            else:
                                pe.wait_ge(qk, n * LEVELS + j + 1)
                            pe.wait_ge(at, n * K + j + 1)
                            for c in range(C):
                                t = slice(c * P, (c + 1) * P)
                                lh, rh = (KK[:, s, t], Q[:, s, t]) if j == 0 else (KL[:, (j - 1) % 2, t], QL[:, (j - 1) % 2, t])
                                mm = pe.matmul(pA[:, j % 2, c, :], lh, rh, start=True, stop=True, skip_group_check=True)
                            mm.then_inc(pr, 1)
                        if B:
                            i = m * C + j
                            if j == 0:
                                pe.wait_ge(v_ld[sb], (r if s == 0 else r + 1) * DMA)
                                pe.wait_ge(at, m * K + K + 2)
                                pe.wait_ge(km, m * 2 + 2)
                            pe.wait_ge(sqd, i + 1)
                            pe.matmul(pS[:, j % 2, 0:R_D], KT[:, sb, j, :], V[:, sb, j, :], start=True, stop=True,
                                      skip_group_check=True)
                            pe.matmul(pO[:, j % 2, 0:R_D], AT[:, sb, j, :], V[:, sb, j, :], start=True, stop=False)
                            pe.wait_ge(su, i + 1)
                            pe.matmul(pO[:, j % 2, 0:R_D], QE[:, sb, j * P:(j + 1) * P], ST[:, :], start=False,
                                      stop=True).then_inc(ch, 1)
                        if Cs and j in (3, 4):
                            h = j - 3
                            pe.wait_ge(hg, n + 1)
                            if h == 0:
                                pe.wait_ge(km, n * 2 if A else 2 * R_H)
                            else:
                                pe.wait_ge(cm, (n - 2) * 2 + 1)
                            for c in range(4):
                                mm = pe.transpose(pK[:, c, :], O[:, s, 4 * h + c, :], ident[:, :])
                            mm.then_inc(ct, 1)
                        if A and j in (5, 6):
                            h = j - 5
                            pe.wait_ge(ke, n + 1)
                            if h:
                                pe.wait_ge(km, n * 2 + 1)
                            elif Cs:
                                pe.wait_ge(cm, (n - 2) * 2 + 2)
                            elif B:
                                pe.wait_ge(km, n * 2)
                            for c in range(4):
                                mm = pe.transpose(pK[:, c, :], KE[:, (4 * h + c) * P:(4 * h + c + 1) * P], ident[:, :])
                            mm.then_inc(kt, 1)
                items(body)(pe)

            @block.vector
            def _(dve):
                dve.sem_inc(bs, 1)
                dve.sem_inc(qk, 1)
                dve.sem_inc(at, 2)
                dve.sem_inc(ad, 2)

                def body(n, s, r, steps):
                    A, B, Cs = ("A" in steps), ("B" in steps), ("C" in steps)
                    m, sb = n - 1, 1 - s
                    if Cs:
                        dve.wait_ge(sqd, (n - 1) * C + 2)
                        dve.tensor_scalar(hs[:, s, 1, :], hs[:, s, 0, :], 1.0 / R_D, EPS, ALU.mult, ALU.add).then_inc(hm, 1)
                    if Cs:
                        dve.wait_ge(hr, n - 1)
                        dve.reciprocal(hs[:, s, 3, :], hs[:, s, 2, :]).then_inc(hi, 1)
                        dve.wait_ge(hi, n - 1)
                        dve.tensor_tensor(O[:, s, :, :], O[:, s, :, :], hs[:, s, 3, :].unsqueeze(2).to_broadcast([P, C, R_D]),
                                          ALU.mult).then_inc(hn, 1)
                    for j in range(K):
                        if "P" in steps and j == 3:
                            dve.wait_ge(q_ld[sb], ((r if s == 0 else r + 1) + 1) * 2 * DMA)
                            dve.tensor_scalar(F[:, sb, :], F[:, sb, :], lw[:, 3, bass.ds(n + 1, 1)], lw[:, 2, bass.ds(n + 1, 1)],
                                              ALU.mult, ALU.add).then_inc(fs, 1)
                            dve.wait_ge(fs, n + 2)
                            dve.tensor_scalar(KK[:, sb, :], F[:, sb, :], -1.0, 1.0, ALU.mult, ALU.add).then_inc(ks, 1)
                        if "P" in steps and j == 5:
                            dve.wait_ge(lf, n + 2)
                            dve.tensor_tensor_scan(BB[:, sb, :], first[:, :], LF[:, :], 0.0, ALU.mult, ALU.add).then_inc(bs, 1)
                        if A and j < LEVELS:
                            h = HALVES[j]
                            dve.wait_ge(es, n * LEVELS + j + 1)
                            e, q, k = (halves(x, h) for x in (dd(j), Q[:, s, :], KK[:, s, :]))
                            dve.tensor_tensor(halves(QL[:, j % 2, :], h)[:, :, 1, :], q[:, :, 1, :], e[:, :, 1, :], ALU.mult)
                            dve.tensor_tensor(halves(KL[:, j % 2, :], h)[:, :, 0, :], k[:, :, 0, :], e[:, :, 0, :],
                                              ALU.mult).then_inc(qk, 1)
                        if A and j == 2:
                            dve.wait_ge(ex, n + 1)
                            dve.tensor_tensor(QE[:, s, :], Q[:, s, :], F[:, s, :], ALU.mult)
                            dve.tensor_tensor(KE[:, :], KK[:, s, :], KE[:, :], ALU.mult).then_inc(ke, 1)
                        if B:
                            i = m * C + j
                            if j == 0:
                                dve.memset(ST[:, :], 0.0).then_inc(su, 1)
                            dve.wait_ge(ch, i + 1 + 2 * C)
                            if j < C - 1:
                                dve.wait_ge(su, i + 1)
                                dve.scalar_tensor_tensor(ST[:, :], ST[:, :], EL[:, sb, j:j + 1], pS[:, j % 2, 0:R_D],
                                                         ALU.mult, ALU.add).then_inc(su, 1)
                            if j == 0:
                                dve.wait_ge(ct, m * 2 + 1)
                            dve.tensor_copy(O[:, sb, j, :], pO[:, j % 2, 0:R_D]).then_inc(om, 1)
                        if A:
                            dve.wait_ge(pr, n * K + j + 1)
                            if j:
                                dve.wait_ge(at, n * K + j + 2)
                            dve.sem_inc(passed, 1)
                            kind = K - 1 if j == 0 else j - 1
                            dve.copy_predicated(AT[:, s, :, :], mk[:, kind, :].bitcast(U32).unsqueeze(1).to_broadcast([P, C, P]),
                                                pA[:, j % 2, :, :]).then_inc(at, 1)
                    if A:
                        dve.wait_ge(at, n * K + K + 2)
                        dve.sem_inc(ad, 1)
                items(body)(dve)

            @block.scalar
            def _(act):
                act.sem_inc(sqd, 2)

                def body(n, s, r, steps):
                    A, B, Cs = ("A" in steps), ("B" in steps), ("C" in steps)
                    m, sb = n - 1, 1 - s
                    if Cs:
                        act.wait_ge(hm, n - 1)
                        act.activation(hs[:, s, 2, :], hs[:, s, 1, :], ACT.Sqrt).then_inc(hr, 1)
                    for j in range(K):
                        if A and 0 < j < LEVELS:
                            act.wait_ge(ds, n * LEVELS + j + 1)
                            act.activation(dd(j), dd(j), ACT.Exp).then_inc(es, 1)
                        if "P" in steps and j == 4:
                            act.wait_ge(fs, n + 2)
                            act.wait_ge(bs, n + 2)
                            act.activation(LF[:, :], F[:, sb, :], ACT.Ln).then_inc(lf, 1)
                        if "P" in steps and j == K - 1:
                            act.wait_ge(ds, (n + 1) * LEVELS + 1)
                            act.activation(dd(0), dd(0), ACT.Exp).then_inc(es, 1)
                        if A and j == 0:
                            act.wait_ge(ks, n + 1)
                            act.activation(F[:, s, :], BB[:, s, :], ACT.Exp)
                            act.activation(EL[:, s, :].unsqueeze(2), chunks(BB[:, s, :])[:, :, P - 1:P], ACT.Exp)
                            act.wait_ge(bl, n + 1)
                            act.activation(KE[:, :], KE[:, :], ACT.Exp).then_inc(ex, 1)
                        if Cs and j in (3, 4):
                            h = j - 3
                            if h == 0:
                                act.wait_ge(yt_free, n - 1)
                            act.wait_ge(ct, (n - 2) * 2 + h + 4)
                            act.activation(YT[:, 4 * h:4 * h + 4, :], pK[:, :, :], ACT.Copy, scale=nw[:, :]).then_inc(cm, 1)
                        if A and j in (5, 6):
                            h = j - 5
                            act.wait_ge(kt, n * 2 + h + 2)
                            act.activation(KT[:, s, 4 * h:4 * h + 4, :], pK[:, :, :], ACT.Copy).then_inc(km, 1)
                        if B:
                            i = m * C + j
                            act.wait_ge(om, i + 1)
                            act.wait_ge(sqd, i + 1)
                            act.activation(junk[:, j % 2, :], pO[:, j % 2, 0:R_D], ACT.Square,
                                           accum_out=hs[:, sb, 0, j:j + 1]).then_inc(sqd, 1)
                items(body)(act)

            @block.gpsimd
            def _(pool):
                pool.sem_inc(hg, 2)

                def body(n, s, r, steps):
                    A, Cs = ("A" in steps), ("C" in steps)

                    def exponents(j, sh):
                        h = HALVES[j]
                        b, d = halves(BB[:, sh, :], h), halves(dd(j), h)
                        mid = b[:, :, 0, h - 1:h].to_broadcast([P, L // (2 * h), h])
                        pool.tensor_tensor(d[:, :, 1, :], b[:, :, 1, :], mid, ALU.subtract)
                        pool.tensor_tensor(d[:, :, 0, :], mid, b[:, :, 0, :], ALU.subtract).then_inc(ds, 1)

                    for j in range(LEVELS):
                        if A and j:
                            pool.wait_ge(qk, n * LEVELS + j)
                            exponents(j, s)
                        if A and j == 0:
                            pool.wait_ge(kt, n * 2 + 1)
                            b = chunks(BB[:, s, :])
                            pool.tensor_tensor(chunks(KE[:, :]), b[:, :, P - 1:P].to_broadcast([P, C, P]), b,
                                               ALU.subtract).then_inc(bl, 1)
                        if Cs and j == 1:
                            pool.wait_ge(hn, n - 1)
                            pool.wait_ge(g_ld[s], r * DMA)
                            pool.tensor_tensor(O[:, s, :, :], O[:, s, :, :], G[:, s, :, :], ALU.mult).then_inc(hg, 1)
                    if "P" in steps:
                        if A:
                            pool.wait_ge(qk, n * LEVELS + 2)
                        pool.wait_ge(bs, n + 3)
                        exponents(0, 1 - s)
                items(body)(pool)


def norm_tokens(nc, tag, x, g, out):
    with Place(nc, tag) as pl:
        xin = pl.sb("xin", [P, TT, D])
        sq = pl.sb("sq", [P, 2, D])
        st = pl.sb("st", [P, 4, TT])
        gb = pl.sb("gb", [P, D])
        ld = [pl.sem(f"x_loaded{t}") for t in range(TT)]
        g_ld = pl.sem("gain_loaded")
        summed = pl.sem("squares_summed")
        mean = pl.sem("mean_ready")
        root = pl.sem("root_ready")
        inv = pl.sem("inverse_ready")
        scaled = pl.sem("rows_scaled")
        out_st = pl.sem("out_stored")
        with nc.Block() as block:
            @block.sync
            def _(sp):
                for t in range(TT):
                    sp.dma_start(xin[:, t, :], x[t * P:(t + 1) * P, :]).then_inc(ld[t], DMA)
                    if t == 1:
                        sp.dma_start(gb[:, :], g.partition_broadcast(P)).then_inc(g_ld, DMA)
                for t in range(TT):
                    sp.wait_ge(scaled, t + 1)
                    sp.dma_start(out[t * P:(t + 1) * P, :], xin[:, t, :]).then_inc(out_st, DMA)
                sp.wait_ge(out_st, TT * DMA)

            @block.scalar
            def _(act):
                act.sem_inc(summed, 2)
                for t in range(TT):
                    act.wait_ge(ld[t], DMA)
                    act.wait_ge(summed, t + 1)
                    act.activation(sq[:, t % 2, :], xin[:, t, :], ACT.Square, accum_out=st[:, 0, t:t + 1]).then_inc(summed, 1)
                act.wait_ge(mean, 1)
                act.activation(st[:, 2, :], st[:, 1, :], ACT.Sqrt).then_inc(root, 1)

            @block.vector
            def _(dve):
                dve.wait_ge(summed, TT + 2)
                dve.tensor_scalar(st[:, 1, :], st[:, 0, :], 1.0 / D, EPS, ALU.mult, ALU.add).then_inc(mean, 1)
                dve.wait_ge(root, 1)
                dve.reciprocal(st[:, 3, :], st[:, 2, :]).then_inc(inv, 1)
                dve.wait_ge(inv, 1)
                dve.wait_ge(g_ld, DMA)
                for t in range(TT):
                    dve.scalar_tensor_tensor(xin[:, t, :], xin[:, t, :], st[:, 3, t:t + 1], gb[:, :], ALU.mult,
                                             ALU.mult).then_inc(scaled, 1)


Z_AT, XBC_AT, DT_AT = 0, X2, X2 + XB2 + G2 * N2
QK_AT = DT_AT + H2
V_AT = QK_AT + 2 * D
GATE_AT = V_AT + D


def build_program(nc, a, out):
    def scratch(name, *shape):
        return nc.dram_tensor(name, shape, F32, kind="Internal").ap()

    p1 = scratch("first_projection", L, WI0 + I_H)
    gT = scratch("gates", 2 * D, L)
    ysT, yaT, mT = scratch("y_ssm", S_W, L), scratch("y_att", A_H * A_D, L), scratch("merged", D, L)
    x1, hT, x2 = scratch("x1", L, D), scratch("hidden", a["w_ffn_gate"].shape[2], L), scratch("x2", L, D)
    z, xbcT, dt = scratch("z", L, X2), scratch("xbc", XB2 + G2 * N2, L), scratch("dt", L, H2)
    xbt, bcT = scratch("x_b", L, 2 * X2), scratch("b_c", 2 * G2 * N2, L)
    qkT, vg, skew = scratch("q_k", 2 * D, L), scratch("v_g", L, 2 * D), scratch("skew", P * D_H * SKEW)
    yT, x3 = scratch("y_even", 2 * D, L), scratch("x3", L, D)
    qfT, ig = scratch("q_f", 2 * R_W, L), scratch("i_g", L, 2 * R_W)
    yhT, x4 = scratch("y_odd", R_W, L), scratch("x4", L, D)

    with ExitStack() as ctx:
        ident = ctx.enter_context(nc.sbuf_tensor("ident", [P, P], F32))
        make_identity(nc, ident)

        def layer_input(tag, x, g, projections):
            with Place(nc, tag) as pl:
                XT = pl.sb("XT", [P, 2, KD, L], F32R)
                norm_to_features(nc, tag + "_norm", x, g, XT, ident)
                projections(XT)

        w = a["w_in"][0]

        def first(XT):
            project(nc, "in", XT, (
                (w[:, 0:2 * NC], p1[:, 0:2 * NC], False, ACT.Copy),
                (w[:, 2 * NC:WI0 + I_H], p1[:, 2 * NC:WI0 + I_H], False, ACT.Copy)))
            with Place(nc, "att") as pl:
                F = pl.sb("F", [P, 8, L])
                V = pl.sb("V", [P, TT, A_D])
                wi = pl.sb("wi", [P, TT, I_H])
                M = pl.sb("M", [P, mask_at(TT)])
                sparse_prepare(nc, "ap", p1, (a["q_norm_g"][0], a["k_norm_g"][0], a["idx_k_norm_g"][0]), F, V, wi, ident)
                masks_and_gates(nc, "am", F, wi, M, XT, w[:, WI0 + I_H:], gT)
                sparse_attend(nc, "aa", F, V, M, ident, yaT)
        layer_input("l0", a["x"][0], a["norm1_g"][0], first)
        s5 = {n: a[n] for n in ("A_re", "A_im", "B_re", "B_im", "C_re", "C_im")}
        s5.update({n: a[n][0] for n in ("log_dt", "D_skip", "w_glu", "b_glu")})
        s5_branch(nc, "s5", p1, s5, ident, ysT)
        merge_branches(nc, "merge", ysT, yaT, a["w_proj_ssm"][0], a["w_proj_attn"][0], gT, mT)
        reduce_tokens(nc, "out1", mT, a["w_out"][0], a["x"][0], x1)
        layer_input("ffn", x1, a["norm2_g"][0],
                    lambda XT: swiglu_up(nc, "up", XT, a["w_ffn_gate"][0], a["w_ffn_up"][0], hT))
        reduce_tokens(nc, "down", hT, a["w_ffn_down"][0], x1, x2)

        e = a["even_w_in_2"][0]

        def even(XT):
            project(nc, "even", XT, (
                (e[:, Z_AT:XBC_AT], z, False, ACT.Silu),
                (e[:, GATE_AT:GATE_AT + D], vg[:, D:2 * D], False, ACT.Silu),
                (e[:, XBC_AT:DT_AT], xbcT, True, ACT.Copy),
                (e[:, QK_AT:V_AT], qkT, True, ACT.Copy),
                (e[:, V_AT:GATE_AT], vg[:, 0:D], False, ACT.Copy),
                (e[:, DT_AT:QK_AT], dt, False, ACT.Copy)))
        layer_input("l1", x2, a["norm_w_2"][0], even)
        conv_silu(nc, "cx", 0, X2 // P, xbcT, a["conv_w_2"][0], a["conv_b_2"][0], ident, None, xbt)
        conv_silu(nc, "cb", X2 // P, 2 * G2, xbcT, a["conv_w_2"][0], a["conv_b_2"][0], ident, bcT, xbt)
        ssd_mixer(nc, "ssd", dt, xbt, bcT, z, {"dt_bias": a["dt_bias_2"][0], "A_log": a["A_log_2"][0],
                                               "D": a["D_skip_2"][0], "norm_w": a["ssd_norm_w_2"][0]}, ident, yT[0:X2, :])
        with Place(nc, "dif") as pl:
            near = pl.sb("near", [P, D_H, NEAR])
            far = pl.sb("far", [P, D_H])
            lam = pl.sb("lam", [P, 1])
            diff_bias(nc, "db", a["rel_bias_2"], a["one_hot"], skew, near, far, lam,
                      [a[n][0] for n in ("lambda_q1_2", "lambda_k1_2", "lambda_q2_2", "lambda_k2_2")])
            diff_attend(nc, "da", qkT, vg, near, far, lam, a["subln_w_2"][0], ident, yT[X2:X2 + D, :])
        reduce_tokens(nc, "out2", yT, a["even_w_out_2"][0], x2, x3)

        o = a["odd_w_in_2"][0]

        def odd(XT):
            project(nc, "odd", XT, (
                (o[:, 0:R_W], qfT[0:R_W, :], True, ACT.Silu),
                (o[:, R_W:2 * R_W], qfT[R_W:2 * R_W, :], True, ACT.Sigmoid),
                (o[:, 2 * R_W:3 * R_W], ig[:, 0:R_W], False, ACT.Copy),
                (o[:, 3 * R_W:4 * R_W], ig[:, R_W:2 * R_W], False, ACT.Silu)))
        layer_input("l2", x3, a["norm_w_2"][1], odd)
        linear_recurrence(nc, "hg", qfT, ig, a["hgrn_lower_bounds_2"], a["level_masks"], a["hgrn_norm_w_2"][0], ident, yhT)
        reduce_tokens(nc, "out3", yhT, a["odd_w_out_2"][0], x3, x4)
        norm_tokens(nc, "fin", x4, a["final_norm_w_2"], out[0])


def kernel(**inputs):
    import concourse.bacc as bacc
    from concourse.bass_utils import run_bass_kernel_spmd

    arrays = {n: np.ascontiguousarray(v) for n, v in inputs.items()}
    for n in ("A_re", "A_im"):
        arrays[n] = arrays[n].reshape(S_J, P)
    for n in ("B_re", "B_im"):
        arrays[n] = arrays[n].reshape(S_J, P, S_CH)
    for n in ("C_re", "C_im"):
        arrays[n] = np.ascontiguousarray(arrays[n][0].transpose(0, 2, 1)).reshape(S_J, P, S_CH)
    arrays["one_hot"] = bucket_one_hot()
    arrays["level_masks"] = level_masks()

    nc = bacc.Bacc("TRN2", target_bir_lowering=False, num_devices=1)
    named, aps = {}, {}
    for n, v in arrays.items():
        named[f"in_{n}"] = v
        aps[n] = nc.dram_tensor(f"in_{n}", v.shape, mybir.dt.from_np(v.dtype), kind="ExternalInput").ap()
    out = nc.dram_tensor("out", (1, L, D), F32, kind="ExternalOutput").ap()
    build_program(nc, aps, out)
    return run_bass_kernel_spmd(nc, [named], core_ids=[0]).results[0]["out"]
```
